# Optimizing a Trainium2 kernel written in Bass

```python
import jax
import jax.numpy as jnp
from jax import lax
import numpy as np
import math

D_MODEL = 1024
BATCH = 1
SEQ = 256
DEPTH = 2

GRID_W = 64
CTX_LEN = 256
EPS = 1e-6

POOL_WINDOWS = (2, 4, 8, 16)
POOL_GROUPS = 4
POOL_GROUP_DIM = D_MODEL // 16
POOL_WIDTH = POOL_GROUPS * POOL_GROUP_DIM

SGU_CHUNK = 128
SGU_HEADS = 4
SGU_HEAD_DIM = D_MODEL // 16
SGU_WIDTH = SGU_HEADS * SGU_HEAD_DIM

NA_HEAD_DIM = 64
NA_HEADS = D_MODEL // 128
NA_WIDTH = NA_HEADS * NA_HEAD_DIM
NA_KH = 8
NA_KW = 16
ROPE_THETA = 10000.0

N_BRANCH = 3
D_FF = 4 * D_MODEL

P_END = POOL_WIDTH
U_END = P_END + SGU_WIDTH
VS_END = U_END + SGU_WIDTH
Q_END = VS_END + NA_WIDTH
K_END = Q_END + NA_WIDTH
V_END = K_END + NA_WIDTH
PROJ_COLS = V_END + N_BRANCH * D_MODEL
SPLIT_POINTS = (P_END, U_END, VS_END, Q_END, K_END, V_END)


def rms_norm(x, g):
    x32 = x.astype(jnp.float32)
    y = x32 * lax.rsqrt(jnp.mean(x32 * x32, axis=-1, keepdims=True) + EPS)
    return (y * g.astype(jnp.float32)).astype(x.dtype)

def modulate(h, shift, scale):
    return h * (1 + scale) + shift

def to_heads(t):
    return t.reshape(t.shape[0], t.shape[1], NA_HEADS, NA_HEAD_DIM)

def pool_mix(p, w_pool, pool_scale):
    B, L, _ = p.shape
    pg = p.reshape(B, L, POOL_GROUPS, POOL_GROUP_DIM).astype(jnp.float32)
    csum = jnp.concatenate([jnp.zeros((B, 1, POOL_GROUPS, POOL_GROUP_DIM), jnp.float32),
                            jnp.cumsum(pg, axis=1)], axis=1)
    t = jnp.arange(L)
    outs = []
    for g, w in enumerate(POOL_WINDOWS):
        lo = jnp.clip(t - w // 2, 0, L)
        hi = jnp.clip(t + (w - w // 2), 0, L)
        cg = csum[:, :, g]
        win_sum = jnp.take(cg, hi, axis=1) - jnp.take(cg, lo, axis=1)
        cnt = (hi - lo).astype(jnp.float32)[None, :, None]
        outs.append(win_sum / cnt - pg[:, :, g])
    pooled = jnp.stack(outs, axis=2).astype(p.dtype)
    y = jnp.einsum('blgd,gde->blge', pooled, w_pool)
    return y.reshape(B, L, POOL_WIDTH) * pool_scale

def sgu_mix(u, v, sgu_w, sgu_b):
    B, L, _ = v.shape
    n_chunks = L // SGU_CHUNK
    v32 = v.astype(jnp.float32)
    mu = jnp.mean(v32, axis=-1, keepdims=True)
    var = jnp.mean(jnp.square(v32 - mu), axis=-1, keepdims=True)
    vn = ((v32 - mu) * lax.rsqrt(var + EPS)).astype(v.dtype)
    vc = vn.reshape(B, n_chunks, SGU_CHUNK, SGU_HEADS, SGU_HEAD_DIM)
    mixed = jnp.einsum('hpq,bcqhd->bcphd', sgu_w, vc) + sgu_b.T[None, None, :, :, None]
    return u * mixed.reshape(B, L, SGU_WIDTH)

def axial_rope(L):
    t = jnp.arange(L)
    row = (t // GRID_W).astype(jnp.float32)
    col = (t % GRID_W).astype(jnp.float32)
    n_freq = NA_HEAD_DIM // 4
    inv_freq = ROPE_THETA ** (-jnp.arange(n_freq, dtype=jnp.float32) / n_freq)
    ang = jnp.concatenate([row[:, None] * inv_freq, col[:, None] * inv_freq], axis=-1)
    return jnp.cos(ang), jnp.sin(ang)

def apply_rope(x, cos, sin):
    x32 = x.astype(jnp.float32)
    x1, x2 = x32[..., 0::2], x32[..., 1::2]
    c = cos[None, :, None, :]
    s = sin[None, :, None, :]
    y = jnp.stack([x1 * c - x2 * s, x1 * s + x2 * c], axis=-1)
    return y.reshape(x.shape).astype(x.dtype)

def context_attention(q, k, v):
    s = jnp.einsum('bqhd,bkhd->bhqk', q, k).astype(jnp.float32) * (NA_HEAD_DIM ** -0.5)
    p = jax.nn.softmax(s, axis=-1).astype(v.dtype)
    return jnp.einsum('bhqk,bkhd->bqhd', p, v)

def neighbourhood_attention(q, k, v, k_ctx, v_ctx, rpb, rows):
    B, L, H, Dh = q.shape
    kh = min(NA_KH, rows)
    kw = NA_KW
    scale = Dh ** -0.5
    kg = k.reshape(B, rows, GRID_W, H, Dh)
    vg = v.reshape(B, rows, GRID_W, H, Dh)
    q_rows = q.reshape(B, rows, GRID_W, H, Dh).transpose(1, 0, 2, 3, 4)
    col = np.arange(GRID_W)
    col_start = np.clip(col - kw // 2, 0, GRID_W - kw)
    col_idx = col_start[:, None] + np.arange(kw)[None, :]
    dc = col_idx - col[:, None] + (NA_KW - 1)
    n_win = kh * kw

    def row_block(args):
        r, q_row = args
        rs = jnp.clip(r - kh // 2, 0, rows - kh)
        k_rows = lax.dynamic_slice_in_dim(kg, rs, kh, axis=1)
        v_rows = lax.dynamic_slice_in_dim(vg, rs, kh, axis=1)
        k_win = k_rows[:, :, col_idx]
        v_win = v_rows[:, :, col_idx]
        dr = rs + jnp.arange(kh) - r + (NA_KH - 1)
        bias = rpb[:, dr][:, :, dc].astype(jnp.float32)
        s_win = jnp.einsum('bqhd,biqjhd->bhqij', q_row, k_win).astype(jnp.float32) * scale
        s_win = s_win + bias.transpose(0, 2, 1, 3)[None]
        s_ctx = jnp.einsum('bqhd,bchd->bhqc', q_row, k_ctx).astype(jnp.float32) * scale
        s = jnp.concatenate([s_win.reshape(B, H, GRID_W, n_win), s_ctx], axis=-1)
        p = jax.nn.softmax(s, axis=-1).astype(v.dtype)
        p_win = p[..., :n_win].reshape(B, H, GRID_W, kh, kw)
        p_ctx = p[..., n_win:]
        return (jnp.einsum('bhqij,biqjhd->bqhd', p_win, v_win)
                + jnp.einsum('bhqc,bchd->bqhd', p_ctx, v_ctx))

    out = lax.map(row_block, (jnp.arange(rows), q_rows))
    return out.transpose(1, 0, 2, 3, 4).reshape(B, L, H, Dh)

def merge_branches(pool_o, sgu_o, attn_o, gate_logits, w_po, w_so, w_ao, w_o):
    gp, gs, ga = jnp.split(jax.nn.sigmoid(gate_logits), N_BRANCH, axis=-1)
    y = gp * (pool_o @ w_po) + gs * (sgu_o @ w_so) + ga * (attn_o @ w_ao)
    return y @ w_o

def sq_relu_mlp(h, w1, w2):
    return jnp.square(jax.nn.relu(h @ w1)) @ w2

def first_inputs(seed: int = 0) -> dict:
    key = jax.random.key(seed)
    ks = jax.random.split(key, 21)
    D = D_MODEL

    def nrm(k, shape, scale):
        return jax.random.normal(k, shape, jnp.float32) * scale

    return {
        'x': nrm(ks[0], (BATCH, SEQ, D), 1.0),
        'c': nrm(ks[1], (BATCH, D), 1.0),
        'ctx': nrm(ks[2], (BATCH, CTX_LEN, D), 1.0),
        'c_ctx': nrm(ks[3], (D,), 1.0),
        'norm1_g': 1.0 + nrm(ks[4], (DEPTH, D), 0.05),
        'norm2_g': 1.0 + nrm(ks[5], (DEPTH, D), 0.05),
        'w_mod': nrm(ks[6], (DEPTH, D, 6 * D), 0.5 * D ** -0.5),
        'b_mod': nrm(ks[7], (DEPTH, 6 * D), 0.02),
        'w_in': nrm(ks[8], (DEPTH, D, PROJ_COLS), D ** -0.5),
        'w_pool': nrm(ks[9], (DEPTH, POOL_GROUPS, POOL_GROUP_DIM, POOL_GROUP_DIM), POOL_GROUP_DIM ** -0.5),
        'pool_scale': 1.0 + nrm(ks[10], (DEPTH, POOL_WIDTH), 0.1),
        'sgu_w': nrm(ks[11], (DEPTH, SGU_HEADS, SGU_CHUNK, SGU_CHUNK), SGU_CHUNK ** -0.5),
        'sgu_b': 1.0 + nrm(ks[12], (DEPTH, SGU_HEADS, SGU_CHUNK), 0.1),
        'na_rpb': nrm(ks[13], (DEPTH, NA_HEADS, 2 * NA_KH - 1, 2 * NA_KW - 1), 0.5),
        'w_pool_out': nrm(ks[14], (DEPTH, POOL_WIDTH, D), POOL_WIDTH ** -0.5),
        'w_sgu_out': nrm(ks[15], (DEPTH, SGU_WIDTH, D), SGU_WIDTH ** -0.5),
        'w_attn_out': nrm(ks[16], (DEPTH, NA_WIDTH, D), NA_WIDTH ** -0.5),
        'w_o': nrm(ks[17], (DEPTH, D, D), D ** -0.5),
        'w_ff1': nrm(ks[18], (DEPTH, D, D_FF), D ** -0.5),
        'w_ff2': nrm(ks[19], (DEPTH, D_FF, D), D_FF ** -0.5),
        'final_g': 1.0 + nrm(ks[20], (D,), 0.05),
    }

def first_block(x, c, ctx, c_ctx, norm1_g, norm2_g, w_mod, b_mod, w_in, w_pool, pool_scale,
              sgu_w, sgu_b, na_rpb, w_pool_out, w_sgu_out, w_attn_out, w_o, w_ff1, w_ff2, final_g):
    n_lat = x.shape[1]
    rows = n_lat // GRID_W
    cos, sin = axial_rope(n_lat)
    silu_c = jax.nn.silu(c)
    silu_cc = jax.nn.silu(c_ctx)
    h, hc = x, ctx
    for l in range(DEPTH):
        mod = silu_c @ w_mod[l] + b_mod[l]
        mod_c = silu_cc @ w_mod[l] + b_mod[l]
        sh1, sc1, g1, sh2, sc2, g2 = jnp.split(mod[:, None, :], 6, axis=-1)
        csh1, csc1, cg1, csh2, csc2, cg2 = jnp.split(mod_c, 6, axis=-1)
        has_ctx_out = l < DEPTH - 1

        ac = modulate(rms_norm(hc, norm1_g[l]), csh1, csc1)
        if has_ctx_out:
            p, u, vs, q, k, v, gl = jnp.split(ac @ w_in[l], SPLIT_POINTS, axis=-1)
            k_ctx, v_ctx = to_heads(k), to_heads(v)
            attn_c = context_attention(to_heads(q), k_ctx, v_ctx).reshape(hc.shape[0], hc.shape[1], NA_WIDTH)
            mix_c = merge_branches(pool_mix(p, w_pool[l], pool_scale[l]), sgu_mix(u, vs, sgu_w[l], sgu_b[l]),
                                   attn_c, gl, w_pool_out[l], w_sgu_out[l], w_attn_out[l], w_o[l])
        else:
            k, v = jnp.split(ac @ w_in[l][:, Q_END:V_END], 2, axis=-1)
            k_ctx, v_ctx = to_heads(k), to_heads(v)

        a = modulate(rms_norm(h, norm1_g[l]), sh1, sc1)
        p, u, vs, q, k, v, gl = jnp.split(a @ w_in[l], SPLIT_POINTS, axis=-1)
        attn = neighbourhood_attention(apply_rope(to_heads(q), cos, sin), apply_rope(to_heads(k), cos, sin),
                                       to_heads(v), k_ctx, v_ctx, na_rpb[l], rows)
        mix = merge_branches(pool_mix(p, w_pool[l], pool_scale[l]), sgu_mix(u, vs, sgu_w[l], sgu_b[l]),
                             attn.reshape(h.shape[0], n_lat, NA_WIDTH), gl,
                             w_pool_out[l], w_sgu_out[l], w_attn_out[l], w_o[l])
        h = h + g1 * mix
        h = h + g2 * sq_relu_mlp(modulate(rms_norm(h, norm2_g[l]), sh2, sc2), w_ff1[l], w_ff2[l])

        if has_ctx_out:
            hc = hc + cg1 * mix_c
            hc = hc + cg2 * sq_relu_mlp(modulate(rms_norm(hc, norm2_g[l]), csh2, csc2), w_ff1[l], w_ff2[l])
    return rms_norm(h, final_g)


N_MIXERS = 3
D_FF_2 = 4 * D_MODEL
NORM_EPS = 1e-6
ROPE_BASE = 10000.0

A_HEADS = 8
A_DQK = D_MODEL // (2 * A_HEADS)
A_DV = D_MODEL // A_HEADS
A_CHUNK = 128
A_IN = 2 * A_HEADS * A_DQK + A_HEADS * A_DV + D_MODEL + 4 * A_HEADS

SWA_HEADS = 16
SWA_KV_HEADS = 4
SWA_DH = D_MODEL // SWA_HEADS
SWA_GROUP = SWA_HEADS // SWA_KV_HEADS
WINDOW = 128
SWA_BLOCK = WINDOW
SWA_IN = (SWA_HEADS + 2 * SWA_KV_HEADS) * SWA_DH

DIFF_HEADS = 8
DIFF_DH = D_MODEL // (2 * DIFF_HEADS)
DIFF_DV = 2 * DIFF_DH
DIFF_BLOCK = 128
DIFF_IN = 4 * DIFF_HEADS * DIFF_DH + DIFF_HEADS * DIFF_DV

N_MLSTM = (DEPTH + N_MIXERS - 1) // N_MIXERS
N_SWA = (DEPTH + N_MIXERS - 2) // N_MIXERS
N_DIFF = (DEPTH + N_MIXERS - 3) // N_MIXERS


F32 = jnp.float32

def _rms_norm(x, g):
    xf = x.astype(F32)
    y = xf * lax.rsqrt(jnp.mean(xf * xf, axis=-1, keepdims=True) + NORM_EPS)
    return (y * g.astype(F32)).astype(x.dtype)

def _modulate(x, shift, scale):
    return x * (1.0 + scale) + shift

def _sq_relu_mlp(u, w1, w2):
    return jnp.square(jax.nn.relu(u @ w1)) @ w2

def _axial_rope_tables(n_tok, head_dim):
    rows = n_tok // GRID_W
    row = jnp.repeat(jnp.arange(rows, dtype=jnp.int32), GRID_W).astype(F32)
    col = jnp.tile(jnp.arange(GRID_W, dtype=jnp.int32), rows).astype(F32)
    quarter = head_dim // 4
    inv = ROPE_BASE ** (-jnp.arange(quarter, dtype=F32) / quarter)
    ang = jnp.concatenate([row[:, None] * inv, col[:, None] * inv], axis=-1)
    return jnp.cos(ang), jnp.sin(ang)

def _apply_rope(x, cos, sin):
    half = x.shape[-1] // 2
    x1, x2 = x[..., :half], x[..., half:]
    cs = cos[:, None, :].astype(x.dtype)
    sn = sin[:, None, :].astype(x.dtype)
    return jnp.concatenate([x1 * cs - x2 * sn, x1 * sn + x2 * cs], axis=-1)

def _to_chunks(t):
    bsz, n, h = t.shape[:3]
    t = t.reshape((bsz, n // A_CHUNK, A_CHUNK, h) + t.shape[3:])
    return jnp.moveaxis(t, 3, 1)

def _from_chunks(t):
    t = jnp.moveaxis(t, 1, 3)
    return t.reshape((t.shape[0], t.shape[1] * t.shape[2]) + t.shape[3:])

def _mlstm_direction(q, k, v, log_i, log_f, state, need_out):
    k_c, v_c = _to_chunks(k), _to_chunks(v)
    li, lf = _to_chunks(log_i), _to_chunks(log_f)
    b = jnp.cumsum(lf, axis=-1)
    b_last = b[..., -1]
    a = b_last[..., None] - b + li
    g = jnp.max(a, axis=-1)
    w = jnp.exp(a - g[..., None])
    kv = jnp.einsum("bhcs,bhcsd,bhcse->bhcde", w, k_c, v_c)
    kn = jnp.einsum("bhcs,bhcsd->bhcd", w, k_c)

    def step(carry, xs):
        c_st, n_st, m_st = carry
        bl, gj, kvj, knj = xs
        m_new = jnp.maximum(bl + m_st, gj)
        decay = jnp.exp(bl + m_st - m_new)
        inject = jnp.exp(gj - m_new)
        c_new = decay[..., None, None] * c_st + inject[..., None, None] * kvj
        n_new = decay[..., None] * n_st + inject[..., None] * knj
        return (c_new, n_new, m_new), (c_st, n_st, m_st)

    xs = (jnp.moveaxis(b_last, 2, 0), jnp.moveaxis(g, 2, 0), jnp.moveaxis(kv, 2, 0), jnp.moveaxis(kn, 2, 0))
    final, starts = lax.scan(step, state, xs)
    if not need_out:
        return None, final
    c0 = jnp.moveaxis(starts[0], 0, 2)
    n0 = jnp.moveaxis(starts[1], 0, 2)
    m0 = jnp.moveaxis(starts[2], 0, 2)
    q_c = _to_chunks(q)
    L = q_c.shape[-2]
    d = b[..., :, None] - b[..., None, :] + li[..., None, :]
    d = jnp.where(jnp.tril(jnp.ones((L, L), dtype=bool)), d, -jnp.inf)
    inter = b + m0[..., None]
    m_t = jnp.maximum(jnp.max(d, axis=-1), inter)
    wq = jnp.exp(d - m_t[..., None]) * jnp.einsum("bhctd,bhcsd->bhcts", q_c, k_c)
    carry_w = jnp.exp(inter - m_t)
    num = jnp.einsum("bhcts,bhcse->bhcte", wq, v_c) + carry_w[..., None] * jnp.einsum("bhctd,bhcde->bhcte", q_c, c0)
    den = jnp.sum(wq, axis=-1) + carry_w * jnp.einsum("bhctd,bhcd->bhct", q_c, n0)
    h = num / jnp.maximum(jnp.abs(den), jnp.exp(-m_t))[..., None]
    return _from_chunks(h), final

def _mlstm_mixer(u_ctx, u_lat, w_in, gate_b, head_norm, w_out, need_ctx):
    qk = A_HEADS * A_DQK
    vd = A_HEADS * A_DV
    splits = [qk, 2 * qk, 2 * qk + vd, 2 * qk + vd + D_MODEL]

    def project(u):
        bsz, n = u.shape[:2]
        q, k, v, o, gates = jnp.split(u @ w_in, splits, axis=-1)
        q = q.astype(F32).reshape(bsz, n, A_HEADS, A_DQK)
        k = k.astype(F32).reshape(bsz, n, A_HEADS, A_DQK) * (A_DQK ** -0.5)
        v = v.astype(F32).reshape(bsz, n, A_HEADS, A_DV)
        gates = gates.astype(F32).reshape(bsz, n, 4, A_HEADS) + gate_b.astype(F32)
        fwd = (gates[:, :, 0], jax.nn.log_sigmoid(gates[:, :, 1]))
        bwd = (gates[:, :, 2], jax.nn.log_sigmoid(gates[:, :, 3]))
        return q, k, v, o, fwd, bwd

    def flip(t):
        return jnp.flip(t, axis=1)

    cq, ck, cv, co, cf, cb = project(u_ctx)
    lq, lk, lv, lo, lf, lb = project(u_lat)
    bsz = u_lat.shape[0]
    zero = (jnp.zeros((bsz, A_HEADS, A_DQK, A_DV), F32), jnp.zeros((bsz, A_HEADS, A_DQK), F32),
            jnp.zeros((bsz, A_HEADS), F32))
    hcf, st_f = _mlstm_direction(cq, ck, cv, cf[0], cf[1], zero, need_ctx)
    hcb, st_b = _mlstm_direction(flip(cq), flip(ck), flip(cv), flip(cb[0]), flip(cb[1]), zero, need_ctx)
    hlf, _ = _mlstm_direction(lq, lk, lv, lf[0], lf[1], st_f, True)
    hlb, _ = _mlstm_direction(flip(lq), flip(lk), flip(lv), flip(lb[0]), flip(lb[1]), st_b, True)

    def finish(hf, hb, o):
        hs = hf + flip(hb)
        hn = hs * lax.rsqrt(jnp.mean(hs * hs, axis=-1, keepdims=True) + NORM_EPS)
        hn = hn * head_norm.astype(F32).reshape(A_HEADS, A_DV)
        bsz_, n = hs.shape[:2]
        return (hn.reshape(bsz_, n, vd).astype(o.dtype) * jax.nn.sigmoid(o)) @ w_out

    y_lat = finish(hlf, hlb, lo)
    y_ctx = finish(hcf, hcb, co) if need_ctx else None
    return y_lat, y_ctx

def _swa_mixer(u_ctx, u_lat, w_in, sink, w_out, cos, sin, need_ctx):
    scale = SWA_DH ** -0.5
    sink_g = sink.astype(F32).reshape(SWA_KV_HEADS, SWA_GROUP)[:, :, None]

    def project(u):
        bsz, n = u.shape[:2]
        q, k, v = jnp.split(u @ w_in, [SWA_HEADS * SWA_DH, (SWA_HEADS + SWA_KV_HEADS) * SWA_DH], axis=-1)
        return (q.reshape(bsz, n, SWA_HEADS, SWA_DH), k.reshape(bsz, n, SWA_KV_HEADS, SWA_DH),
                v.reshape(bsz, n, SWA_KV_HEADS, SWA_DH))

    cq, ck, cv = project(u_ctx)
    lq, lk, lv = project(u_lat)
    lq = _apply_rope(lq, cos, sin)
    lk = _apply_rope(lk, cos, sin)
    bsz, n_tok = u_lat.shape[:2]
    nb = n_tok // SWA_BLOCK
    kp = jnp.pad(lk, ((0, 0), (SWA_BLOCK, SWA_BLOCK), (0, 0), (0, 0)))
    vp = jnp.pad(lv, ((0, 0), (SWA_BLOCK, SWA_BLOCK), (0, 0), (0, 0)))
    q_blocks = jnp.moveaxis(lq.reshape(bsz, nb, SWA_BLOCK, SWA_KV_HEADS, SWA_GROUP, SWA_DH), 1, 0)
    q_idx = jnp.arange(SWA_BLOCK)[:, None]
    k_idx = jnp.arange(3 * SWA_BLOCK)[None, :]
    rel = k_idx - SWA_BLOCK - q_idx

    def block(args):
        j, qb = args
        kb = lax.dynamic_slice_in_dim(kp, j * SWA_BLOCK, 3 * SWA_BLOCK, axis=1)
        vb = lax.dynamic_slice_in_dim(vp, j * SWA_BLOCK, 3 * SWA_BLOCK, axis=1)
        kpos = j * SWA_BLOCK - SWA_BLOCK + k_idx
        valid = (jnp.abs(rel) <= WINDOW) & (kpos >= 0) & (kpos < n_tok)
        s_lat = jnp.einsum("bqhgd,bkhd->bhgqk", qb, kb).astype(F32) * scale
        s_lat = jnp.where(valid, s_lat, -jnp.inf)
        s_ctx = jnp.einsum("bqhgd,bchd->bhgqc", qb, ck).astype(F32) * scale
        m = jnp.maximum(jnp.maximum(jnp.max(s_lat, -1), jnp.max(s_ctx, -1)), sink_g)
        p_lat = jnp.exp(s_lat - m[..., None])
        p_ctx = jnp.exp(s_ctx - m[..., None])
        den = jnp.sum(p_lat, -1) + jnp.sum(p_ctx, -1) + jnp.exp(sink_g - m)
        o = jnp.einsum("bhgqk,bkhd->bqhgd", p_lat, vb) + jnp.einsum("bhgqc,bchd->bqhgd", p_ctx, cv)
        return o / jnp.moveaxis(den, 3, 1)[..., None]

    o_lat = lax.map(block, (jnp.arange(nb), q_blocks))
    o_lat = jnp.moveaxis(o_lat, 0, 1).reshape(bsz, n_tok, SWA_HEADS * SWA_DH)
    y_lat = o_lat.astype(u_lat.dtype) @ w_out
    if not need_ctx:
        return y_lat, None
    n_ctx = u_ctx.shape[1]
    cqg = cq.reshape(bsz, n_ctx, SWA_KV_HEADS, SWA_GROUP, SWA_DH)
    s = jnp.einsum("bqhgd,bchd->bhgqc", cqg, ck).astype(F32) * scale
    m = jnp.maximum(jnp.max(s, -1), sink_g)
    p = jnp.exp(s - m[..., None])
    den = jnp.sum(p, -1) + jnp.exp(sink_g - m)
    o_ctx = jnp.einsum("bhgqc,bchd->bqhgd", p, cv) / jnp.moveaxis(den, 3, 1)[..., None]
    y_ctx = o_ctx.reshape(bsz, n_ctx, SWA_HEADS * SWA_DH).astype(u_ctx.dtype) @ w_out
    return y_lat, y_ctx

def _diff_mixer(u_ctx, u_lat, w_in, lam_q1, lam_k1, lam_q2, lam_k2, head_norm, w_out, cos, sin,
                layer_idx, need_ctx):
    scale = DIFF_DH ** -0.5
    lam_init = 0.8 - 0.6 * math.exp(-0.3 * layer_idx)
    lam = (jnp.exp(jnp.sum(lam_q1.astype(F32) * lam_k1.astype(F32)))
           - jnp.exp(jnp.sum(lam_q2.astype(F32) * lam_k2.astype(F32))) + lam_init)
    qk = 2 * DIFF_HEADS * DIFF_DH

    def project(u, rope):
        bsz, n = u.shape[:2]
        q, k, v = jnp.split(u @ w_in, [qk, 2 * qk], axis=-1)
        q = q.reshape(bsz, n, 2 * DIFF_HEADS, DIFF_DH)
        k = k.reshape(bsz, n, 2 * DIFF_HEADS, DIFF_DH)
        if rope:
            q = _apply_rope(q, cos, sin)
            k = _apply_rope(k, cos, sin)
        return (q.reshape(bsz, n, DIFF_HEADS, 2, DIFF_DH), k.reshape(bsz, n, DIFF_HEADS, 2, DIFF_DH),
                v.reshape(bsz, n, DIFF_HEADS, DIFF_DV))

    def finish(o, dtype):
        od = o[:, :, :, 0] - lam * o[:, :, :, 1]
        od = od * lax.rsqrt(jnp.mean(od * od, axis=-1, keepdims=True) + NORM_EPS)
        od = od * head_norm.astype(F32).reshape(DIFF_HEADS, DIFF_DV) * (1.0 - lam_init)
        bsz, n = od.shape[:2]
        return od.reshape(bsz, n, DIFF_HEADS * DIFF_DV).astype(dtype) @ w_out

    cq, ck, cv = project(u_ctx, False)
    lq, lk, lv = project(u_lat, True)
    bsz, n_tok = u_lat.shape[:2]
    nb = n_tok // DIFF_BLOCK
    q_blocks = jnp.moveaxis(lq.reshape(bsz, nb, DIFF_BLOCK, DIFF_HEADS, 2, DIFF_DH), 1, 0)

    def block(qb):
        s_lat = jnp.einsum("bqhmd,bkhmd->bhmqk", qb, lk).astype(F32) * scale
        s_ctx = jnp.einsum("bqhmd,bchmd->bhmqc", qb, ck).astype(F32) * scale
        mx = jnp.maximum(jnp.max(s_lat, -1), jnp.max(s_ctx, -1))[..., None]
        p_lat = jnp.exp(s_lat - mx)
        p_ctx = jnp.exp(s_ctx - mx)
        den = jnp.sum(p_lat, -1) + jnp.sum(p_ctx, -1)
        o = jnp.einsum("bhmqk,bkhe->bqhme", p_lat, lv) + jnp.einsum("bhmqc,bche->bqhme", p_ctx, cv)
        return o / jnp.moveaxis(den, 3, 1)[..., None]

    o_lat = lax.map(block, q_blocks)
    o_lat = jnp.moveaxis(o_lat, 0, 1).reshape(bsz, n_tok, DIFF_HEADS, 2, DIFF_DV)
    y_lat = finish(o_lat, u_lat.dtype)
    if not need_ctx:
        return y_lat, None
    s = jnp.einsum("bqhmd,bkhmd->bhmqk", cq, ck).astype(F32) * scale
    a = jax.nn.softmax(s, axis=-1)
    o_ctx = jnp.einsum("bhmqk,bkhe->bqhme", a, cv)
    return y_lat, finish(o_ctx, u_ctx.dtype)

def second_inputs(seed: int = 0) -> dict:
    key = jax.random.key(seed)
    ks = jax.random.split(key, 25)
    D = D_MODEL

    def nrm(k, shape, scale):
        return jax.random.normal(k, shape, F32) * scale

    forget_bias = jnp.linspace(3.0, 6.0, A_HEADS, dtype=F32)
    zeros_h = jnp.zeros((A_HEADS,), F32)
    gate_base = jnp.stack([zeros_h, forget_bias, zeros_h, forget_bias])
    return {
        "x": nrm(ks[0], (BATCH, SEQ, D), 1.0),
        "c": nrm(ks[1], (BATCH, D), 1.0),
        "ctx": nrm(ks[2], (BATCH, CTX_LEN, D), 1.0),
        "c_ctx": nrm(ks[3], (D,), 1.0),
        "ada_w": nrm(ks[4], (DEPTH, D, 6 * D), 0.5 * D ** -0.5),
        "ada_b": nrm(ks[5], (DEPTH, 6 * D), 0.02),
        "norm_mix": 1.0 + nrm(ks[6], (DEPTH, D), 0.02),
        "norm_ffn": 1.0 + nrm(ks[7], (DEPTH, D), 0.02),
        "ffn_w1": nrm(ks[8], (DEPTH, D, D_FF_2), D ** -0.5),
        "ffn_w2": nrm(ks[9], (DEPTH, D_FF_2, D), D_FF_2 ** -0.5),
        "mlstm_w_in": nrm(ks[10], (N_MLSTM, D, A_IN), D ** -0.5),
        "mlstm_gate_b": gate_base + nrm(ks[11], (N_MLSTM, 4, A_HEADS), 0.1),
        "mlstm_head_norm": 1.0 + nrm(ks[12], (N_MLSTM, A_HEADS * A_DV), 0.02),
        "mlstm_w_out": nrm(ks[13], (N_MLSTM, A_HEADS * A_DV, D), (A_HEADS * A_DV) ** -0.5),
        "swa_w_in": nrm(ks[14], (N_SWA, D, SWA_IN), D ** -0.5),
        "swa_sink": nrm(ks[15], (N_SWA, SWA_HEADS), 0.5),
        "swa_w_out": nrm(ks[16], (N_SWA, SWA_HEADS * SWA_DH, D), (SWA_HEADS * SWA_DH) ** -0.5),
        "diff_w_in": nrm(ks[17], (N_DIFF, D, DIFF_IN), D ** -0.5),
        "diff_lambda_q1": nrm(ks[18], (N_DIFF, DIFF_DH), 0.1),
        "diff_lambda_k1": nrm(ks[19], (N_DIFF, DIFF_DH), 0.1),
        "diff_lambda_q2": nrm(ks[20], (N_DIFF, DIFF_DH), 0.1),
        "diff_lambda_k2": nrm(ks[21], (N_DIFF, DIFF_DH), 0.1),
        "diff_head_norm": 1.0 + nrm(ks[22], (N_DIFF, DIFF_HEADS * DIFF_DV), 0.02),
        "diff_w_out": nrm(ks[23], (N_DIFF, DIFF_HEADS * DIFF_DV, D), (DIFF_HEADS * DIFF_DV) ** -0.5),
        "final_norm": 1.0 + nrm(ks[24], (D,), 0.02),
    }

def second_block(x, c, ctx, c_ctx, ada_w, ada_b, norm_mix, norm_ffn, ffn_w1, ffn_w2,
              mlstm_w_in, mlstm_gate_b, mlstm_head_norm, mlstm_w_out,
              swa_w_in, swa_sink, swa_w_out,
              diff_w_in, diff_lambda_q1, diff_lambda_k1, diff_lambda_q2, diff_lambda_k2,
              diff_head_norm, diff_w_out, final_norm):
    n_tok = x.shape[1]
    cos_s, sin_s = _axial_rope_tables(n_tok, SWA_DH)
    cos_d, sin_d = _axial_rope_tables(n_tok, DIFF_DH)
    cond_lat = jax.nn.silu(c)[:, None, :]
    cond_ctx = jax.nn.silu(c_ctx)[None, None, :]
    h, hc = x, ctx
    for i in range(DEPTH):
        kind, slot = i % N_MIXERS, i // N_MIXERS
        need_ctx = i < DEPTH - 1
        mod_l = jnp.split(cond_lat @ ada_w[i] + ada_b[i], 6, axis=-1)
        mod_c = jnp.split(cond_ctx @ ada_w[i] + ada_b[i], 6, axis=-1)
        u = _modulate(_rms_norm(h, norm_mix[i]), mod_l[0], mod_l[1])
        uc = _modulate(_rms_norm(hc, norm_mix[i]), mod_c[0], mod_c[1])
        if kind == 0:
            y, yc = _mlstm_mixer(uc, u, mlstm_w_in[slot], mlstm_gate_b[slot], mlstm_head_norm[slot],
                                 mlstm_w_out[slot], need_ctx)
        elif kind == 1:
            y, yc = _swa_mixer(uc, u, swa_w_in[slot], swa_sink[slot], swa_w_out[slot], cos_s, sin_s, need_ctx)
        else:
            y, yc = _diff_mixer(uc, u, diff_w_in[slot], diff_lambda_q1[slot], diff_lambda_k1[slot],
                                diff_lambda_q2[slot], diff_lambda_k2[slot], diff_head_norm[slot],
                                diff_w_out[slot], cos_d, sin_d, i, need_ctx)
        h = h + mod_l[2] * y
        h = h + mod_l[5] * _sq_relu_mlp(_modulate(_rms_norm(h, norm_ffn[i]), mod_l[3], mod_l[4]),
                                        ffn_w1[i], ffn_w2[i])
        if need_ctx:
            hc = hc + mod_c[2] * yc
            hc = hc + mod_c[5] * _sq_relu_mlp(_modulate(_rms_norm(hc, norm_ffn[i]), mod_c[3], mod_c[4]),
                                              ffn_w1[i], ffn_w2[i])
    return _rms_norm(h, final_norm)


def setup_inputs(seed=0):
    out = dict(first_inputs(seed))
    for name, value in second_inputs(seed + 1).items():
        if name != "x":
            out[name + "_2"] = value
    return out


def reference(
    x, c, ctx, c_ctx, norm1_g, norm2_g, w_mod, b_mod, w_in, w_pool, pool_scale, sgu_w, sgu_b,
    na_rpb, w_pool_out, w_sgu_out, w_attn_out, w_o, w_ff1, w_ff2, final_g, c_2, ctx_2, c_ctx_2,
    ada_w_2, ada_b_2, norm_mix_2, norm_ffn_2, ffn_w1_2, ffn_w2_2, mlstm_w_in_2, mlstm_gate_b_2,
    mlstm_head_norm_2, mlstm_w_out_2, swa_w_in_2, swa_sink_2, swa_w_out_2, diff_w_in_2,
    diff_lambda_q1_2, diff_lambda_k1_2, diff_lambda_q2_2, diff_lambda_k2_2, diff_head_norm_2,
    diff_w_out_2, final_norm_2,
):
    x = first_block(
        x, c, ctx, c_ctx, norm1_g, norm2_g, w_mod, b_mod, w_in, w_pool, pool_scale, sgu_w,
        sgu_b, na_rpb, w_pool_out, w_sgu_out, w_attn_out, w_o, w_ff1, w_ff2, final_g,
    )
    return second_block(
        x, c_2, ctx_2, c_ctx_2, ada_w_2, ada_b_2, norm_mix_2, norm_ffn_2, ffn_w1_2, ffn_w2_2,
        mlstm_w_in_2, mlstm_gate_b_2, mlstm_head_norm_2, mlstm_w_out_2, swa_w_in_2, swa_sink_2,
        swa_w_out_2, diff_w_in_2, diff_lambda_q1_2, diff_lambda_k1_2, diff_lambda_q2_2,
        diff_lambda_k2_2, diff_head_norm_2, diff_w_out_2, final_norm_2,
    )


_drawn_inputs = setup_inputs


def setup_inputs(seed=0):
    import zlib

    import numpy as np

    out = dict(_drawn_inputs(seed))
    spreads = {}
    factors = {'na_rpb': 7.042,
     'norm_mix_2': 6.592,
     'norm_ffn_2': 4.599,
     'mlstm_head_norm_2': 8.0,
     'swa_sink_2': 8.0,
     'final_norm_2': 2.797}
    for name, (base, spread) in spreads.items():
        noise = np.random.default_rng([zlib.crc32(name.encode()), seed]).standard_normal(out[name].shape)
        drawn = base * np.exp(spread * noise) if base else spread * noise
        out[name] = jnp.asarray(drawn.astype(out[name].dtype))
    for name, factor in factors.items():
        out[name] = (out[name] * factor).astype(out[name].dtype)
    return out
```

```python
from contextlib import ExitStack

import numpy as np
import concourse.bass as bass
from concourse import mybir

F32 = mybir.dt.float32
ALU = mybir.AluOpType
ACT = mybir.ActivationFunctionType
AX_X = mybir.AxisListType.X

P = 128
D = 1024
KC = D // P
LAT = 256
CTX = 256
ALL = LAT + CTX
DFF = 4 * D
EPS = 1e-6
NEG = -1e30
GRID = 64
HD = 64
QSCALE = HD ** -0.5
RPB_H, RPB_W = 15, 31
SLOTS = 3
MH = 8
MDV = D // MH

V_COND = 0
V_BMOD = V_COND + 2 * KC * 2
V_N1 = V_BMOD + 4 * 48
V_N2 = V_N1 + 4 * KC
V_FIN = V_N2 + 4 * KC
V_PS = V_FIN + 2 * KC
V_HN = V_PS + 4
V_END = V_HN + MH

A_POOL, A_SGU, A_WP = 0, 2048, 2560
A_ROPE, A_MASK, A_SIZE = 2816, 3328, 3840
A_MF, A_MB = 0, 1024


def make_plan():
    phases = []
    n = dict(t=0, u=0, norm=0, head=0, mu=0, aux=0)

    def phase(kind, tiles=0, units=0, **kw):
        ph = dict(kind=kind, t=n["t"], u=n["u"], norm=n["norm"], head=n["head"], mu=n["mu"],
                  tiles=tiles, units=units, **kw)
        phases.append(ph)
        n["t"] += tiles
        n["u"] += units
        return ph

    for layer in range(4):
        block, l = layer // 2, layer % 2
        cols = ALL if l == 0 else LAT
        base = dict(layer=layer, block=block, l=l, cols=cols)
        if l == 0:
            phase("load_ctx", **base)
        phase("aux", aux=n["aux"], **base)
        n["aux"] += 1
        phase("mod", tiles=12, units=1, **base)
        phase("norm", final=False, which=0, width=ALL, **base)
        n["norm"] += 1
        if block == 0:
            phase("b1_in", tiles=5, units=cols // P + 2 + cols // P + 4 + 4 + 4, **base)
            phase("rope", units=8, chunks=8, **base)
            phase("pool_sgu", units=6, **base)
            phase("b1_gates", tiles=6, units=24, **base)
            heads = [("lat", h) for h in range(8)] + ([("ctx", h) for h in range(8)] if l == 0 else [])
            phase("attn", heads=heads, **base)
            n["head"] += len(heads)
            phase("merge", tiles=2, units=24, **base)
            phase("to_h", tiles=2, units=8, kb=1, src="y", gate=2, name="w_o", **base)
        elif l == 0:
            phase("m_in", tiles=7, units=4 + 4 + 8 + 8 + 4, **base)
            phase("m_gates", units=1, **base)
            phase("m_heads", **base)
            n["mu"] += 4 * MH
            phase("m_norm", units=8, **base)
            phase("to_h", tiles=2, units=8, kb=1, src="hs", gate=2, name="m_out", **base)
        else:
            phase("s_in", tiles=3, units=8 + 2 + 4, **base)
            phase("rope", units=10, chunks=10, **base)
            heads = [("lat", h) for h in range(16)]
            phase("attn", heads=heads, **base)
            n["head"] += len(heads)
            phase("to_h", tiles=2, units=8, kb=1, src="attn", gate=2, name="s_out", **base)
        phase("norm", final=False, which=1, width=cols, **base)
        n["norm"] += 1
        phase("ff1", tiles=8, units=32, **base)
        phase("to_h", tiles=8, units=8, kb=4, src="ff", gate=5, name="ff2", **base)
        if l == 1:
            phase("norm", final=True, which=2, width=LAT, **base)
            n["norm"] += 1
    phase("store")
    return phases


def build(nc, io):
    plan = make_plan()
    ctx = ExitStack()
    with ctx:
        def sb(name, shape):
            return ctx.enter_context(nc.sbuf_tensor(name, shape, F32))

        def sem(name):
            return ctx.enter_context(nc.semaphore(name))

        ring = sb("ring", [P, SLOTS, KC, 512])
        h = sb("h", [P, KC, ALL])
        a = sb("a", [P, KC, ALL])
        big = sb("big", [P, 32, 512])
        mid = sb("mid", [P, 16 * 256])
        bias = sb("bias", [P, 2, 2, LAT])
        scr = sb("scr", [P, 2, 2, 512])
        pt = sb("pt", [P, 2, 2, 4, P])
        aux = sb("aux", [P, A_SIZE])
        rot = sb("rot", [P, 2, P])
        ident = sb("ident", [P, P])
        ones = sb("ones", [P, P])
        ones_h = sb("ones_h", [P, P])
        sel = sb("sel", [MH, MH, P])
        vec = sb("vec", [P, V_END])
        silu = sb("silu", [P, 2, KC, 2])
        mod = sb("mod", [P, 48, 2])
        gain = sb("gain", [P, 2, KC, 2])
        sgub = sb("sgub", [4, 2, P])
        gateb = sb("gateb", [MH, 4])
        sink = sb("sink", [P, 16])
        nmax = sb("nmax", [P, 2, 2])
        rsum = sb("rsum", [P, 2, 2])
        esink = sb("esink", [P, 2, 2])
        rinv = sb("rinv", [P, 2, 2])
        lnst = sb("lnst", [P, 8])
        tm = sb("tm", [P, 2, 4, MH, 2])
        den = sb("den", [P, 2, 2, 2])
        pscr = scr[:, 0, :, :]
        PS = ctx.enter_context(nc.psum_tensor("PS", [P, 8, 512], F32))

        sig = big[:, 0:24, :]
        qT = big[:, 24:28, :]
        kT = big[:, 28:32, :]
        v_tm = mid[:, 0:2048].rearrange("p (t n) -> p t n", t=4)
        uT = mid[:, 2048:3072].rearrange("p (c n) -> p c n", c=2)
        p_tm = mid[:, 3072:4096].rearrange("p (t n) -> p t n", t=4)
        poolT = mid[:, 3072:4096].rearrange("p (c n) -> p c n", c=2)
        vs_tm = scr[:, 0, :, :].rearrange("p a n -> p (a n)").rearrange("p (t n) -> p t n", t=4)
        pooled = pt[:, 0, :, :, :].rearrange("p a b n -> p (a b n)").rearrange("p (c n) -> p c n", c=2)
        mq = big[:, 0:4, :]
        mk = big[:, 4:8, :]
        sigo = big[:, 8:16, :]
        hs = big[:, 16:24, :]
        G = big[0:MH, 24:28, :]
        Bc = big[0:MH, 28:30, :]
        one_row = big[0:MH, 30, :]
        mv = mid[:, :].rearrange("p (t n) -> p t n", t=4)
        sq_ = big[:, 0:8, 0:LAT]
        sk = big[:, 8:10, :]
        sv = big[:, 10:12, :].rearrange("p a n -> p (a n)").rearrange("p (t n) -> p t n", t=4)
        sqb = scr[:, 0, :, :]
        nrm = scr[:, 1, :, :]
        rs = pt[:, 1, 0, :, :].rearrange("p b n -> p (b n)")

        s_const = sem("const_loaded")
        s_slot = [sem(f"weights_loaded_{i}") for i in range(SLOTS)]
        s_wused = sem("weight_tile_used")
        s_ctxld = sem("context_loaded")
        s_aux = sem("tables_loaded")
        s_unit = sem("unit_done")
        s_free = [sem(f"bank_evacuated_{i}") for i in range(4)]
        s_silu = sem("silu_ready")
        s_silu_a = sem("silu_sigmoid")
        s_gain = sem("gain_ready")
        s_sq = sem("squares_ready")
        s_squsd = sem("squares_used")
        s_var = sem("variance_ready")
        s_std = sem("std_ready")
        s_nrm = sem("normed_ready")
        s_a = sem("input_ready")
        s_dve = sem("dve_step")
        s_act = sem("act_step")
        s_pool = sem("pool_step")
        s_ff = sem("hidden_ready")
        s_bias = sem("bias_ready")
        s_biasld = sem("bias_loaded")
        s_sc = sem("scores_done")
        s_nm = sem("max_ready")
        s_exp = sem("exp_done")
        s_rinv = sem("rinv_ready")
        s_prob = sem("probs_ready")
        s_tr = sem("transposed")
        s_pta = sem("probsT_by_act")
        s_ptd = sem("probsT_by_dve")
        s_pv = sem("pv_done")
        s_o = sem("attn_out_ready")
        s_sgu = sem("sgu_normed")
        s_lnv = sem("ln_var")
        s_lns = sem("ln_std")
        s_ga = sem("gate_exp")
        s_gd = sem("gate_rows_ready")
        s_gr = sem("guard_ready")
        s_qk = sem("m_qk_done")
        s_D = sem("m_decay_args")
        s_A = sem("m_decay_ready")
        s_W = sem("m_weighted")
        s_P = sem("m_probs_ready")
        s_mt = sem("m_transposed")
        s_mpt = sem("m_probsT_ready")
        s_mpv = sem("m_pv_done")
        s_mo = sem("m_out_ready")
        s_msq = sem("m_squares")
        s_mrs = sem("m_var_sqrt")
        s_hn = sem("m_normed")
        s_hs = sem("m_gated")
        s_out = sem("out_stored")

        tiles = []

        def rows(w, k=KC):
            return w.rearrange("(k p) n -> p k n", p=P)

        for ph in plan:
            if not ph.get("tiles"):
                continue
            slot = lambda: ring[:, len(tiles) % SLOTS, :, :]
            l, b = ph["l"], ph["block"]
            kind = ph["kind"]

            def cols_of(w, c0, n):
                tiles.append([(slot()[:, :, 0:n], rows(w[:, c0:c0 + n]))])

            if kind == "mod":
                for i in range(12):
                    cols_of(io["w_mod" if b == 0 else "ada_w_2"][l], 512 * i, 512)
            elif kind == "b1_in":
                for c0, n in ((0, 512), (512, 256), (768, 512), (1280, 512), (1792, 512)):
                    cols_of(io["w_in"][l], c0, n)
            elif kind == "b1_gates":
                for i in range(6):
                    cols_of(io["w_in"][l], 2304 + 512 * i, 512)
            elif kind == "merge":
                for i in range(2):
                    s = slot()
                    c = slice(512 * i, 512 * i + 512)
                    tiles.append([(s[:, 0:2, :], rows(io["w_pool_out"][l][:, c])),
                                  (s[:, 2:4, :], rows(io["w_sgu_out"][l][:, c])),
                                  (s[:, 4:8, :], rows(io["w_attn_out"][l][:, c]))])
            elif kind == "m_in":
                for i in range(6):
                    cols_of(io["mlstm_w_in_2"][0], 512 * i, 512)
                cols_of(io["mlstm_w_in_2"][0], 3072, 32)
            elif kind == "s_in":
                for i in range(2):
                    s, w = slot(), rows(io["swa_w_in_2"][0][:, 512 * i:512 * i + 512])
                    tiles.append([(s[:, :, P * j + HD * half:P * j + HD * half + HD],
                                   w[:, :, 256 * half + HD * j:256 * half + HD * j + HD])
                                  for half in range(2) for j in range(4)])
                cols_of(io["swa_w_in_2"][0], 1024, 512)
            elif kind == "ff1":
                for i in range(8):
                    cols_of(io["w_ff1" if b == 0 else "ffn_w1_2"][l], 512 * i, 512)
            elif ph["name"] == "ff2":
                w = io["w_ff2" if b == 0 else "ffn_w2_2"][l]
                for i in range(2):
                    for kb in range(4):
                        tiles.append([(slot(), rows(w[D * kb:D * kb + D, 512 * i:512 * i + 512]))])
            elif ph["name"] == "s_out":
                w = io["swa_w_out_2"][0].rearrange("(g s j d) n -> s d g j n", g=2, s=2, j=4, d=HD)
                for i in range(2):
                    s = slot()
                    tiles.append([(s[HD * half:HD * half + HD, 4 * g:4 * g + 4, :], w[half, :, g, :, 512 * i:512 * i + 512])
                                  for half in range(2) for g in range(2)])
            else:
                w = io["w_o"][l] if ph["name"] == "w_o" else io["mlstm_w_out_2"][0]
                for i in range(2):
                    cols_of(w, 512 * i, 512)
        landed = []
        total = [0] * SLOTS
        for t, parts in enumerate(tiles):
            total[t % SLOTS] += 16 * len(parts)
            landed.append(total[t % SLOTS])

        release, inner = [], 0
        for ph in plan:
            if not ph.get("tiles"):
                continue
            nt, u = ph.get("cols", 0) // P, ph["u"]
            ends = {"b1_in": (nt + 2, nt, 4, 4, 4), "b1_gates": (4,) * 6, "merge": (12, 12),
                    "m_in": (4, 4, 4, 4, 4, 4, 4), "s_in": (4, 4, 6), "ff1": (4,) * 8,
                    "mod": (0,) * 11 + (1,), "to_h": ((0,) * (ph.get("kb", 1) - 1) + (4,)) * 2}[ph["kind"]]
            for e in ends:
                u += e
                inner += not e
                release.append((s_unit, u) if e else (s_wused, inner))
            assert u == ph["u"] + ph["units"] and len(ends) == ph["tiles"]

        def wait_units(eng, n):
            for b in range(4):
                if (n - b + 3) // 4 > 0:
                    eng.wait_ge(s_free[b], (n - b + 3) // 4)

        def wait_unit(eng, u):
            eng.wait_ge(s_free[u % 4], u // 4 + 1)

        def segs(width):
            return [(0, slice(0, LAT))] + ([(1, slice(LAT, ALL))] if width == ALL else [])

        def rope_chunk(ph, c):
            if ph["block"] == 0:
                return (qT if c < 4 else kT)[:, c % 4, 0:LAT]
            return sq_[:, c, :] if c < 8 else sk[:, c - 8, 0:LAT]

        def head_parts(ph, i):
            kind, hh = ph["heads"][i]
            if ph["block"] == 0:
                base, ch = HD * (hh % 2), hh // 2
                if kind == "lat":
                    qs, ks, vs, nk = slice(0, LAT), slice(0, ALL), v_tm[:, 0:4, HD * hh:HD * hh + HD], ALL
                else:
                    qs, ks, vs, nk = slice(LAT, ALL), slice(LAT, ALL), v_tm[:, 2:4, HD * hh:HD * hh + HD], CTX
                q = qT[base:base + HD, ch, qs]
                return q, kT[base:base + HD, ch, ks], vs, base, nk, q
            kv = hh // 4
            base = HD * (kv % 2)
            q = sq_[base:base + HD, 4 * (hh // 8) + hh % 4, :]
            return q, sk[base:base + HD, kv // 2, :], sv[:, :, HD * kv:HD * kv + HD], base, ALL, q

        def nbias(ph, i):
            return 8 * ph["l"] + i

        rpb = io["na_rpb"]
        block = ctx.enter_context(nc.Block())

        @block.sync
        def _(sp):
            for dst, src in ((vec[:, :], io["vec"]), (ones[:, :], io["ones"]), (ones_h[:, :], io["ones_h"]),
                             (ident[:, :], io["ident"]), (rot[:, :, :], io["rot"]), (sel[:, :, :], io["sel"]),
                             (sgub[:, :, :], io["sgub"]), (gateb[:, :], io["gateb"]),
                             (sink[:, :], io["swa_sink_2"].partition_broadcast(P)),
                             (h[:, :, 0:LAT], io["xT"].rearrange("(k p) n -> p k n", p=P))):
                sp.dma_start(dst, src).then_inc(s_const, 16)
            for ph in plan:
                kind = ph["kind"]
                if kind == "load_ctx":
                    if ph["block"] == 1:
                        wait_units(sp, ph["u"])
                    sp.dma_start(h[:, :, LAT:ALL], io[f"ctxT{ph['block']}"].rearrange("(k p) n -> p k n", p=P)
                                 ).then_inc(s_ctxld, 16)
                elif kind == "aux":
                    if ph["layer"] > 0:
                        wait_units(sp, ph["u"])
                    if ph["block"] == 0:
                        l = ph["l"]
                        parts = ((A_POOL, 2048, io["pool_win"]), (A_SGU, 512, io["sgu_wT"][l]),
                                 (A_WP, 256, io["w_pool_bd"][l]), (A_ROPE, 512, io["rope1"]),
                                 (A_MASK, 512, io["na_mask"]))
                    elif ph["l"] == 0:
                        parts = ((A_MF, 2048, io["m_mask"]),)
                    else:
                        parts = ((A_ROPE, 512, io["rope2"]), (A_MASK, 512, io["swa_mask"]))
                    for off, n, src in parts:
                        sp.dma_start(aux[:, off:off + n], src).then_inc(s_aux, 16)
                for t in range(ph["t"], ph["t"] + ph["tiles"]):
                    if t >= SLOTS:
                        sp.wait_ge(*release[t - SLOTS])
                    for dst, src in tiles[t]:
                        sp.dma_start(dst, src).then_inc(s_slot[t % SLOTS], 16)
            sp.wait_ge(s_a, KC * plan[-1]["norm"])
            sp.dma_start(io["out"].rearrange("(k p) n -> p k n", p=P), h[:, :, 0:LAT]).then_inc(s_out, 16)
            sp.wait_ge(s_out, 16)

        AUX_LANDED = [80, 160, 176, 208]
        CONST = 160

        @block.tensor
        def _(pe):
            pe.wait_ge(s_const, CONST)

            def tile(t):
                pe.wait_ge(s_slot[t % SLOTS], landed[t])
                return ring[:, t % SLOTS, :, :]

            def bank(u):
                if u >= 4:
                    pe.wait_ge(s_free[u % 4], u // 4)
                return PS[:, u % 4, :]

            def fm(u, w, c, src, n, wait_input=None, m=P):
                out = bank(u)[0:m, 0:n]
                for k in range(KC):
                    if wait_input is not None:
                        pe.wait_ge(s_a, wait_input + k + 1)
                    mm = nc.tensor.matmul(out, w[:, k, c], src[:, k, 0:n], start=(k == 0), stop=(k == KC - 1))
                mm.then_inc(s_unit, 1)

            def tokm(u, w, c, tt, n, wait_input=None):
                out = bank(u)[:, 0:n]
                for k in range(KC):
                    if wait_input is not None:
                        pe.wait_ge(s_a, wait_input + k + 1)
                    mm = nc.tensor.matmul(out, a[:, k, P * tt:P * tt + P], w[:, k, c], start=(k == 0), stop=(k == KC - 1))
                mm.then_inc(s_unit, 1)
                return mm

            for ph in plan:
                kind, u, t = ph["kind"], ph["u"], ph["t"]
                cols = ph.get("cols")
                if kind == "mod":
                    pe.wait_ge(s_silu, ph["block"] + 1)
                    out = bank(u)
                    for i in range(12):
                        w = tile(t + i)
                        for c in range(4):
                            for k in range(KC):
                                mm = nc.tensor.matmul(out[:, 2 * (4 * i + c):2 * (4 * i + c) + 2],
                                                      w[:, k, P * c:P * c + P], silu[:, ph["block"], k, :],
                                                      start=(k == 0), stop=(k == KC - 1))
                        mm.then_inc(s_wused if i < 11 else s_unit, 1)
                elif kind == "norm":
                    i0 = KC * ph["norm"]
                    for k in range(KC):
                        pe.wait_ge(s_sq, i0 + k + 1)
                        nc.tensor.matmul(PS[:, 4, 0:ph["width"]], ones[:, :], sqb[:, k % 2, 0:ph["width"]],
                                         start=(k == 0), stop=(k == KC - 1)).then_inc(s_squsd, 1)
                elif kind == "b1_in":
                    nt = cols // P
                    need = KC * ph["norm"] - KC
                    w = tile(t)
                    for tt in range(nt):
                        tokm(u, w, slice(0, 256), tt, 256, need)
                        u += 1
                    for c in range(2):
                        fm(u, w, slice(256 + P * c, 384 + P * c), a, cols)
                        u += 1
                    w = tile(t + 1)
                    for tt in range(nt):
                        tokm(u, w, slice(0, 256), tt, 256)
                        u += 1
                    for j, n in ((2, cols), (3, ALL)):
                        w = tile(t + j)
                        for c in range(4):
                            fm(u, w, slice(P * c, P * c + P), a, n)
                            u += 1
                    w = tile(t + 4)
                    for tt in range(4):
                        tokm(u, w, slice(0, 512), tt, 512)
                        u += 1
                elif kind == "rope":
                    wait_units(pe, u)
                    for c in range(ph["chunks"]):
                        src = rope_chunk(ph, c)
                        nc.tensor.matmul(bank(u + c)[:, 0:LAT], rot[:, ph["block"], :], src,
                                         start=True, stop=True).then_inc(s_unit, 1)
                elif kind == "pool_sgu":
                    nseg = cols // LAT
                    pe.wait_ge(s_aux, AUX_LANDED[ph["layer"]])
                    win = aux[:, A_POOL:A_POOL + 2048].rearrange("p (k g n) -> p k g n", k=2, g=4)
                    for pair in range(2):
                        out = bank(u)
                        for s in range(nseg):
                            for half in range(2):
                                g = 2 * pair + half
                                for k in range(2):
                                    mm = nc.tensor.matmul(
                                        out[HD * half:HD * half + HD, LAT * s:LAT * s + LAT],
                                        p_tm[:, 2 * s + k, HD * g:HD * g + HD], win[:, k, g, :],
                                        start=(k == 0), stop=(k == 1))
                        mm.then_inc(s_unit, 1)
                        u += 1
                    wp = aux[:, A_WP:A_WP + 256].rearrange("p (c n) -> p c n", c=2)
                    for pair in range(2):
                        wait_unit(pe, u - 2)
                        nc.tensor.matmul(bank(u)[:, 0:cols], wp[:, pair, :], pooled[:, pair, 0:cols],
                                         start=True, stop=True).then_inc(s_unit, 1)
                        u += 1
                    pe.wait_ge(s_sgu, ph["layer"] + 1)
                    sw = aux[:, A_SGU:A_SGU + 512].rearrange("p (g n) -> p g n", g=4)
                    for pair in range(2):
                        out = bank(u)
                        for tt in range(cols // P):
                            for half in range(2):
                                g = 2 * pair + half
                                o = out[HD * half:HD * half + HD, P * tt:P * tt + P]
                                nc.tensor.matmul(o, vs_tm[:, tt, HD * g:HD * g + HD], sw[:, g, :],
                                                 start=True, stop=False)
                                mm = nc.tensor.matmul(o, sel[0:4, g, 0:HD], sgub[:, ph["l"], :],
                                                      start=False, stop=True)
                        mm.then_inc(s_unit, 1)
                        u += 1
                elif kind in ("b1_gates", "ff1"):
                    need = KC * ph["norm"] - KC if kind == "ff1" else None
                    for i in range(ph["tiles"]):
                        w = tile(t + i)
                        for c in range(4):
                            fm(u, w, slice(P * c, P * c + P), a, cols, need if i == 0 else None)
                            u += 1
                elif kind == "attn":
                    wait_units(pe, u)
                    n = len(ph["heads"])

                    def scores(i):
                        x = ph["head"] + i
                        if x >= 2:
                            pe.wait_ge(s_exp, x - 1)
                        q, k, _, _, nk, _ = head_parts(ph, i)
                        for qt in range(2):
                            mm = nc.tensor.matmul(PS[:, 2 * (x % 2) + qt, 0:nk], q[:, P * qt:P * qt + P], k,
                                                  start=True, stop=True)
                        mm.then_inc(s_sc, 1)

                    def turn_and_pv(i):
                        x = ph["head"] + i
                        _, _, v, out_base, nk, _ = head_parts(ph, i)
                        pe.wait_ge(s_prob, x + 1)
                        if x >= 1:
                            pe.wait_ge(s_pta, x)
                            pe.wait_ge(s_ptd, x)
                        for qt in range(2):
                            for k in range(nk // P):
                                mm = nc.tensor.transpose(PS[:, 4 + qt, P * k:P * k + P],
                                                         scr[:, x % 2, qt, P * k:P * k + P], ident[:, :])
                        mm.then_inc(s_tr, 1)
                        pe.wait_ge(s_pta, x + 1)
                        pe.wait_ge(s_ptd, x + 1)
                        if x >= 2:
                            pe.wait_ge(s_o, x - 1)
                        o = PS[out_base:out_base + HD, 6 + x % 2, 0:LAT]
                        for k in range(nk // P):
                            mm = nc.tensor.matmul(o, v[:, k, :], pt[:, x % 2, :, k, :],
                                                  start=(k == 0), stop=(k == nk // P - 1))
                        mm.then_inc(s_pv, 1)

                    scores(0)
                    for i in range(n):
                        if i + 1 < n:
                            scores(i + 1)
                        turn_and_pv(i)
                elif kind == "merge":
                    pe.wait_ge(s_o, ph["head"])
                    for i in range(2):
                        w = tile(t + i)
                        for c in range(4):
                            for src, k0, nk in ((poolT, 0, 2), (uT, 2, 2), (qT, 4, 4)):
                                out = bank(u)[:, 0:cols]
                                for k in range(nk):
                                    mm = nc.tensor.matmul(out, w[:, k0 + k, P * c:P * c + P], src[:, k, 0:cols],
                                                          start=(k == 0), stop=(k == nk - 1))
                                mm.then_inc(s_unit, 1)
                                u += 1
                elif kind == "to_h":
                    if ph["src"] == "attn":
                        pe.wait_ge(s_o, ph["head"])
                    elif ph["src"] == "hs":
                        pe.wait_ge(s_hs, MH)
                    elif ph["src"] == "y":
                        wait_units(pe, u)
                    src = dict(y=a, attn=sq_, hs=hs, ff=big)[ph["src"]]
                    ff0 = 32 * ph["layer"]
                    for i in range(2):
                        for kb in range(ph["kb"]):
                            w = tile(t)
                            for c in range(4):
                                out = (bank(u + c) if kb == 0 else PS[:, (u + c) % 4, :])[:, 0:cols]
                                for k in range(KC):
                                    if ph["src"] == "ff" and c == 0 and i == 0:
                                        pe.wait_ge(s_ff, ff0 + KC * kb + k + 1)
                                    mm = nc.tensor.matmul(out, w[:, k, P * c:P * c + P], src[:, KC * kb + k, 0:cols],
                                                          start=(kb == 0 and k == 0),
                                                          stop=(kb == ph["kb"] - 1 and k == KC - 1),
                                                          skip_group_check=True)
                                if kb == ph["kb"] - 1:
                                    mm.then_inc(s_unit, 1)
                                elif c == 3:
                                    mm.then_inc(s_wused, 1)
                            t += 1
                        u += 4
                elif kind == "m_in":
                    need = KC * ph["norm"] - KC
                    for i in range(2):
                        w = tile(t + i)
                        for c in range(4):
                            fm(u, w, slice(P * c, P * c + P), a, ALL, need if i == 0 else None)
                            u += 1
                    for i in range(2):
                        w = tile(t + 2 + i)
                        for tt in range(4):
                            tokm(u, w, slice(0, 512), tt, 512)
                            u += 1
                    for i in range(2):
                        w = tile(t + 4 + i)
                        for c in range(4):
                            fm(u, w, slice(P * c, P * c + P), a, ALL)
                            u += 1
                    w = tile(t + 6)
                    for j in range(4):
                        fm(u, w, slice(MH * j, MH * j + MH), a, ALL, m=MH)
                        u += 1
                elif kind == "m_gates":
                    pe.wait_ge(s_gr, 1)
                    out = bank(u).rearrange("p (w t g n) -> p w t g n", w=2, t=4, g=2, n=32)
                    for what in range(2):
                        for d in range(2):
                            src = G[:, 2 * d + 1, :] if what == 0 else Bc[:, d, :]
                            for tt in range(4):
                                mm = nc.tensor.transpose(out[:, what, tt, d, 0:MH], src[:, P * tt:P * tt + P],
                                                         ident[0:MH, 0:MH])
                    mm.then_inc(s_unit, 1)
                elif kind == "m_heads":
                    wait_units(pe, u)
                    pe.wait_ge(s_aux, AUX_LANDED[2])

                    def qk(b):
                        hh, qt = b // 4, b % 4
                        if qt == 0:
                            if b:
                                pe.wait_ge(s_D, b)
                            for d in range(2):
                                nc.tensor.matmul(PS[:, d, :], sel[:, hh, :], G[:, 2 * d, :], start=True, stop=True)
                        if b >= 2:
                            pe.wait_ge(s_W, b - 1)
                        c0 = 0 if qt < 2 else LAT
                        base = HD * (hh % 2)
                        nc.tensor.matmul(PS[:, 2 + b % 2, 0:ALL - c0],
                                         mq[base:base + HD, hh // 2, P * qt:P * qt + P],
                                         mk[base:base + HD, hh // 2, c0:ALL], start=True, stop=True).then_inc(s_qk, 1)

                    def pv(b):
                        hh, qt = b // 4, b % 4
                        k0 = 0 if qt < 2 else 2
                        pe.wait_ge(s_P, b + 1)
                        if b >= 2:
                            pe.wait_ge(s_mpt, b - 1)
                        for k in range(k0, 4):
                            mm = nc.tensor.transpose(PS[:, 4 + b % 2, P * (k - k0):P * (k - k0) + P],
                                                     scr[:, b % 2, 0, P * (k - k0):P * (k - k0) + P], ident[:, :])
                        mm.then_inc(s_mt, 1)
                        pe.wait_ge(s_mpt, b + 1)
                        if qt == 0 and hh >= 2:
                            pe.wait_ge(s_mo, hh - 1)
                        for k in range(k0, 4):
                            mm = nc.tensor.matmul(PS[:, 6 + hh % 2, P * qt:P * qt + P], mv[:, k, P * hh:P * hh + P],
                                                  pt[:, b % 2, 0, k - k0, :], start=(k == k0), stop=(k == 3))
                        mm.then_inc(s_mpv, 1)

                    n = 4 * MH
                    qk(0)
                    for b in range(n):
                        if b + 1 < n:
                            qk(b + 1)
                        pv(b)
                elif kind == "m_norm":
                    for hh in range(MH):
                        pe.wait_ge(s_msq, hh + 1)
                        nc.tensor.matmul(bank(u + hh), ones_h[:, :], a[:, hh, :], start=True, stop=True
                                         ).then_inc(s_unit, 1)
                elif kind == "s_in":
                    need = KC * ph["norm"] - KC
                    for i in range(2):
                        w = tile(t + i)
                        for j in range(4):
                            out = bank(u)[:, 0:LAT]
                            for k in range(KC):
                                if i == 0:
                                    pe.wait_ge(s_a, need + k + 1)
                                mm = nc.tensor.matmul(out, w[:, k, P * j:P * j + P], a[:, k, 0:LAT],
                                                      start=(k == 0), stop=(k == KC - 1))
                            mm.then_inc(s_unit, 1)
                            u += 1
                    w = tile(t + 2)
                    for c in range(2):
                        fm(u, w, slice(P * c, P * c + P), a, ALL)
                        u += 1
                    for tt in range(4):
                        tokm(u, w, slice(256, 512), tt, 256)
                        u += 1

        @block.scalar
        def _(act):
            act.wait_ge(s_const, CONST)
            steps = [0]

            def step(ins):
                steps[0] += 1
                ins.then_inc(s_act, 1)
                act.wait_ge(s_act, steps[0])

            def copy_unit(u, out, src_cols, func=ACT.Copy, m=P, **kw):
                act.wait_ge(s_unit, u + 1)
                nc.scalar.activation(out, PS[0:m, u % 4, src_cols], func, **kw).then_inc(s_free[u % 4], 1)

            for ph in plan:
                kind, u = ph["kind"], ph["u"]
                cols = ph.get("cols")
                if kind == "load_ctx":
                    c0 = V_COND + ph["block"] * 2 * KC
                    nc.scalar.activation(silu[:, ph["block"], :, :].rearrange("p k n -> p (k n)"),
                                         vec[:, c0:c0 + 2 * KC], ACT.Sigmoid).then_inc(s_silu_a, 1)
                elif kind == "norm":
                    n0 = ph["norm"]
                    act.wait_ge(s_var, n0 + 1)
                    nc.scalar.activation(rs[:, 0:ph["width"]], rs[:, 0:ph["width"]], ACT.Sqrt).then_inc(s_std, 1)
                    which, b = ph["which"], ph["block"]
                    for k in range(KC):
                        act.wait_ge(s_nrm, KC * n0 + k + 1)
                        if ph["final"]:
                            nc.scalar.activation(h[:, k, 0:LAT], nrm[:, k % 2, 0:LAT], ACT.Copy,
                                                 scale=vec[:, V_FIN + KC * b + k:V_FIN + KC * b + k + 1]
                                                 ).then_inc(s_a, 1)
                            continue
                        if which == 0 and k == 0:
                            act.wait_ge(s_gain, ph["layer"] + 1)
                        for s, c in segs(ph["width"]):
                            ins = nc.scalar.activation(a[:, k, c], nrm[:, k % 2, c], ACT.Identity,
                                                       scale=gain[:, which, k, s:s + 1],
                                                       bias=mod[:, 24 * which + k, s:s + 1])
                        ins.then_inc(s_a, 1)
                elif kind == "b1_in":
                    nt = cols // P
                    for tt in range(nt):
                        copy_unit(u, p_tm[:, tt, :], slice(0, 256))
                        u += 1
                    for c in range(2):
                        copy_unit(u, uT[:, c, 0:cols], slice(0, cols))
                        u += 1
                    for tt in range(nt):
                        if tt == 0:
                            act.wait_ge(s_squsd, KC * ph["norm"])
                        copy_unit(u, vs_tm[:, tt, :], slice(0, 256))
                        u += 1
                    ln0 = 0 if ph["l"] == 0 else 4
                    for tt in range(nt):
                        act.wait_ge(s_lnv, ln0 + tt + 1)
                        nc.scalar.activation(lnst[:, 4:5], lnst[:, 3:4], ACT.Sqrt).then_inc(s_lns, 1)
                    for c in range(4):
                        act.wait_ge(s_unit, u + 1)
                        nc.scalar.activation(
                            qT[:, c, 0:cols].rearrange("p (q n) -> p q n", n=P)[:, :, ::-1],
                            PS[:, u % 4, 0:cols].rearrange("p (q n) -> p q n", n=P), ACT.Copy, scale=QSCALE
                        ).then_inc(s_free[u % 4], 1)
                        u += 1
                elif kind == "b1_gates":
                    for i in range(24):
                        copy_unit(u + i, sig[:, i, 0:cols], slice(0, cols), ACT.Sigmoid)
                elif kind == "ff1":
                    for i in range(32):
                        copy_unit(u + i, big[:, i, 0:cols], slice(0, cols), ACT.Relu)
                elif kind == "attn":
                    n = len(ph["heads"])

                    def exps(i):
                        x = ph["head"] + i
                        nk = head_parts(ph, i)[4]
                        act.wait_ge(s_nm, x + 1)
                        if x >= 2:
                            act.wait_ge(s_tr, x - 1)
                        for qt in range(2):
                            if ph["block"] == 1:
                                hh = ph["heads"][i][1]
                                nc.scalar.activation(esink[:, x % 2, qt:qt + 1], sink[:, hh:hh + 1], ACT.Exp,
                                                     bias=nmax[:, x % 2, qt:qt + 1])
                            ins = nc.scalar.activation(scr[:, x % 2, qt, 0:nk], PS[:, 2 * (x % 2) + qt, 0:nk], ACT.Exp,
                                                       bias=nmax[:, x % 2, qt:qt + 1],
                                                       accum_out=rsum[:, x % 2, qt:qt + 1])
                        ins.then_inc(s_exp, 1)

                    def probs_t(i):
                        x = ph["head"] + i
                        nk = head_parts(ph, i)[4]
                        act.wait_ge(s_tr, x + 1)
                        if x >= 2:
                            act.wait_ge(s_pv, x - 1)
                        nc.scalar.activation(pt[:, x % 2, 0, 0:nk // P, :],
                                             PS[:, 4, 0:nk].rearrange("p (k n) -> p k n", n=P), ACT.Copy
                                             ).then_inc(s_pta, 1)

                    for i in range(n + 1):
                        if i < n:
                            exps(i)
                        if i >= 1:
                            probs_t(i - 1)
                elif kind == "m_in":
                    for c in range(8):
                        copy_unit(u + c, (mq if c < 4 else mk)[:, c % 4, :], slice(0, 512),
                                  scale=1.0 if c < 4 else QSCALE)
                    u += 16
                    for c in range(8):
                        copy_unit(u + c, sigo[:, c, :], slice(0, 512), ACT.Sigmoid)
                    u += 8
                    for j in range(4):
                        copy_unit(u + j, G[:, j, :], slice(0, 512), ACT.Identity, m=MH, bias=gateb[:, j:j + 1])
                elif kind == "m_gates":
                    wait_units(act, u)
                    for d in range(2):
                        step(nc.scalar.activation(Bc[:, d, :], G[:, 2 * d + 1, :], ACT.Abs))
                        step(nc.scalar.activation(Bc[:, d, :], Bc[:, d, :], ACT.Exp, scale=-1.0))
                        nc.scalar.activation(Bc[:, d, :], Bc[:, d, :], ACT.Ln, bias=1.0).then_inc(s_ga, 1)
                    act.wait_ge(s_gd, 1)
                    nc.scalar.activation(Bc[:, :, :], Bc[:, :, :], ACT.Exp, scale=-1.0).then_inc(s_gr, 1)
                elif kind == "m_heads":
                    def decay(b):
                        nk = ALL if b % 4 < 2 else CTX
                        act.wait_ge(s_D, b + 1)
                        nc.scalar.activation(scr[:, b % 2, :, 0:nk], scr[:, b % 2, :, 0:nk], ACT.Exp).then_inc(s_A, 1)

                    def turned(b):
                        nk = ALL if b % 4 < 2 else CTX
                        act.wait_ge(s_mt, b + 1)
                        if b >= 2:
                            act.wait_ge(s_mpv, b - 1)
                        nc.scalar.activation(pt[:, b % 2, 0, 0:nk // P, :],
                                             PS[:, 4 + b % 2, 0:nk].rearrange("p (k n) -> p k n", n=P), ACT.Copy
                                             ).then_inc(s_mpt, 1)

                    def head_out(hh):
                        act.wait_ge(s_mpv, 4 * hh + 4)
                        nc.scalar.activation(hs[:, hh, :], PS[:, 6 + hh % 2, :], ACT.Copy).then_inc(s_mo, 1)

                    n = 4 * MH
                    for b in range(n + 1):
                        if b < n:
                            decay(b)
                        if b >= 1:
                            turned(b - 1)
                            if b % 4 == 1 and b > 4:
                                head_out(b // 4 - 1)
                    head_out(MH - 1)
                elif kind == "m_norm":
                    wait_units(act, u + 8)
                    nc.scalar.activation(big[:, 0:8, :], big[:, 0:8, :], ACT.Sqrt).then_inc(s_mrs, 1)
                elif kind == "s_in":
                    for c in range(8):
                        copy_unit(u + c, sq_[:, c, :], slice(0, LAT), scale=QSCALE)

        @block.vector
        def _(dve):
            dve.wait_ge(s_const, CONST)
            steps = [0]

            def step(ins):
                steps[0] += 1
                ins.then_inc(s_dve, 1)
                dve.wait_ge(s_dve, steps[0])

            V = nc.vector
            lnc = [0]

            def copy_unit(u, out, src_cols):
                dve.wait_ge(s_unit, u + 1)
                V.tensor_copy(out, PS[:, u % 4, src_cols]).then_inc(s_free[u % 4], 1)

            for ph in plan:
                kind, u = ph["kind"], ph["u"]
                cols = ph.get("cols")
                if kind == "load_ctx":
                    c0 = V_COND + ph["block"] * 2 * KC
                    dve.wait_ge(s_silu_a, ph["block"] + 1)
                    s = silu[:, ph["block"], :, :].rearrange("p k n -> p (k n)")
                    V.tensor_tensor(s, s, vec[:, c0:c0 + 2 * KC], ALU.mult).then_inc(s_silu, 1)
                elif kind == "mod":
                    layer = ph["layer"]
                    dve.wait_ge(s_unit, u + 1)
                    b0 = V_BMOD + 48 * layer
                    bb = vec[:, b0:b0 + 48].unsqueeze(2).broadcast_to([P, 48, 2])
                    step(V.tensor_tensor(mod[:, :, :], PS[:, u % 4, 0:96].rearrange("p (c s) -> p c s", s=2), bb, ALU.add))
                    for which, vg in ((0, V_N1), (1, V_N2)):
                        g = vec[:, vg + KC * layer:vg + KC * layer + KC].unsqueeze(2).broadcast_to([P, KC, 2])
                        sc = mod[:, 24 * which + 8:24 * which + 16, :]
                        step(V.tensor_scalar(gain[:, which, :, :], sc, 1.0, None, ALU.add))
                        ins = V.tensor_tensor(gain[:, which, :, :], gain[:, which, :, :], g, ALU.mult)
                        if which == 0:
                            step(ins)
                    ins.then_inc(s_gain, 1)
                    dve.wait_ge(s_gain, layer + 1)
                    V.tensor_copy(lnst[:, 7:8], gain[:, 0, 0, 0:1]).then_inc(s_free[u % 4], 1)
                elif kind == "norm":
                    n0, w = ph["norm"], ph["width"]
                    dve.wait_ge(s_squsd, KC * n0 + KC)
                    V.tensor_scalar(rs[:, 0:w], PS[:, 4, 0:w], EPS, None, ALU.add).then_inc(s_var, 1)
                    dve.wait_ge(s_std, n0 + 1)
                    step(V.reciprocal(rs[:, 0:w], rs[:, 0:w]))
                    for k in range(KC):
                        i = KC * n0 + k
                        if i >= 2:
                            dve.wait_ge(s_a, i - 1)
                        V.tensor_tensor(nrm[:, k % 2, 0:w], h[:, k, 0:w], rs[:, 0:w], ALU.mult).then_inc(s_nrm, 1)
                elif kind == "b1_in":
                    nt = cols // P
                    u_vs = u + nt + 2
                    u_k = u_vs + nt + 4
                    for tt in range(nt):
                        wait_unit(dve, u_vs + tt)
                        x = vs_tm[:, tt, :]
                        step(V.reduce_sum(lnst[:, 0:1], x, AX_X))
                        step(V.tensor_scalar(lnst[:, 1:2], lnst[:, 0:1], 1.0 / 256, None, ALU.mult))
                        step(V.tensor_scalar(x, x, lnst[:, 1:2], None, ALU.subtract))
                        step(V.tensor_tensor_reduce(pt[:, 0, 0, 0:2, :].rearrange("p b n -> p (b n)"), x, x, 1.0, 0.0,
                                                    ALU.mult, ALU.add, lnst[:, 2:3]))
                        V.tensor_scalar(lnst[:, 3:4], lnst[:, 2:3], 1.0 / 256, EPS, ALU.mult, ALU.add
                                        ).then_inc(s_lnv, 1)
                        lnc[0] += 1
                        dve.wait_ge(s_lns, lnc[0])
                        step(V.reciprocal(lnst[:, 5:6], lnst[:, 4:5]))
                        ins = V.tensor_scalar(x, x, lnst[:, 5:6], None, ALU.mult)
                        if tt == nt - 1:
                            ins.then_inc(s_sgu, 1)
                    for c in range(4):
                        copy_unit(u_k + c, kT[:, c, :], slice(0, 512))
                    for tt in range(4):
                        copy_unit(u_k + 4 + tt, v_tm[:, tt, :], slice(0, 512))
                elif kind == "rope":
                    dve.wait_ge(s_aux, AUX_LANDED[ph["layer"]])
                    wait_units(dve, u)
                    cs = aux[:, A_ROPE:A_ROPE + 512].rearrange("p (s n) -> p s n", s=2)
                    for c in range(ph["chunks"]):
                        x = rope_chunk(ph, c)
                        dve.wait_ge(s_unit, u + c + 1)
                        tmp = bias[:, 0, :, 0:P]

                        def tiles_of(y):
                            return y.rearrange("p (q n) -> p q n", n=P)

                        cos, sin = tiles_of(cs[:, 0, :]), tiles_of(cs[:, 1, :])
                        if ph["block"] == 0 and c < 4:
                            cos, sin = cos[:, :, ::-1], sin[:, :, ::-1]
                        x = tiles_of(x)
                        V.tensor_tensor(tmp, tiles_of(PS[:, (u + c) % 4, 0:LAT]), sin, ALU.mult)
                        step(V.tensor_tensor(x, x, cos, ALU.mult))
                        V.tensor_tensor(x, x, tmp, ALU.add).then_inc(s_free[(u + c) % 4], 1)
                        dve.wait_ge(s_free[(u + c) % 4], (u + c) // 4 + 1)
                elif kind == "pool_sgu":
                    for pair in range(2):
                        copy_unit(u, pooled[:, pair, 0:cols], slice(0, cols))
                        u += 1
                    for pair in range(2):
                        dve.wait_ge(s_unit, u + 1)
                        c = V_PS + 2 * ph["l"] + pair
                        V.tensor_scalar(poolT[:, pair, 0:cols], PS[:, u % 4, 0:cols], vec[:, c:c + 1], None, ALU.mult
                                        ).then_inc(s_free[u % 4], 1)
                        u += 1
                    for pair in range(2):
                        dve.wait_ge(s_unit, u + 1)
                        V.tensor_tensor(uT[:, pair, 0:cols], PS[:, u % 4, 0:cols], uT[:, pair, 0:cols], ALU.mult
                                        ).then_inc(s_free[u % 4], 1)
                        u += 1
                elif kind == "attn":
                    n = len(ph["heads"])
                    if ph["block"] == 1:
                        dve.wait_ge(s_aux, AUX_LANDED[3])

                    def rowmax(i):
                        x = ph["head"] + i
                        what, hh = ph["heads"][i]
                        nk = head_parts(ph, i)[4]
                        S = PS[:, 2 * (x % 2):2 * (x % 2) + 2, :]
                        dve.wait_ge(s_sc, x + 1)
                        if what == "lat":
                            if ph["block"] == 0:
                                dve.wait_ge(s_bias, nbias(ph, i) + 1)
                                add = bias[:, hh % 2, :, :]
                            else:
                                add = aux[:, A_MASK:A_MASK + 512].rearrange("p (q n) -> p q n", q=2)
                            step(V.tensor_tensor(S[:, :, 0:LAT], S[:, :, 0:LAT], add, ALU.add))
                        m = nmax[:, x % 2, :]
                        step(V.tensor_reduce(m, S[:, :, 0:nk], AX_X, ALU.max))
                        if ph["block"] == 1:
                            step(V.tensor_scalar(m, m, sink[:, hh:hh + 1], None, ALU.max))
                        V.tensor_scalar(m, m, -1.0, None, ALU.mult).then_inc(s_nm, 1)

                    def inverse(i):
                        x = ph["head"] + i
                        dve.wait_ge(s_exp, x + 1)
                        if ph["block"] == 1:
                            step(V.tensor_tensor(rsum[:, x % 2, :], rsum[:, x % 2, :], esink[:, x % 2, :], ALU.add))
                        if x >= 2:
                            dve.wait_ge(s_prob, x - 1)
                        V.reciprocal(rinv[:, x % 2, :], rsum[:, x % 2, :]).then_inc(s_rinv, 1)

                    def probs_t(i):
                        x = ph["head"] + i
                        nk = head_parts(ph, i)[4]
                        dve.wait_ge(s_tr, x + 1)
                        if x >= 2:
                            dve.wait_ge(s_pv, x - 1)
                        V.tensor_copy(pt[:, x % 2, 1, 0:nk // P, :],
                                      PS[:, 5, 0:nk].rearrange("p (k n) -> p k n", n=P)).then_inc(s_ptd, 1)

                    def out(i):
                        x = ph["head"] + i
                        base, o = head_parts(ph, i)[3], head_parts(ph, i)[5]
                        dve.wait_ge(s_pv, x + 1)
                        src = PS[base:base + HD, 6 + x % 2, 0:LAT].rearrange("p (q n) -> p q n", q=2)
                        if ph["block"] == 0:
                            src = src[:, :, ::-1]
                        V.tensor_copy(o.rearrange("p (q n) -> p q n", q=2), src).then_inc(s_o, 1)

                    rowmax(0)
                    for i in range(n + 1):
                        if i < n:
                            inverse(i)
                            if i + 1 < n:
                                rowmax(i + 1)
                            probs_t(i)
                        if i >= 1:
                            out(i - 1)
                elif kind == "merge":
                    for c in range(KC):
                        for br in range(3):
                            dve.wait_ge(s_unit, u + 1)
                            g = sig[:, KC * br + c, 0:cols]
                            ps = PS[:, u % 4, 0:cols]
                            if br == 0:
                                ins = V.tensor_tensor(a[:, c, 0:cols], ps, g, ALU.mult)
                            else:
                                step(V.tensor_tensor(g, ps, g, ALU.mult))
                                ins = V.tensor_tensor(a[:, c, 0:cols], a[:, c, 0:cols], g, ALU.add)
                            ins.then_inc(s_free[u % 4], 1)
                            wait_unit(dve, u)
                            u += 1
                elif kind == "to_h":
                    for c in range(KC):
                        dve.wait_ge(s_unit, u + 1)
                        for s, cc in segs(cols):
                            ins = V.scalar_tensor_tensor(out=h[:, c, cc], in0=PS[:, u % 4, cc],
                                                         scalar=mod[:, 8 * ph["gate"] + c, s:s + 1],
                                                         in1=h[:, c, cc], op0=ALU.mult, op1=ALU.add)
                        ins.then_inc(s_free[u % 4], 1)
                        u += 1
                elif kind == "m_in":
                    u += 8
                    for i in range(8):
                        copy_unit(u + i, mv[:, i % 4, 512 * (i // 4):512 * (i // 4) + 512], slice(0, 512))
                elif kind == "m_gates":
                    wait_units(dve, u)
                    step(V.memset(one_row, 1.0))
                    for d in range(2):
                        li, lf, B = G[:, 2 * d, :], G[:, 2 * d + 1, :], Bc[:, d, :]
                        dve.wait_ge(s_ga, d + 1)
                        step(V.tensor_scalar(lf, lf, 0.0, None, ALU.min))
                        step(V.tensor_tensor(lf, lf, B, ALU.subtract))
                        if d == 0:
                            parts = (slice(LAT, ALL), slice(0, LAT))
                            last = (slice(ALL - 1, ALL), None)
                        else:
                            parts = (slice(ALL - 1, LAT - 1, -1), slice(LAT - 1, None, -1))
                            last = (slice(LAT, LAT + 1), None)
                        ini = 0.0
                        for pr, la in zip(parts, last):
                            step(V.tensor_tensor_scan(B[:, pr], one_row[:, pr], lf[:, pr], ini, ALU.mult, ALU.add))
                            ini = None if la is None else B[:, la]
                        step(V.tensor_tensor(li, li, B, ALU.subtract))
                        M = lf
                        ini = 0.0
                        for pr, la in zip(parts, last):
                            step(V.tensor_tensor_scan(M[:, pr], li[:, pr], li[:, pr], ini, ALU.max, ALU.max))
                            ini = None if la is None else M[:, la]
                        ins = V.tensor_tensor(B, B, M, ALU.add)
                        if d == 1:
                            ins.then_inc(s_gd, 1)
                        else:
                            step(ins)
                    dve.wait_ge(s_unit, u + 1)
                    src = PS[:, u % 4, :].rearrange("p (w t g n) -> p w t g n", w=2, t=4, g=2, n=32)
                    for what in range(2):
                        for d in range(2):
                            ins = V.tensor_scalar(tm[:, what, :, :, d], src[:, what, :, d, 0:MH],
                                                  -1.0 if what == 0 else 1.0, None, ALU.mult)
                            if not (what and d):
                                step(ins)
                    ins.then_inc(s_free[u % 4], 1)
                elif kind == "m_heads":
                    dve.wait_ge(s_aux, AUX_LANDED[2])
                    mask = aux[:, A_MF:A_MF + 2048].rearrange("p (d q n) -> p d q n", d=2, q=2)
                    wait_units(dve, u)

                    def args(b):
                        hh, qt = b // 4, b % 4
                        c0 = 0 if qt < 2 else LAT
                        nk = ALL - c0
                        dve.wait_ge(s_qk, b + 1)
                        if b >= 2:
                            dve.wait_ge(s_mt, b - 1)
                        for d in range(2):
                            ins = V.scalar_tensor_tensor(out=scr[:, b % 2, d, 0:nk], in0=PS[:, d, c0:ALL],
                                                         scalar=tm[:, 0, qt, hh, d:d + 1],
                                                         in1=mask[:, d, qt % 2, 0:nk], op0=ALU.add, op1=ALU.min)
                        ins.then_inc(s_D, 1)

                    def weigh(b):
                        hh, qt = b // 4, b % 4
                        nk = ALL if qt < 2 else CTX
                        dve.wait_ge(s_A, b + 1)
                        dn = den[:, b % 2, 0, :]
                        rc = den[:, b % 2, 1, :]
                        for d in range(2):
                            x = scr[:, b % 2, d, 0:nk]
                            ins = V.tensor_tensor_reduce(x, x, PS[:, 2 + b % 2, 0:nk], 1.0, 0.0, ALU.mult, ALU.add,
                                                         dn[:, d:d + 1])
                        ins.then_inc(s_W, 1)
                        dve.wait_ge(s_W, b + 1)
                        step(V.scalar_tensor_tensor(out=rc, in0=dn, scalar=-1.0, in1=dn, op0=ALU.mult, op1=ALU.max))
                        step(V.tensor_tensor(rc, rc, tm[:, 1, qt, hh, :], ALU.max))
                        step(V.reciprocal(rc, rc))
                        x0, x1 = scr[:, b % 2, 0, 0:nk], scr[:, b % 2, 1, 0:nk]
                        step(V.tensor_scalar(x0, x0, rc[:, 0:1], None, ALU.mult))
                        V.scalar_tensor_tensor(out=x0, in0=x1, scalar=rc[:, 1:2], in1=x0, op0=ALU.mult, op1=ALU.add
                                               ).then_inc(s_P, 1)

                    n = 4 * MH
                    args(0)
                    for b in range(n):
                        if b + 1 < n:
                            args(b + 1)
                        weigh(b)
                elif kind == "m_norm":
                    rb = big[:, 0:8, :]
                    for hh in range(MH):
                        dve.wait_ge(s_unit, u + hh + 1)
                        V.tensor_scalar(rb[:, hh, :], PS[:, (u + hh) % 4, :], EPS, None, ALU.add
                                        ).then_inc(s_free[(u + hh) % 4], 1)
                    dve.wait_ge(s_mrs, 1)
                    step(V.reciprocal(rb, rb))
                    for hh in range(MH):
                        V.scalar_tensor_tensor(out=hs[:, hh, :], in0=hs[:, hh, :],
                                               scalar=vec[:, V_HN + hh:V_HN + hh + 1], in1=rb[:, hh, :],
                                               op0=ALU.mult, op1=ALU.mult).then_inc(s_hn, 1)
                elif kind == "s_in":
                    u += 8
                    for c in range(2):
                        copy_unit(u + c, sk[:, c, :], slice(0, 512))
                    for tt in range(4):
                        copy_unit(u + 2 + tt, sv[:, tt, :], slice(0, 256))

        @block.gpsimd
        def _(pool):
            pool.wait_ge(s_const, CONST)
            steps = [0]
            nb = [0]
            for ph in plan:
                kind, u = ph["kind"], ph["u"]
                cols = ph.get("cols")
                if kind == "norm":
                    if ph["which"] == 0:
                        pool.wait_ge(s_ctxld, 16 * (ph["block"] + 1))
                    wait_units(pool, u)
                    for k in range(KC):
                        i = KC * ph["norm"] + k
                        if i >= 2:
                            pool.wait_ge(s_squsd, i - 1)
                        w = ph["width"]
                        nc.gpsimd.tensor_tensor(sqb[:, k % 2, 0:w], h[:, k, 0:w], h[:, k, 0:w], ALU.mult
                                                ).then_inc(s_sq, 1)
                elif kind == "ff1":
                    for i in range(32):
                        wait_unit(pool, u + i)
                        x = big[:, i, 0:cols]
                        nc.gpsimd.tensor_tensor(x, x, x, ALU.mult).then_inc(s_ff, 1)
                elif kind == "attn":
                    n = len(ph["heads"])

                    def load_bias(i):
                        hh = ph["heads"][i][1]
                        x = ph["head"] + i
                        if i >= 2:
                            pool.wait_ge(s_nm, x - 1)
                        for r in range(4):
                            off = (8 * ph["l"] + hh) * RPB_H * RPB_W + (7 - r) * RPB_W + 15 - (GRID - 1)
                            src = bass.AP(rpb.tensor, rpb.offset + off, [[1, GRID], [RPB_W, 4], [1, GRID]])
                            dst = bias[GRID * (1 - r % 2):GRID * (1 - r % 2) + GRID, hh % 2, r // 2, :]
                            pool.dma_start(dst.rearrange("p (i c) -> p i c", i=4), src).then_inc(s_biasld, 16)
                            nb[0] += 16

                    def mask_bias(i):
                        hh = ph["heads"][i][1]
                        pool.wait_ge(s_biasld, nb[0])
                        b = bias[:, hh % 2, :, :]
                        nc.gpsimd.tensor_tensor(b, b, aux[:, A_MASK:A_MASK + 512].rearrange("p (q n) -> p q n", q=2),
                                                ALU.add).then_inc(s_bias, 1)

                    lat = n if ph["block"] else 8
                    if ph["block"] == 0:
                        pool.wait_ge(s_aux, AUX_LANDED[ph["layer"]])
                        wait_units(pool, u)
                        load_bias(0)
                        mask_bias(0)
                        load_bias(1)
                        mask_bias(1)
                    for i in range(n):
                        x = ph["head"] + i
                        nk = head_parts(ph, i)[4]
                        pool.wait_ge(s_rinv, x + 1)
                        for qt in range(2):
                            p_ = scr[:, x % 2, qt, 0:nk]
                            ins = nc.gpsimd.tensor_scalar(p_, p_, rinv[:, x % 2, qt:qt + 1], None, ALU.mult)
                        ins.then_inc(s_prob, 1)
                        if ph["block"] == 0 and i + 2 < 8:
                            load_bias(i + 2)
                            mask_bias(i + 2)
                elif kind == "m_norm":
                    for hh in range(MH):
                        pool.wait_ge(s_mo, hh + 1)
                        nc.gpsimd.tensor_tensor(a[:, hh, :], hs[:, hh, :], hs[:, hh, :], ALU.mult).then_inc(s_msq, 1)
                    for hh in range(MH):
                        pool.wait_ge(s_hn, hh + 1)
                        nc.gpsimd.tensor_tensor(hs[:, hh, :], hs[:, hh, :], sigo[:, hh, :], ALU.mult
                                                ).then_inc(s_hs, 1)


_SHAPES = None


def shape_constants():
    c = {}
    c["ones"] = np.full((P, P), 1.0 / D, np.float32)
    c["ones_h"] = np.full((P, P), 1.0 / MDV, np.float32)
    c["ident"] = np.eye(P, dtype=np.float32)
    rot = np.zeros((P, 2, P), np.float32)
    for base in (0, HD):
        for j in range(HD // 2):
            lo, hi = base + 2 * j, base + 2 * j + 1
            rot[hi, 0, lo] = -1.0
            rot[lo, 0, hi] = 1.0
            lo, hi = base + j, base + j + HD // 2
            rot[hi, 1, lo] = -1.0
            rot[lo, 1, hi] = 1.0
    c["rot"] = rot
    sel = np.zeros((MH, MH, P), np.float32)
    for i in range(MH):
        sel[i, i] = 1.0
    c["sel"] = sel
    t = np.arange(LAT)
    nf = HD // 4
    inv = np.float32(10000.0) ** (-np.arange(nf, dtype=np.float32) / np.float32(nf))
    row, col = (t // GRID).astype(np.float32), (t % GRID).astype(np.float32)
    ang = np.concatenate([row[:, None] * inv, col[:, None] * inv], axis=-1)
    cs = np.stack([np.cos(ang), np.sin(ang)]).astype(np.float32).transpose(2, 0, 1)
    c["rope1"] = np.tile(np.repeat(cs, 2, axis=0), (2, 1, 1)).reshape(P, 512)
    c["rope2"] = np.tile(cs, (4, 1, 1)).reshape(P, 512)
    start = np.clip(col - 8, 0, GRID - 16)
    ok = (col[None, :] >= start[:, None]) & (col[None, :] < start[:, None] + 16)

    def tiled(m):
        return np.ascontiguousarray(m.astype(np.float32).reshape(2, P, -1).transpose(1, 0, 2)).reshape(P, -1)

    c["na_mask"] = np.ascontiguousarray(tiled(np.where(ok, 0.0, NEG))[::-1])
    c["swa_mask"] = tiled(np.where(np.abs(t[:, None] - t[None, :]) <= 128, 0.0, NEG))
    fwd = np.concatenate([np.where(t[None, :] <= t[:, None], 0.0, NEG), np.zeros((LAT, CTX))], axis=1)
    bwd = np.concatenate([np.where(t[None, :] >= t[:, None], 0.0, NEG), np.zeros((LAT, CTX))], axis=1)
    c["m_mask"] = np.concatenate([tiled(fwd), tiled(bwd)], axis=1)
    win = np.zeros((4, LAT, LAT), np.float32)
    for g, w in enumerate((2, 4, 8, 16)):
        lo, hi = np.clip(t - w // 2, 0, LAT), np.clip(t + w - w // 2, 0, LAT)
        inside = (t[:, None] >= lo[None, :]) & (t[:, None] < hi[None, :])
        win[g] = np.where(inside, 1.0 / (hi - lo)[None, :].astype(np.float32), 0.0) - np.eye(LAT)
    c["pool_win"] = np.ascontiguousarray(win.reshape(4, 2, P, LAT).transpose(2, 1, 0, 3)).reshape(P, 2048)
    return c


def lay_out(inp):
    f = {k: np.asarray(v) for k, v in inp.items()}

    def colv(x):
        return x.reshape(-1, P).T

    parts = []
    for cc, cx in (("c", "c_ctx"), ("c_2", "c_ctx_2")):
        parts.append(np.stack([colv(f[cc].reshape(-1)), colv(f[cx].reshape(-1))], axis=2).reshape(P, -1))
    for name in ("b_mod", "ada_b_2", "norm1_g", "norm_mix_2", "norm2_g", "norm_ffn_2", "final_g", "final_norm_2",
                 "pool_scale", "mlstm_head_norm_2"):
        parts.append(colv(f[name].reshape(-1)))
    out = {"vec": np.concatenate(parts, axis=1)}
    out["xT"] = f["x"][0].T
    out["ctxT0"] = f["ctx"][0].T
    out["ctxT1"] = f["ctx_2"][0].T
    out["sgu_wT"] = f["sgu_w"].transpose(0, 3, 1, 2).reshape(2, P, 512)
    out["sgub"] = f["sgu_b"].transpose(1, 0, 2)
    out["gateb"] = f["mlstm_gate_b_2"][0].T
    bd = np.zeros((2, P, 2, P), np.float32)
    for g in range(4):
        o = HD * (g % 2)
        bd[:, o:o + HD, g // 2, o:o + HD] = f["w_pool"][:, g]
    out["w_pool_bd"] = bd.reshape(2, P, 256)
    for name in ("w_mod", "ada_w_2", "w_in", "w_pool_out", "w_sgu_out", "w_attn_out", "w_o", "w_ff1", "w_ff2",
                 "ffn_w1_2", "ffn_w2_2", "mlstm_w_in_2", "mlstm_w_out_2", "swa_w_in_2", "swa_w_out_2", "na_rpb"):
        out[name] = f[name]
    out["swa_sink_2"] = f["swa_sink_2"].reshape(-1)
    return out


def kernel(**inputs):
    import concourse.bacc as bacc
    from concourse.bass_utils import run_bass_kernel_spmd

    arrays = lay_out(inputs)
    arrays.update(shape_constants())
    nc = bacc.Bacc("TRN2", target_bir_lowering=False, num_devices=1)
    io, sent = {}, {}
    for name, x in arrays.items():
        x = np.ascontiguousarray(x)
        sent[f"in_{name}"] = x
        io[name] = nc.dram_tensor(f"in_{name}", x.shape, F32, kind="ExternalInput").ap()
    io["out"] = nc.dram_tensor("outT", (D, LAT), F32, kind="ExternalOutput").ap()
    build(nc, io)
    r = run_bass_kernel_spmd(nc, [sent], core_ids=[0])
    return np.ascontiguousarray(r.results[0]["outT"].T).reshape(1, LAT, D)
```

```python
from contextlib import ExitStack

import numpy as np
import concourse.bass as bass
from concourse import mybir

F32 = mybir.dt.float32
F32R = mybir.dt.float32r
ALU = mybir.AluOpType
ACT = mybir.ActivationFunctionType
AX_X = mybir.AxisListType.X

P = 128
D = 1024
KC = D // P
LAT = 256
CTX = 256
ALL = LAT + CTX
DFF = 4 * D
EPS = 1e-6
NEG = -1e30
GRID = 64
HD = 64
QSCALE = HD ** -0.5
RPB_H, RPB_W = 15, 31
SLOTS = 3
TILE = 2048
MH = 8
MDV = D // MH

V_COND = 0
V_BMOD = V_COND + 2 * KC * 2
V_N1 = V_BMOD + 4 * 48
V_N2 = V_N1 + 4 * KC
V_FIN = V_N2 + 4 * KC
V_PS = V_FIN + 2 * KC
V_HN = V_PS + 4
V_END = V_HN + MH

A_SGU, A_WP = 0, 512
A_ROPE, A_MASK = 768, 1280
A_MF = 0
A_SIZE = 2048


def make_plan():
    phases = []
    hunits = []
    n = dict(s=0, u=0, x=0, norm=0, head=0, mu=0, final=0, y=0)

    def phase(kind, tiles=(), units=0, mods=(), per=1, every=1, splits=0, **kw):
        ph = dict(kind=kind, norm=n["norm"], head=n["head"], x=n["x"], y=n["y"], u=n["u"], **kw)
        mods = list(mods)
        steps = []
        for i, e in enumerate(tiles):
            st = dict(s=n["s"] if e is not None else None, u=n["u"], units=e or 0, mods=[], modu=None)
            n["s"] += e is not None
            n["u"] += e or 0
            if i % every == 0:
                st["mods"], mods = mods[:per], mods[per:]
                if any(half for _, _, half in st["mods"]):
                    st["modu"] = n["u"]
                    n["u"] += 1
            steps.append(st)
        assert not mods
        n["u"] += units
        n["x"] += splits
        ph.update(steps=steps, end=n["u"])
        if kind == "to_h":
            hunits[:] = [st["u"] + c for st in steps for c in range(st["units"])]
        if kind == "norm":
            ph["hunits"] = list(hunits)
        phases.append(ph)
        return ph

    def blocks(layer, first, last):
        return [(layer, b, half) for b in range(first, last) for half in range(2)]

    phase("mod0", tiles=(None,) * 4, mods=blocks(0, 0, 4), per=2, layer=0, cols=ALL)
    for layer in range(4):
        block, l = layer // 2, layer % 2
        cols = ALL if l == 0 else LAT
        nt = cols // P
        base = dict(layer=layer, block=block, l=l, cols=cols)
        if l == 0:
            phase("load_ctx", **base)
        phase("aux", **base)
        phase("norm", final=False, which=0, width=ALL, splits=KC, **base)
        n["norm"] += 1
        if block == 0:
            phase("b1_in", tiles=(nt, 2, nt, 2, 2, 2, 2, 4, 4), **base)
            phase("rope", units=8, chunks=8, **base)
            phase("pool_sgu", units=6, **base)
            heads = [("lat", h) for h in range(8)] + ([("ctx", h) for h in range(8)] if l == 0 else [])
            phase("attn", heads=heads, **base)
            n["head"] += len(heads)
            phase("merge", tiles=(6, 2, 2, 2) * 4, mods=blocks(layer, 4, 12), splits=KC, **base)
            n["y"] += 24
            phase("to_h", tiles=(2,) * 4, src="y", gate=2, name="w_o", **base)
        elif l == 0:
            phase("m_in", tiles=(2, 2, 2, 2) + (4,) * 4 + (2,) * 4 + (4,), mods=blocks(layer, 4, 10), **base)
            phase("m_gates", units=1, **base)
            phase("m_heads", **base)
            phase("m_norm", units=8, splits=KC, **base)
            phase("to_h", tiles=(2,) * 4, mods=blocks(layer, 10, 12), src="a", gate=2, name="m_out", **base)
        else:
            phase("s_in", tiles=(2,) * 5 + (4,), mods=blocks(layer, 4, 10), per=2, **base)
            phase("rope", units=10, chunks=10, **base)
            heads = [("lat", h) for h in range(16)]
            phase("attn", heads=heads, **base)
            n["head"] += len(heads)
            phase("to_h", tiles=(2,) * 4, mods=blocks(layer, 10, 12), src="attn", gate=2, name="s_out", **base)
        phase("norm", final=False, which=1, width=cols, splits=KC, **base)
        n["norm"] += 1
        phase("ff1", tiles=(2,) * 16, mods=blocks(layer + 1, 0, 4) if layer < 3 else (), every=2, **base)
        phase("to_h", tiles=((0,) * 7 + (4,)) * 2, splits=16, src="ff", gate=5, name="ff2", **base)
        if l == 1:
            phase("norm", final=True, which=2, width=LAT, **base)
            n["norm"] += 1
    return phases


def build(nc, io):
    plan = make_plan()
    ctx = ExitStack()
    with ctx:
        def sb(name, shape, dtype=F32):
            return ctx.enter_context(nc.sbuf_tensor(name, shape, dtype))

        def sem(name):
            return ctx.enter_context(nc.semaphore(name))

        ring = sb("ring", [P, SLOTS, TILE])
        w_h = sb("w_h", [P, 2, TILE], F32R)
        w_l = sb("w_l", [P, 2, TILE], F32R)
        h = sb("h", [P, KC, ALL])
        with nc.sbuf_tensor("hid", [P, 32, 512], F32) as hid:
            pass
        m_h = sb("m_h", [P, KC, 512], F32R)
        m_l = sb("m_l", [P, KC, 512], F32R)
        big = sb("big", [P, 16, 512])
        with nc.sbuf_tensor("af", [P, 16, 512], F32) as af:
            pass
        a_h = sb("a_h", [P, KC, 512], F32R)
        a_l = sb("a_l", [P, KC, 512], F32R)
        bias = sb("bias", [P, 2, 512])
        scr = sb("scr", [P, 2, 2, 512])
        pt = sb("pt", [P, 2, 2, 4, P])
        aux = sb("aux", [P, A_SIZE])
        rot = sb("rot", [P, 2, P])
        ident = sb("ident", [P, P])
        ones = sb("ones", [P, P])
        unit = sb("unit", [P, 2])
        vec = sb("vec", [P, V_END])
        silu = sb("silu", [P, 2, KC, 2])
        mod = sb("mod", [P, 2, 48, 2])
        gain = sb("gain", [P, 2, KC, 2])
        sgub = sb("sgub", [4, 2, P])
        gateb = sb("gateb", [MH, 4])
        sink = sb("sink", [P, 16])
        nmax = sb("nmax", [P, 2, 2])
        rsum = sb("rsum", [P, 2, 2])
        esink = sb("esink", [P, 2, 2])
        rinv = sb("rinv", [P, 2, 2])
        lnst = sb("lnst", [P, 8])
        tm = sb("tm", [P, 2, 4, MH, 2])
        den = sb("den", [P, 2, 2, 2])
        acc = bias
        PS = ctx.enter_context(nc.psum_tensor("PS", [P, 8, 512], F32))

        qT = big[:, 0:4, :]
        kT = big[:, 4:8, :]
        v_tm = big[:, 8:12, :]
        uT = big[:, 12:14, :]
        p_tm = big[:, 14:16, :].rearrange("p a n -> p (a n)").rearrange("p (t n) -> p t n", t=4)
        yT = big[:, 0:8, :]
        br = big[:, 8:14, :]
        gate = big[:, 14:16, :]
        win = hid[:, 4:8, :].rearrange("p a n -> p (a n)").rearrange("p (k g n) -> p k g n", k=2, g=4)
        vs_tm = scr[:, 0, :, :].rearrange("p a n -> p (a n)").rearrange("p (t n) -> p t n", t=4)
        pooled = pt[:, 0, :, :, :].rearrange("p a b n -> p (a b n)").rearrange("p (c n) -> p c n", c=2)
        mq = big[:, 0:4, :]
        mk = big[:, 4:8, :]
        mv = big[:, 8:16, :].rearrange("p a n -> p (a n)").rearrange("p (t n) -> p t n", t=4)
        sigo = hid[:, 0:8, :]
        hs = hid[:, 8:16, :]
        G = af[0:MH, 0:4, :]
        Bc = af[0:MH, 4:6, :]
        one_row = af[0:MH, 6, :]
        msq = af[:, 8:16, :]
        sq_ = big[:, 0:8, 0:LAT]
        sk = big[:, 8:10, :]
        sv = big[:, 10:12, :].rearrange("p a n -> p (a n)").rearrange("p (t n) -> p t n", t=4)
        sqb = scr[:, 0, :, :]
        ssum = pt[:, 0, 0, :, :].rearrange("p b n -> p (b n)")
        nrm = scr[:, 1, :, :]
        rs = pt[:, 1, 0, :, :].rearrange("p b n -> p (b n)")

        s_const = sem("const_loaded")
        s_slot = [sem(f"weights_loaded_{i}") for i in range(SLOTS)]
        s_inner = sem("tile_done_inside_unit")
        s_wh = sem("weights_rounded")
        s_wl = sem("weights_split")
        s_xh = sem("input_rounded")
        s_xl = sem("input_split")
        s_mtile = sem("mod_tile_used")
        s_fin = sem("final_norm_written")
        s_ctxld = sem("context_loaded")
        s_aux = sem("tables_loaded")
        s_unit = sem("unit_done")
        s_free = [sem(f"bank_evacuated_{i}") for i in range(4)]
        s_silu = sem("silu_ready")
        s_silu_a = sem("silu_sigmoid")
        s_sq = sem("square_sum_ready")
        s_sqm = sem("mean_square_done")
        s_var = sem("variance_ready")
        s_std = sem("std_ready")
        s_nrm = sem("normed_ready")
        s_dve = sem("dve_step")
        s_act = sem("act_step")
        s_pool = sem("pool_step")
        s_ff = sem("hidden_ready")
        s_bias = sem("bias_ready")
        s_biasld = sem("bias_loaded")
        s_sc = sem("scores_done")
        s_nm = sem("max_ready")
        s_exp = sem("exp_done")
        s_prob = sem("probs_ready")
        s_tr = sem("transposed")
        s_pta = sem("probsT_by_act")
        s_ptd = sem("probsT_by_dve")
        s_pv = sem("pv_done")
        s_o = sem("attn_out_ready")
        s_y = sem("gated_branch_added")
        s_sgu = sem("sgu_normed")
        s_lnv = sem("ln_var")
        s_lns = sem("ln_std")
        s_ga = sem("gate_exp")
        s_gd = sem("gate_rows_ready")
        s_gr = sem("guard_ready")
        s_qk = sem("m_qk_done")
        s_D = sem("m_decay_args")
        s_A = sem("m_decay_ready")
        s_W = sem("m_weighted")
        s_P = sem("m_probs_ready")
        s_mt = sem("m_transposed")
        s_mpt = sem("m_probsT_ready")
        s_mpv = sem("m_pv_done")
        s_mo = sem("m_out_ready")
        s_msq = sem("m_squares")
        s_mrs = sem("m_var_sqrt")
        s_hn = sem("m_normed")
        s_hs = sem("m_gated")
        s_out = sem("out_stored")

        def rows(w):
            return w.rearrange("(k p) n -> p k n", p=P)

        split_src = []

        def view8(t):
            return t.rearrange("p (k n) -> p k n", k=8)

        def view4(t):
            return t.rearrange("p (k n) -> p k n", k=4)

        def whole(w, c0):
            split_src.append([(lambda t: view8(t), rows(w[:, c0:c0 + 256]))])

        for ph in plan:
            if not ph["steps"] or ph["kind"] == "mod0":
                continue
            l, b, kind = ph["l"], ph["block"], ph["kind"]
            if kind == "b1_in":
                for i in range(9):
                    whole(io["w_in"][l], 256 * i)
            elif kind == "merge":
                for i in range(4):
                    c = slice(256 * i, 256 * i + 256)
                    split_src.append([(lambda t: view8(t)[:, 0:2, :], rows(io["w_pool_out"][l][:, c])),
                                      (lambda t: view8(t)[:, 2:4, :], rows(io["w_sgu_out"][l][:, c])),
                                      (lambda t: view8(t)[:, 4:8, :], rows(io["w_attn_out"][l][:, c]))])
                    for g in range(3):
                        whole(io["w_in"][l], 2304 + D * g + 256 * i)
            elif kind == "m_in":
                for i in range(12):
                    whole(io["mlstm_w_in_2"][0], 256 * i)
                split_src.append([(lambda t, r=r: view8(t)[:, :, 32 * r:32 * r + 32],
                                   rows(io["mlstm_w_in_2"][0][:, 3072:3104])) for r in range(8)])
            elif kind == "s_in":
                w = io["swa_w_in_2"][0]
                for i in range(2):
                    for jj in range(2):
                        split_src.append([
                            (lambda t, d=P * j + HD * half: view8(t)[:, :, d:d + HD],
                             rows(w[:, 512 * i + 256 * half + HD * (2 * jj + j):
                                    512 * i + 256 * half + HD * (2 * jj + j) + HD]))
                            for half in range(2) for j in range(2)])
                for i in range(2):
                    whole(w, 1024 + 256 * i)
            elif kind == "ff1":
                for i in range(16):
                    whole(io["w_ff1" if b == 0 else "ffn_w1_2"][l], 256 * i)
            elif ph["name"] == "ff2":
                w = io["w_ff2" if b == 0 else "ffn_w2_2"][l]
                for i in range(2):
                    for kb in range(8):
                        split_src.append([(lambda t: view4(t), rows(w[512 * kb:512 * kb + 512, 512 * i:512 * i + 512]))])
            elif ph["name"] == "s_out":
                w = io["swa_w_out_2"][0].rearrange("(g s j d) n -> s d g j n", g=2, s=2, j=4, d=HD)
                for i in range(4):
                    split_src.append([(lambda t, half=half, g=g: view8(t)[HD * half:HD * half + HD, 4 * g:4 * g + 4, :],
                                       w[half, :, g, :, 256 * i:256 * i + 256])
                                      for half in range(2) for g in range(2)])
            else:
                for i in range(4):
                    whole(io["w_o"][l] if ph["name"] == "w_o" else io["mlstm_w_out_2"][0], 256 * i)

        stream, split_raw, mod_raw = [], {}, {}

        def push_mods(st):
            for key in st["mods"]:
                layer, b, half = key
                w = io["w_mod" if layer < 2 else "ada_w_2"][layer % 2]
                mod_raw[key] = len(stream)
                stream.append(("mod", len(mod_raw),
                               [(lambda t: view4(t), rows(w[512 * half:512 * half + 512, 512 * b:512 * b + 512]))]))

        def push_split(s):
            if s < len(split_src):
                split_raw[s] = len(stream)
                stream.append(("split", s + 1, split_src[s]))

        for ph in plan:
            for st in ph["steps"]:
                if st["s"] is not None:
                    push_split(st["s"] + 1)
                push_mods(st)
            if ph["kind"] == "mod0":
                push_split(0)
        landed, total = [], [0] * SLOTS
        for t, (_, _, parts) in enumerate(stream):
            total[t % SLOTS] += 16 * len(parts)
            landed.append(total[t % SLOTS])

        release, inner = [], 0
        for ph in plan:
            for st in ph["steps"]:
                if st["s"] is not None:
                    inner += not st["units"]
                    release.append((s_unit, st["u"] + st["units"]) if st["units"] else (s_inner, inner))
        NSPLIT = len(release)
        assert NSPLIT == len(split_src)

        def raw_slot(eng, t):
            eng.wait_ge(s_slot[t % SLOTS], landed[t])
            return ring[:, t % SLOTS, :]

        mod_count = {key: stream[t][1] for key, t in mod_raw.items()}

        def wait_units(eng, n):
            for b in range(4):
                if (n - b + 3) // 4 > 0:
                    eng.wait_ge(s_free[b], (n - b + 3) // 4)

        def wait_unit(eng, u):
            eng.wait_ge(s_free[u % 4], u // 4 + 1)

        def segs(width):
            return [(0, slice(0, LAT))] + ([(1, slice(LAT, ALL))] if width == ALL else [])

        def rope_chunk(ph, c):
            if ph["block"] == 0:
                return (qT if c < 4 else kT)[:, c % 4, 0:LAT]
            return sq_[:, c, :] if c < 8 else sk[:, c - 8, 0:LAT]

        def head_parts(ph, i):
            kind, hh = ph["heads"][i]
            if ph["block"] == 0:
                base, ch = HD * (hh % 2), hh // 2
                if kind == "lat":
                    qs, ks, vs, nk = slice(0, LAT), slice(0, ALL), v_tm[:, 0:4, HD * hh:HD * hh + HD], ALL
                else:
                    qs, ks, vs, nk = slice(LAT, ALL), slice(LAT, ALL), v_tm[:, 2:4, HD * hh:HD * hh + HD], CTX
                out = [x[base:base + HD, 4 + ch, qs] for x in (m_h, m_l)]
                return qT[base:base + HD, ch, qs], kT[base:base + HD, ch, ks], vs, base, nk, out
            kv = hh // 4
            base = HD * (kv % 2)
            ch = 4 * (hh // 8) + hh % 4
            out = [x[base:base + HD, ch, 0:LAT] for x in (m_h, m_l)]
            return sq_[base:base + HD, ch, :], sk[base:base + HD, kv // 2, :], sv[:, :, HD * kv:HD * kv + HD], base, ALL, out

        def nbias(ph, i):
            return 8 * ph["l"] + i

        def hidden_free(ph, g):
            return release[ph["steps"][max(g - 2, 0)]["s"] - (1 if g < 2 else 0)]

        mod_before = {}
        before = None
        for ph in plan:
            for st in ph["steps"]:
                for key in st["mods"]:
                    if key[2] == 0 and before is not None:
                        mod_before[key] = before
                if st["modu"] is not None:
                    before = st["modu"]

        def mod_vectors(key):
            layer, b, _ = key
            return 2 if layer % 2 == 0 or b < 4 else 1

        rpb = io["na_rpb"]
        block = ctx.enter_context(nc.Block())

        @block.sync
        def _(sp):
            for dst, src in ((vec[:, :], io["vec"]), (ones[:, :], io["ones"]), (unit[:, :], io["unit"]),
                             (ident[:, :], io["ident"]), (rot[:, :, :], io["rot"]),
                             (sgub[:, :, :], io["sgub"]), (gateb[:, :], io["gateb"]),
                             (sink[:, :], io["swa_sink_2"].partition_broadcast(P)),
                             (h[:, :, 0:LAT], io["xT"].rearrange("(k p) n -> p k n", p=P))):
                sp.dma_start(dst, src).then_inc(s_const, 16)

            sent = [0]

            def send(upto):
                for t in range(sent[0], upto):
                    if t >= SLOTS:
                        what, count, _ = stream[t - SLOTS]
                        sp.wait_ge(s_wl if what == "split" else s_mtile, count)
                    for put, src in stream[t][2]:
                        sp.dma_start(put(ring[:, t % SLOTS, :]), src).then_inc(s_slot[t % SLOTS], 16)
                sent[0] = max(sent[0], upto)

            for ph in plan:
                kind = ph["kind"]
                if kind == "load_ctx":
                    if ph["block"] == 1:
                        wait_units(sp, ph["u"])
                    sp.dma_start(h[:, :, LAT:ALL], io[f"ctxT{ph['block']}"].rearrange("(k p) n -> p k n", p=P)
                                 ).then_inc(s_ctxld, 16)
                elif kind == "aux":
                    if ph["layer"] > 0:
                        wait_units(sp, ph["u"])
                    if ph["block"] == 0:
                        l = ph["l"]
                        parts = ((A_SGU, 512, io["sgu_wT"][l]), (A_WP, 256, io["w_pool_bd"][l]),
                                 (A_ROPE, 512, io["rope1"]), (A_MASK, 512, io["na_mask"]))
                        sp.dma_start(win, io["pool_win"].rearrange("p (k g n) -> p k g n", k=2, g=4)).then_inc(s_aux, 16)
                    elif ph["l"] == 0:
                        parts = ((A_MF, 2048, io["m_mask"]),)
                    else:
                        parts = ((A_ROPE, 512, io["rope2"]), (A_MASK, 512, io["swa_mask"]))
                    for off, n, src in parts:
                        sp.dma_start(aux[:, off:off + n], src).then_inc(s_aux, 16)
                for st in ph["steps"]:
                    if st["s"] is not None and st["s"] + 1 in split_raw:
                        send(split_raw[st["s"] + 1] + 1)
                    for key in st["mods"]:
                        send(mod_raw[key] + 1)
                if kind == "mod0":
                    send(split_raw[0] + 1)
            sp.wait_ge(s_fin, 2 * KC)
            sp.dma_start(io["out"].rearrange("(k p) n -> p k n", p=P), h[:, :, 0:LAT]).then_inc(s_out, 16)
            sp.wait_ge(s_out, 16)

        AUX_LANDED = [80, 160, 176, 208]
        CONST = 144

        @block.tensor
        def _(pe):
            pe.wait_ge(s_const, CONST)

            def tile(st):
                pe.wait_ge(s_wl, st["s"] + 1)
                return w_h[:, st["s"] % 2, :], w_l[:, st["s"] % 2, :]

            def bank(u):
                if u >= 4:
                    pe.wait_ge(s_free[u % 4], u // 4)
                return PS[:, u % 4, :]

            def product(out, stat, mov, start, stop):
                kw = dict(skip_group_check=True)
                nc.tensor.matmul(out, stat[0], mov[0], start=start, stop=False, **kw)
                nc.tensor.matmul(out, stat[0], mov[1], start=False, stop=False, **kw)
                return nc.tensor.matmul(out, stat[1], mov[0], start=False, stop=stop, **kw)

            def fm(u, w, c, src, n, ks=range(KC), wait_input=None):
                out = bank(u)[:, 0:n]
                for k in ks:
                    if wait_input is not None:
                        pe.wait_ge(s_xl, wait_input + k + 1)
                    mm = product(out, [view8(x)[:, k, c] for x in w], [x[:, k, 0:n] for x in src],
                                 k == ks[0], k == ks[-1])
                mm.then_inc(s_unit, 1)

            def tokm(u, w, tt, wait_input=None):
                out = bank(u)[:, 0:256]
                for k in range(KC):
                    if wait_input is not None:
                        pe.wait_ge(s_xl, wait_input + k + 1)
                    mm = product(out, [x[:, k, P * tt:P * tt + P] for x in (a_h, a_l)],
                                 [view8(x)[:, k, :] for x in w], k == 0, k == KC - 1)
                mm.then_inc(s_unit, 1)

            def mod_unit(st):
                if st["modu"] is None:
                    return
                pe.wait_ge(s_mtile, mod_count[st["mods"][-1]])
                out = bank(st["modu"])[:, 0:8].rearrange("p (c s) -> p c s", s=2)
                for s in range(mod_vectors(st["mods"][-1])):
                    for c in range(4):
                        mm = nc.tensor.matmul(out[:, c, s:s + 1], acc[:, s, P * c:P * c + P], unit[:, 0:1],
                                              start=True, stop=True)
                mm.then_inc(s_unit, 1)

            PA, PM = (a_h, a_l), (m_h, m_l)
            for ph in plan:
                kind, u = ph["kind"], ph["u"]
                cols = ph.get("cols")
                if kind == "mod0":
                    for st in ph["steps"]:
                        mod_unit(st)
                elif kind == "norm":
                    pe.wait_ge(s_sq, ph["norm"] + 1)
                    nc.tensor.matmul(PS[:, 4, 0:ph["width"]], ones[:, :], ssum[:, 0:ph["width"]],
                                     start=True, stop=True).then_inc(s_sqm, 1)
                elif kind == "b1_in":
                    for i, st in enumerate(ph["steps"]):
                        w, u = tile(st), st["u"]
                        need = ph["x"] - KC if i == 0 else None
                        for j in range(st["units"]):
                            if i in (0, 2, 7, 8):
                                tokm(u + j, w, j, need)
                            else:
                                fm(u + j, w, slice(P * j, P * j + P), PA, ALL if i >= 5 else cols)
                        mod_unit(st)
                elif kind == "rope":
                    wait_units(pe, u)
                    for c in range(ph["chunks"]):
                        src = rope_chunk(ph, c)
                        nc.tensor.matmul(bank(u + c)[:, 0:LAT], rot[:, ph["block"], :], src,
                                         start=True, stop=True).then_inc(s_unit, 1)
                elif kind == "pool_sgu":
                    nseg = cols // LAT
                    pe.wait_ge(s_aux, AUX_LANDED[ph["layer"]])
                    for pair in range(2):
                        out = bank(u)
                        for s in range(nseg):
                            for half in range(2):
                                g = 2 * pair + half
                                for k in range(2):
                                    mm = nc.tensor.matmul(
                                        out[HD * half:HD * half + HD, LAT * s:LAT * s + LAT],
                                        p_tm[:, 2 * s + k, HD * g:HD * g + HD], win[:, k, g, :],
                                        start=(k == 0), stop=(k == 1))
                        mm.then_inc(s_unit, 1)
                        u += 1
                    wp = aux[:, A_WP:A_WP + 256].rearrange("p (c n) -> p c n", c=2)
                    for pair in range(2):
                        wait_unit(pe, u - 2)
                        nc.tensor.matmul(bank(u)[:, 0:cols], wp[:, pair, :], pooled[:, pair, 0:cols],
                                         start=True, stop=True).then_inc(s_unit, 1)
                        u += 1
                    pe.wait_ge(s_sgu, ph["layer"] + 1)
                    sw = aux[:, A_SGU:A_SGU + 512].rearrange("p (g n) -> p g n", g=4)
                    for pair in range(2):
                        out = bank(u)
                        for tt in range(cols // P):
                            for half in range(2):
                                g = 2 * pair + half
                                o = out[HD * half:HD * half + HD, P * tt:P * tt + P]
                                nc.tensor.matmul(o, vs_tm[:, tt, HD * g:HD * g + HD], sw[:, g, :],
                                                 start=True, stop=False)
                                mm = nc.tensor.matmul(o, ident[0:4, g:g + 1].broadcast_to([4, HD]), sgub[:, ph["l"], :],
                                                      start=False, stop=True)
                        mm.then_inc(s_unit, 1)
                        u += 1
                elif kind == "ff1":
                    for i, st in enumerate(ph["steps"]):
                        w = tile(st)
                        for c in range(2):
                            fm(st["u"] + c, w, slice(P * c, P * c + P), PA, cols,
                               wait_input=ph["x"] - KC if i == 0 else None)
                        mod_unit(st)
                elif kind == "attn":
                    wait_units(pe, u)
                    n = len(ph["heads"])

                    def scores(i):
                        x = ph["head"] + i
                        if x >= 2:
                            pe.wait_ge(s_exp, x - 1)
                        q, k, _, _, nk, _ = head_parts(ph, i)
                        for qt in range(2):
                            mm = nc.tensor.matmul(PS[:, 2 * (x % 2) + qt, 0:nk], q[:, P * qt:P * qt + P], k,
                                                  start=True, stop=True)
                        mm.then_inc(s_sc, 1)

                    def turn_and_pv(i):
                        x = ph["head"] + i
                        _, _, v, out_base, nk, _ = head_parts(ph, i)
                        pe.wait_ge(s_prob, x + 1)
                        if x >= 1:
                            pe.wait_ge(s_pta, x)
                            pe.wait_ge(s_ptd, x)
                        for qt in range(2):
                            for k in range(nk // P):
                                mm = nc.tensor.transpose(PS[:, 4 + qt, P * k:P * k + P],
                                                         scr[:, x % 2, qt, P * k:P * k + P], ident[:, :])
                        mm.then_inc(s_tr, 1)
                        pe.wait_ge(s_pta, x + 1)
                        pe.wait_ge(s_ptd, x + 1)
                        if x >= 2:
                            pe.wait_ge(s_o, x - 1)
                        o = PS[out_base:out_base + HD, 6 + x % 2, 0:LAT]
                        for k in range(nk // P):
                            mm = nc.tensor.matmul(o, v[:, k, :], pt[:, x % 2, :, k, :],
                                                  start=(k == 0), stop=(k == nk // P - 1))
                        mm.then_inc(s_pv, 1)

                    scores(0)
                    for i in range(n):
                        if i + 1 < n:
                            scores(i + 1)
                        turn_and_pv(i)
                elif kind == "merge":
                    pe.wait_ge(s_o, ph["head"])
                    for i, st in enumerate(ph["steps"]):
                        w, u = tile(st), st["u"]
                        if i % 4 == 0:
                            for c in range(2):
                                for b, ks in enumerate((range(0, 2), range(2, 4), range(4, 8))):
                                    fm(u + 3 * c + b, w, slice(P * c, P * c + P), PM, cols, ks)
                        else:
                            for c in range(2):
                                fm(u + c, w, slice(P * c, P * c + P), PA, cols)
                        mod_unit(st)
                elif kind == "to_h" and ph["src"] != "ff":
                    if ph["src"] == "attn":
                        pe.wait_ge(s_o, ph["head"])
                    for i, st in enumerate(ph["steps"]):
                        w = tile(st)
                        for c in range(2):
                            fm(st["u"] + c, w, slice(P * c, P * c + P), PA if ph["src"] == "a" else PM, cols,
                               wait_input=ph["x"] - KC if i == 0 and ph["src"] != "attn" else None)
                        mod_unit(st)
                elif kind == "to_h":
                    for i in range(2):
                        u = ph["steps"][8 * i + 7]["u"]
                        for kb in range(8):
                            st = ph["steps"][8 * i + kb]
                            w = tile(st)
                            g = 8 * i + kb
                            pe.wait_ge(s_xl, ph["x"] + g + 1)
                            for c in range(4):
                                out = (bank(u + c) if kb == 0 else PS[:, (u + c) % 4, :])[:, 0:cols]
                                for k in range(4):
                                    j = 4 * (g % 2) + k
                                    mm = product(out, [view4(x)[:, k, P * c:P * c + P] for x in w],
                                                 [x[:, j, 0:cols] for x in PA], kb == 0 and k == 0,
                                                 kb == 7 and k == 3)
                                if kb == 7:
                                    mm.then_inc(s_unit, 1)
                            if kb < 7:
                                mm.then_inc(s_inner, 1)
                elif kind == "m_in":
                    for i, st in enumerate(ph["steps"]):
                        w, u = tile(st), st["u"]
                        need = ph["x"] - KC if i == 0 else None
                        for j in range(st["units"]):
                            if 4 <= i < 8:
                                tokm(u + j, w, j)
                            elif i < 12:
                                fm(u + j, w, slice(P * j, P * j + P), PA, ALL, wait_input=need)
                            else:
                                fm(u + j, w, slice(MH * j, MH * j + P), PA, ALL)
                        mod_unit(st)
                elif kind == "m_gates":
                    pe.wait_ge(s_gr, 1)
                    out = bank(u).rearrange("p (w t g n) -> p w t g n", w=2, t=4, g=2, n=32)
                    for what in range(2):
                        for d in range(2):
                            src = G[:, 2 * d + 1, :] if what == 0 else Bc[:, d, :]
                            for tt in range(4):
                                mm = nc.tensor.transpose(out[:, what, tt, d, 0:MH], src[:, P * tt:P * tt + P],
                                                         ident[0:MH, 0:MH])
                    mm.then_inc(s_unit, 1)
                elif kind == "m_heads":
                    wait_units(pe, u)
                    pe.wait_ge(s_aux, AUX_LANDED[2])

                    def qk(b):
                        hh, qt = b // 4, b % 4
                        if qt == 0:
                            if b:
                                pe.wait_ge(s_D, b)
                            for d in range(2):
                                nc.tensor.matmul(PS[:, d, :], ident[0:MH, hh:hh + 1].broadcast_to([MH, P]),
                                                 G[:, 2 * d, :], start=True, stop=True)
                        if b >= 2:
                            pe.wait_ge(s_W, b - 1)
                        c0 = 0 if qt < 2 else LAT
                        base = HD * (hh % 2)
                        nc.tensor.matmul(PS[:, 2 + b % 2, 0:ALL - c0],
                                         mq[base:base + HD, hh // 2, P * qt:P * qt + P],
                                         mk[base:base + HD, hh // 2, c0:ALL], start=True, stop=True).then_inc(s_qk, 1)

                    def pv(b):
                        hh, qt = b // 4, b % 4
                        k0 = 0 if qt < 2 else 2
                        pe.wait_ge(s_P, b + 1)
                        if b >= 2:
                            pe.wait_ge(s_mpt, b - 1)
                        for k in range(k0, 4):
                            mm = nc.tensor.transpose(PS[:, 4 + b % 2, P * (k - k0):P * (k - k0) + P],
                                                     scr[:, b % 2, 0, P * (k - k0):P * (k - k0) + P], ident[:, :])
                        mm.then_inc(s_mt, 1)
                        pe.wait_ge(s_mpt, b + 1)
                        if qt == 0 and hh >= 2:
                            pe.wait_ge(s_mo, hh - 1)
                        for k in range(k0, 4):
                            mm = nc.tensor.matmul(PS[:, 6 + hh % 2, P * qt:P * qt + P], mv[:, k, P * hh:P * hh + P],
                                                  pt[:, b % 2, 0, k - k0, :], start=(k == k0), stop=(k == 3))
                        mm.then_inc(s_mpv, 1)

                    n = 4 * MH
                    qk(0)
                    qk(1)
                    for b in range(n):
                        if b + 2 < n:
                            qk(b + 2)
                        pv(b)
                elif kind == "m_norm":
                    for hh in range(MH):
                        pe.wait_ge(s_msq, hh + 1)
                        nc.tensor.matmul(bank(u + hh), ones[:, :], msq[:, hh, :], start=True, stop=True
                                         ).then_inc(s_unit, 1)
                elif kind == "s_in":
                    for i, st in enumerate(ph["steps"]):
                        w, u = tile(st), st["u"]
                        need = ph["x"] - KC if i == 0 else None
                        for j in range(st["units"]):
                            if i == 5:
                                tokm(u + j, w, j)
                            else:
                                fm(u + j, w, slice(P * j, P * j + P), PA, ALL if i == 4 else LAT, wait_input=need)
                        mod_unit(st)

        @block.scalar
        def _(act):
            act.wait_ge(s_const, CONST)
            steps = [0]

            def step(ins):
                steps[0] += 1
                ins.then_inc(s_act, 1)
                act.wait_ge(s_act, steps[0])

            def copy_unit(u, out, src_cols, func=ACT.Copy, m=P, **kw):
                act.wait_ge(s_unit, u + 1)
                nc.scalar.activation(out, PS[0:m, u % 4, src_cols], func, **kw).then_inc(s_free[u % 4], 1)

            def round_w(n):
                if n >= NSPLIT:
                    return
                raw = raw_slot(act, split_raw[n])
                if n >= 2:
                    act.wait_ge(*release[n - 2])
                nc.scalar.activation(w_h[:, n % 2, :], raw, ACT.Copy).then_inc(s_wh, 1)

            def steps_of(ph):
                for i, st in enumerate(ph["steps"]):
                    if st["s"] is not None:
                        round_w(st["s"] + 1)
                    yield i, st, st["u"]

            for b in range(2):
                c0 = V_COND + b * 2 * KC
                nc.scalar.activation(silu[:, b, :, :].rearrange("p k n -> p (k n)"),
                                     vec[:, c0:c0 + 2 * KC], ACT.Sigmoid).then_inc(s_silu_a, 1)
            for ph in plan:
                kind, u = ph["kind"], ph["u"]
                cols = ph.get("cols")
                if kind == "mod0":
                    round_w(0)
                elif kind == "norm":
                    n0 = ph["norm"]
                    act.wait_ge(s_var, n0 + 1)
                    nc.scalar.activation(rs[:, 0:ph["width"]], rs[:, 0:ph["width"]], ACT.Sqrt).then_inc(s_std, 1)
                    which, b = ph["which"], ph["block"]
                    if not ph["final"]:
                        wait_units(act, ph["u"])
                    for k in range(KC):
                        act.wait_ge(s_nrm, KC * n0 + k + 1)
                        if ph["final"]:
                            nc.scalar.activation(h[:, k, 0:LAT], nrm[:, k % 2, 0:LAT], ACT.Copy,
                                                 scale=vec[:, V_FIN + KC * b + k:V_FIN + KC * b + k + 1]
                                                 ).then_inc(s_fin, 1)
                            continue
                        for s, c in segs(ph["width"]):
                            ins = nc.scalar.activation(nrm[:, k % 2, c], nrm[:, k % 2, c], ACT.Identity,
                                                       scale=gain[:, which, k, s:s + 1],
                                                       bias=mod[:, ph["layer"] % 2, 24 * which + k, s:s + 1])
                        step(ins)
                        nc.scalar.activation(a_h[:, k, 0:ph["width"]], nrm[:, k % 2, 0:ph["width"]], ACT.Copy
                                             ).then_inc(s_xh, 1)
                elif kind == "b1_in":
                    for i, st, u in steps_of(ph):
                        for j in range(st["units"]):
                            if i == 0:
                                copy_unit(u + j, p_tm[:, j, :], slice(0, 256))
                            elif i == 1:
                                copy_unit(u + j, uT[:, j, 0:cols], slice(0, cols))
                            elif i == 2:
                                copy_unit(u + j, vs_tm[:, j, :], slice(0, 256))
                            elif i in (3, 4):
                                act.wait_ge(s_unit, u + j + 1)
                                nc.scalar.activation(
                                    qT[:, 2 * (i - 3) + j, 0:cols].rearrange("p (q n) -> p q n", n=P)[:, :, ::-1],
                                    PS[:, (u + j) % 4, 0:cols].rearrange("p (q n) -> p q n", n=P), ACT.Copy,
                                    scale=QSCALE).then_inc(s_free[(u + j) % 4], 1)
                            elif i >= 7:
                                copy_unit(u + j, v_tm[:, j, 256 * (i - 7):256 * (i - 7) + 256], slice(0, 256))
                        if i == 4:
                            ln0 = 4 * ph["l"]
                            for tt in range(cols // P):
                                act.wait_ge(s_lnv, ln0 + tt + 1)
                                nc.scalar.activation(lnst[:, 4:5], lnst[:, 3:4], ACT.Sqrt).then_inc(s_lns, 1)
                elif kind == "ff1":
                    for i, st, u in steps_of(ph):
                        for c in range(2):
                            copy_unit(u + c, hid[:, 2 * i + c, 0:cols], slice(0, cols), ACT.Relu)
                elif kind == "to_h" and ph["src"] == "ff":
                    def round_hidden(g):
                        if g >= 16:
                            return
                        act.wait_ge(s_ff, 32 * ph["layer"] + 4 * (g % 8) + 4)
                        act.wait_ge(*hidden_free(ph, g))
                        nc.scalar.activation(a_h[:, 4 * (g % 2):4 * (g % 2) + 4, 0:cols],
                                             hid[:, 4 * (g % 8):4 * (g % 8) + 4, 0:cols], ACT.Copy).then_inc(s_xh, 1)

                    round_hidden(0)
                    for i, st, u in steps_of(ph):
                        round_hidden(i + 1)
                elif kind == "to_h":
                    for i, st, u in steps_of(ph):
                        pass
                elif kind == "merge":
                    def round_y(c):
                        act.wait_ge(s_y, ph["y"] + 6 * (c // 2) + 4 + c % 2 + 1)
                        nc.scalar.activation(m_h[:, c, 0:cols], yT[:, c, 0:cols], ACT.Copy).then_inc(s_xh, 1)

                    for i, st, u in steps_of(ph):
                        g = i % 4 - 1
                        if g < 0:
                            if i:
                                act.wait_ge(s_y, ph["y"] + 6 * (i // 4))
                            for j in range(6):
                                copy_unit(u + j, br[:, j, 0:cols], slice(0, cols))
                        else:
                            for c in range(2):
                                idx = 6 * (i // 4) + 2 * g + c
                                if idx >= 2:
                                    act.wait_ge(s_y, ph["y"] + idx - 1)
                                copy_unit(u + c, gate[:, c, 0:cols], slice(0, cols), ACT.Sigmoid)
                        if i == 13:
                            act.wait_ge(*release[ph["steps"][12]["s"]])
                        if i >= 13:
                            round_y(2 * (i - 13))
                            round_y(2 * (i - 13) + 1)
                    round_y(6)
                    round_y(7)
                elif kind == "attn":
                    n = len(ph["heads"])

                    def exps(i):
                        x = ph["head"] + i
                        nk = head_parts(ph, i)[4]
                        act.wait_ge(s_nm, x + 1)
                        if x >= 2:
                            act.wait_ge(s_tr, x - 1)
                        for qt in range(2):
                            if ph["block"] == 1:
                                hh = ph["heads"][i][1]
                                nc.scalar.activation(esink[:, x % 2, qt:qt + 1], sink[:, hh:hh + 1], ACT.Exp,
                                                     bias=nmax[:, x % 2, qt:qt + 1])
                            ins = nc.scalar.activation(scr[:, x % 2, qt, 0:nk], PS[:, 2 * (x % 2) + qt, 0:nk], ACT.Exp,
                                                       bias=nmax[:, x % 2, qt:qt + 1],
                                                       accum_out=rsum[:, x % 2, qt:qt + 1])
                        ins.then_inc(s_exp, 1)

                    def probs_t(i):
                        x = ph["head"] + i
                        nk = head_parts(ph, i)[4]
                        act.wait_ge(s_tr, x + 1)
                        if x >= 2:
                            act.wait_ge(s_pv, x - 1)
                        nc.scalar.activation(pt[:, x % 2, 0, 0:nk // P, :],
                                             PS[:, 4, 0:nk].rearrange("p (k n) -> p k n", n=P), ACT.Copy
                                             ).then_inc(s_pta, 1)

                    for i in range(n + 1):
                        if i < n:
                            exps(i)
                        if i >= 1:
                            probs_t(i - 1)
                elif kind == "m_in":
                    for i, st, u in steps_of(ph):
                        for j in range(st["units"]):
                            if i < 4:
                                copy_unit(u + j, (mq if i < 2 else mk)[:, 2 * (i % 2) + j, :], slice(0, 512),
                                          scale=1.0 if i < 2 else QSCALE)
                            elif 8 <= i < 12:
                                copy_unit(u + j, sigo[:, 2 * (i - 8) + j, :], slice(0, 512), ACT.Sigmoid)
                            elif i == 12:
                                if j == 0:
                                    act.wait_ge(s_unit, u + 4)
                                copy_unit(u + j, G[:, j, :], slice(0, 512), ACT.Identity, m=MH, bias=gateb[:, j:j + 1])
                elif kind == "m_gates":
                    wait_units(act, u)
                    for d in range(2):
                        step(nc.scalar.activation(Bc[:, d, :], G[:, 2 * d + 1, :], ACT.Abs))
                        step(nc.scalar.activation(Bc[:, d, :], Bc[:, d, :], ACT.Exp, scale=-1.0))
                        nc.scalar.activation(Bc[:, d, :], Bc[:, d, :], ACT.Ln, bias=1.0).then_inc(s_ga, 1)
                    act.wait_ge(s_gd, 1)
                    nc.scalar.activation(Bc[:, :, :], Bc[:, :, :], ACT.Exp, scale=-1.0).then_inc(s_gr, 1)
                elif kind == "m_heads":
                    def decay(b):
                        nk = ALL if b % 4 < 2 else CTX
                        act.wait_ge(s_D, b + 1)
                        nc.scalar.activation(scr[:, b % 2, :, 0:nk], scr[:, b % 2, :, 0:nk], ACT.Exp).then_inc(s_A, 1)

                    def turned(b):
                        nk = ALL if b % 4 < 2 else CTX
                        act.wait_ge(s_mt, b + 1)
                        if b >= 2:
                            act.wait_ge(s_mpv, b - 1)
                        nc.scalar.activation(pt[:, b % 2, 0, 0:nk // P, :],
                                             PS[:, 4 + b % 2, 0:nk].rearrange("p (k n) -> p k n", n=P), ACT.Copy
                                             ).then_inc(s_mpt, 1)

                    def head_out(hh):
                        act.wait_ge(s_mpv, 4 * hh + 4)
                        nc.scalar.activation(hs[:, hh, :], PS[:, 6 + hh % 2, :], ACT.Copy).then_inc(s_mo, 1)

                    n = 4 * MH
                    for b in range(n + 1):
                        if b < n:
                            decay(b)
                        if b >= 1:
                            turned(b - 1)
                            if b % 4 == 1 and b > 4:
                                head_out(b // 4 - 1)
                    head_out(MH - 1)
                elif kind == "m_norm":
                    for hh in range(MH):
                        wait_unit(act, u + hh)
                        nc.scalar.activation(big[:, hh, :], big[:, hh, :], ACT.Sqrt).then_inc(s_mrs, 1)
                    for hh in range(MH):
                        act.wait_ge(s_hs, hh + 1)
                        nc.scalar.activation(a_h[:, hh, :], hs[:, hh, :], ACT.Copy).then_inc(s_xh, 1)
                elif kind == "s_in":
                    for i, st, u in steps_of(ph):
                        for j in range(st["units"] if i < 4 else 0):
                            copy_unit(u + j, sq_[:, 2 * i + j, :], slice(0, LAT), scale=QSCALE)

        @block.vector
        def _(dve):
            dve.wait_ge(s_const, CONST)
            steps = [0]

            def step(ins):
                steps[0] += 1
                ins.then_inc(s_dve, 1)
                dve.wait_ge(s_dve, steps[0])

            V = nc.vector
            lnc = [0]

            def copy_unit(u, out, src_cols):
                dve.wait_ge(s_unit, u + 1)
                V.tensor_copy(out, PS[:, u % 4, src_cols]).then_inc(s_free[u % 4], 1)

            def split_w(n):
                if n >= NSPLIT:
                    return
                dve.wait_ge(s_wh, n + 1)
                if n >= 2:
                    dve.wait_ge(*release[n - 2])
                V.tensor_tensor(w_l[:, n % 2, :], ring[:, split_raw[n] % SLOTS, :], w_h[:, n % 2, :].bitcast(F32),
                                ALU.subtract).then_inc(s_wl, 1)

            def mod_tile(key, st):
                layer, b, half = key
                w = view4(raw_slot(dve, mod_raw[key]))
                if half == 0 and key in mod_before:
                    dve.wait_ge(s_unit, mod_before[key] + 1)
                if half:
                    dve.wait_ge(s_mtile, mod_count[key] - 1)
                nv = mod_vectors(key)
                last = [None, None]
                for k in range(4):
                    for v in range(nv):
                        if last[v] is not None:
                            dve.wait_ge(s_dve, last[v])
                        sc = silu[:, layer // 2, 4 * half + k, v:v + 1]
                        if half == 0 and k == 0:
                            ins = V.tensor_scalar(acc[:, v, :], w[:, k, :], sc, None, ALU.mult)
                        else:
                            ins = V.scalar_tensor_tensor(out=acc[:, v, :], in0=w[:, k, :], scalar=sc,
                                                         in1=acc[:, v, :], op0=ALU.mult, op1=ALU.add)
                        if k == 3 and v == nv - 1:
                            ins.then_inc(s_mtile, 1)
                        else:
                            steps[0] += 1
                            last[v] = steps[0]
                            ins.then_inc(s_dve, 1)

            def mod_columns(st):
                if st["modu"] is None:
                    return
                layer, b, _ = st["mods"][-1]
                nv, mu = mod_vectors(st["mods"][-1]), st["modu"]
                dve.wait_ge(s_unit, mu + 1)
                m = mod[:, layer % 2, :, :]
                b0 = V_BMOD + 48 * layer + 4 * b
                ins = V.tensor_tensor(m[:, 4 * b:4 * b + 4, 0:nv],
                                      PS[:, mu % 4, 0:8].rearrange("p (c s) -> p c s", s=2)[:, :, 0:nv],
                                      vec[:, b0:b0 + 4].unsqueeze(2).broadcast_to([P, 4, nv]), ALU.add)
                if b in (3, 9):
                    which = 0 if b == 3 else 1
                    vg = (V_N1, V_N2)[which]
                    step(ins)
                    out = gain[:, which, :, 0:nv]
                    step(V.tensor_scalar(out, m[:, 24 * which + 8:24 * which + 16, 0:nv], 1.0, None, ALU.add))
                    ins = V.tensor_tensor(out, out, vec[:, vg + KC * layer:vg + KC * layer + KC]
                                          .unsqueeze(2).broadcast_to([P, KC, nv]), ALU.mult)
                ins.then_inc(s_free[mu % 4], 1)

            def steps_of(ph):
                for i, st in enumerate(ph["steps"]):
                    if st["s"] is not None:
                        split_w(st["s"] + 1)
                    for key in st["mods"]:
                        mod_tile(key, st)
                    yield i, st, st["u"]
                    mod_columns(st)

            def rest_x(n, lo, x, hi):
                dve.wait_ge(s_xh, n + 1)
                V.tensor_tensor(lo, x, hi.bitcast(F32), ALU.subtract).then_inc(s_xl, 1)

            for b in range(2):
                c0 = V_COND + b * 2 * KC
                dve.wait_ge(s_silu_a, b + 1)
                x = silu[:, b, :, :].rearrange("p k n -> p (k n)")
                step(V.tensor_tensor(x, x, vec[:, c0:c0 + 2 * KC], ALU.mult))
            for ph in plan:
                kind, u = ph["kind"], ph["u"]
                cols = ph.get("cols")
                if kind == "mod0":
                    for _ in steps_of(ph):
                        pass
                    split_w(0)
                elif kind == "norm":
                    n0, w = ph["norm"], ph["width"]
                    dve.wait_ge(s_sqm, n0 + 1)
                    V.tensor_scalar(rs[:, 0:w], PS[:, 4, 0:w], EPS, None, ALU.add).then_inc(s_var, 1)
                    dve.wait_ge(s_std, n0 + 1)
                    step(V.reciprocal(rs[:, 0:w], rs[:, 0:w]))

                    def scaled(k):
                        if k < KC:
                            if k >= 2 and not ph["final"]:
                                dve.wait_ge(s_xl, ph["x"] + k - 1)
                            V.tensor_tensor(nrm[:, k % 2, 0:w], h[:, k, 0:w], rs[:, 0:w], ALU.mult).then_inc(s_nrm, 1)

                    scaled(0)
                    scaled(1)
                    for k in range(KC):
                        if ph["final"]:
                            dve.wait_ge(s_fin, KC * ph["block"] + k + 1)
                        else:
                            rest_x(ph["x"] + k, a_l[:, k, 0:w], nrm[:, k % 2, 0:w], a_h[:, k, 0:w])
                        scaled(k + 2)
                elif kind == "b1_in":
                    for i, st, u in steps_of(ph):
                        if i in (5, 6):
                            for j in range(2):
                                copy_unit(u + j, kT[:, 2 * (i - 5) + j, :], slice(0, 512))
                        if i == 4:
                            for tt in range(cols // P):
                                wait_unit(dve, ph["steps"][2]["u"] + tt)
                                x = vs_tm[:, tt, :]
                                step(V.reduce_sum(lnst[:, 0:1], x, AX_X))
                                step(V.tensor_scalar(lnst[:, 1:2], lnst[:, 0:1], 1.0 / 256, None, ALU.mult))
                                step(V.tensor_scalar(x, x, lnst[:, 1:2], None, ALU.subtract))
                                step(V.tensor_tensor_reduce(pt[:, 0, 0, 0:2, :].rearrange("p b n -> p (b n)"), x, x,
                                                            1.0, 0.0, ALU.mult, ALU.add, lnst[:, 2:3]))
                                V.tensor_scalar(lnst[:, 3:4], lnst[:, 2:3], 1.0 / 256, EPS, ALU.mult, ALU.add
                                                ).then_inc(s_lnv, 1)
                                lnc[0] += 1
                                dve.wait_ge(s_lns, lnc[0])
                                step(V.reciprocal(lnst[:, 5:6], lnst[:, 4:5]))
                                ins = V.tensor_scalar(x, x, lnst[:, 5:6], None, ALU.mult)
                                if tt == cols // P - 1:
                                    ins.then_inc(s_sgu, 1)
                elif kind == "rope":
                    dve.wait_ge(s_aux, AUX_LANDED[ph["layer"]])
                    wait_units(dve, u)
                    cs = aux[:, A_ROPE:A_ROPE + 512].rearrange("p (s n) -> p s n", s=2)
                    for c in range(ph["chunks"]):
                        x = rope_chunk(ph, c)
                        dve.wait_ge(s_unit, u + c + 1)
                        tmp = bias[:, 0, 0:LAT].rearrange("p (q n) -> p q n", n=P)

                        def tiles_of(y):
                            return y.rearrange("p (q n) -> p q n", n=P)

                        cos, sin = tiles_of(cs[:, 0, :]), tiles_of(cs[:, 1, :])
                        if ph["block"] == 0 and c < 4:
                            cos, sin = cos[:, :, ::-1], sin[:, :, ::-1]
                        x = tiles_of(x)
                        V.tensor_tensor(tmp, tiles_of(PS[:, (u + c) % 4, 0:LAT]), sin, ALU.mult)
                        step(V.tensor_tensor(x, x, cos, ALU.mult))
                        V.tensor_tensor(x, x, tmp, ALU.add).then_inc(s_free[(u + c) % 4], 1)
                        dve.wait_ge(s_free[(u + c) % 4], (u + c) // 4 + 1)
                elif kind == "pool_sgu":
                    for pair in range(2):
                        copy_unit(u, pooled[:, pair, 0:cols], slice(0, cols))
                        u += 1
                    for pair in range(2):
                        dve.wait_ge(s_unit, u + 1)
                        c = V_PS + 2 * ph["l"] + pair
                        hi = m_h[:, pair, 0:cols]
                        step(V.tensor_scalar(hi, PS[:, u % 4, 0:cols], vec[:, c:c + 1], None, ALU.mult))
                        V.scalar_tensor_tensor(out=m_l[:, pair, 0:cols], in0=PS[:, u % 4, 0:cols], scalar=vec[:, c:c + 1],
                                               in1=hi.bitcast(F32), op0=ALU.mult, op1=ALU.subtract
                                               ).then_inc(s_free[u % 4], 1)
                        u += 1
                    for pair in range(2):
                        dve.wait_ge(s_unit, u + 1)
                        x, hi = uT[:, pair, 0:cols], m_h[:, 2 + pair, 0:cols]
                        step(V.tensor_tensor(x, PS[:, u % 4, 0:cols], x, ALU.mult))
                        step(V.tensor_copy(hi, x))
                        V.tensor_tensor(m_l[:, 2 + pair, 0:cols], x, hi.bitcast(F32), ALU.subtract
                                        ).then_inc(s_free[u % 4], 1)
                        u += 1
                elif kind == "attn":
                    n = len(ph["heads"])
                    if ph["block"] == 1:
                        dve.wait_ge(s_aux, AUX_LANDED[3])

                    def rowmax(i):
                        x = ph["head"] + i
                        what, hh = ph["heads"][i]
                        nk = head_parts(ph, i)[4]
                        S = PS[:, 2 * (x % 2):2 * (x % 2) + 2, :]
                        dve.wait_ge(s_sc, x + 1)
                        if what == "lat":
                            if ph["block"] == 0:
                                dve.wait_ge(s_bias, nbias(ph, i) + 1)
                                add = bias[:, hh % 2, :].rearrange("p (q n) -> p q n", q=2)
                            else:
                                add = aux[:, A_MASK:A_MASK + 512].rearrange("p (q n) -> p q n", q=2)
                            step(V.tensor_tensor(S[:, :, 0:LAT], S[:, :, 0:LAT], add, ALU.add))
                        m = nmax[:, x % 2, :]
                        step(V.tensor_reduce(m, S[:, :, 0:nk], AX_X, ALU.max))
                        if ph["block"] == 1:
                            step(V.tensor_scalar(m, m, sink[:, hh:hh + 1], None, ALU.max))
                        V.tensor_scalar(m, m, -1.0, None, ALU.mult).then_inc(s_nm, 1)

                    def inverse(i):
                        x = ph["head"] + i
                        dve.wait_ge(s_exp, x + 1)
                        if ph["block"] == 1:
                            step(V.tensor_tensor(rsum[:, x % 2, :], rsum[:, x % 2, :], esink[:, x % 2, :], ALU.add))
                        step(V.reciprocal(rinv[:, x % 2, :], rsum[:, x % 2, :]))
                        nk = head_parts(ph, i)[4]
                        for qt in range(2):
                            p_ = scr[:, x % 2, qt, 0:nk]
                            ins = V.tensor_scalar(p_, p_, rinv[:, x % 2, qt:qt + 1], None, ALU.mult)
                        ins.then_inc(s_prob, 1)

                    def probs_t(i):
                        x = ph["head"] + i
                        nk = head_parts(ph, i)[4]
                        dve.wait_ge(s_tr, x + 1)
                        if x >= 2:
                            dve.wait_ge(s_pv, x - 1)
                        V.tensor_copy(pt[:, x % 2, 1, 0:nk // P, :],
                                      PS[:, 5, 0:nk].rearrange("p (k n) -> p k n", n=P)).then_inc(s_ptd, 1)

                    def out(i):
                        x = ph["head"] + i
                        base, o = head_parts(ph, i)[3], head_parts(ph, i)[5]
                        dve.wait_ge(s_pv, x + 1)
                        src = PS[base:base + HD, 6 + x % 2, 0:LAT].rearrange("p (q n) -> p q n", q=2)
                        if ph["block"] == 0:
                            src = src[:, :, ::-1]
                        hi, lo = (y.rearrange("p (q n) -> p q n", q=2) for y in o)
                        step(V.tensor_copy(hi, src))
                        V.tensor_tensor(lo, src, hi.bitcast(F32), ALU.subtract).then_inc(s_o, 1)

                    rowmax(0)
                    for i in range(n + 1):
                        if i < n:
                            inverse(i)
                            if i + 1 < n:
                                rowmax(i + 1)
                            probs_t(i)
                        if i >= 1:
                            out(i - 1)
                elif kind == "merge":
                    def rest_y(c):
                        rest_x(ph["x"] + c, m_l[:, c, 0:cols], yT[:, c, 0:cols], m_h[:, c, 0:cols])

                    for i, st, u in steps_of(ph):
                        g = i % 4 - 1
                        for c in range(2 if g >= 0 else 0):
                            wait_unit(dve, ph["steps"][i - 1 - g]["u"] + 3 * c + g)
                            wait_unit(dve, u + c)
                            y, x, gt = yT[:, 2 * (i // 4) + c, 0:cols], br[:, 3 * c + g, 0:cols], gate[:, c, 0:cols]
                            if g == 0:
                                ins = V.tensor_tensor(y, x, gt, ALU.mult)
                            else:
                                step(V.tensor_tensor(x, x, gt, ALU.mult))
                                ins = V.tensor_tensor(y, y, x, ALU.add)
                            ins.then_inc(s_y, 1)
                            if g >= 0 and c == 1:
                                dve.wait_ge(s_y, ph["y"] + 6 * (i // 4) + 2 * g + 2)
                        if i >= 13:
                            rest_y(2 * (i - 13))
                            rest_y(2 * (i - 13) + 1)
                    rest_y(6)
                    rest_y(7)
                elif kind == "to_h":
                    for i, st, u in steps_of(ph):
                        for j in range(st["units"]):
                            c = (2 * i + j) if ph["src"] != "ff" else 4 * (i // 8) + j
                            dve.wait_ge(s_unit, u + j + 1)
                            for s, cc in segs(cols):
                                ins = V.scalar_tensor_tensor(
                                    out=h[:, c, cc], in0=PS[:, (u + j) % 4, cc],
                                    scalar=mod[:, ph["layer"] % 2, 8 * ph["gate"] + c, s:s + 1],
                                    in1=h[:, c, cc], op0=ALU.mult, op1=ALU.add)
                            ins.then_inc(s_free[(u + j) % 4], 1)
                elif kind == "ff1":
                    for _ in steps_of(ph):
                        pass
                elif kind == "m_in":
                    for i, st, u in steps_of(ph):
                        for j in range(st["units"] if 4 <= i < 8 else 0):
                            copy_unit(u + j, mv[:, j, 256 * (i - 4):256 * (i - 4) + 256], slice(0, 256))
                elif kind == "m_gates":
                    wait_units(dve, u)
                    step(V.memset(one_row, 1.0))
                    for d in range(2):
                        li, lf, B = G[:, 2 * d, :], G[:, 2 * d + 1, :], Bc[:, d, :]
                        dve.wait_ge(s_ga, d + 1)
                        step(V.tensor_scalar(lf, lf, 0.0, None, ALU.min))
                        step(V.tensor_tensor(lf, lf, B, ALU.subtract))
                        if d == 0:
                            parts = (slice(LAT, ALL), slice(0, LAT))
                            last = (slice(ALL - 1, ALL), None)
                        else:
                            parts = (slice(ALL - 1, LAT - 1, -1), slice(LAT - 1, None, -1))
                            last = (slice(LAT, LAT + 1), None)
                        ini = 0.0
                        for pr, la in zip(parts, last):
                            step(V.tensor_tensor_scan(B[:, pr], one_row[:, pr], lf[:, pr], ini, ALU.mult, ALU.add))
                            ini = None if la is None else B[:, la]
                        step(V.tensor_tensor(li, li, B, ALU.subtract))
                        M = lf
                        ini = 0.0
                        for pr, la in zip(parts, last):
                            step(V.tensor_tensor_scan(M[:, pr], li[:, pr], li[:, pr], ini, ALU.max, ALU.max))
                            ini = None if la is None else M[:, la]
                        ins = V.tensor_tensor(B, B, M, ALU.add)
                        if d == 1:
                            ins.then_inc(s_gd, 1)
                        else:
                            step(ins)
                    dve.wait_ge(s_unit, u + 1)
                    src = PS[:, u % 4, :].rearrange("p (w t g n) -> p w t g n", w=2, t=4, g=2, n=32)
                    for what in range(2):
                        for d in range(2):
                            ins = V.tensor_scalar(tm[:, what, :, :, d], src[:, what, :, d, 0:MH],
                                                  -1.0 if what == 0 else 1.0, None, ALU.mult)
                            if not (what and d):
                                step(ins)
                    ins.then_inc(s_free[u % 4], 1)
                elif kind == "m_heads":
                    dve.wait_ge(s_aux, AUX_LANDED[2])
                    mask = aux[:, A_MF:A_MF + 2048].rearrange("p (d q n) -> p d q n", d=2, q=2)
                    wait_units(dve, u)

                    def args(b, d):
                        hh, qt = b // 4, b % 4
                        c0 = 0 if qt < 2 else LAT
                        nk = ALL - c0
                        if d == 0:
                            dve.wait_ge(s_qk, b + 1)
                            if b >= 2:
                                dve.wait_ge(s_mt, b - 1)
                        ins = V.scalar_tensor_tensor(out=scr[:, b % 2, d, 0:nk], in0=PS[:, d, c0:ALL],
                                                     scalar=tm[:, 0, qt, hh, d:d + 1],
                                                     in1=mask[:, d, qt % 2, 0:nk], op0=ALU.add, op1=ALU.min)
                        if d == 1:
                            ins.then_inc(s_D, 1)

                    n = 4 * MH
                    args(0, 0)
                    args(0, 1)
                    for b in range(n):
                        hh, qt = b // 4, b % 4
                        nk = ALL if qt < 2 else CTX
                        dve.wait_ge(s_A, b + 1)
                        dn, rc = den[:, b % 2, 0, :], den[:, b % 2, 1, :]
                        x0, x1 = scr[:, b % 2, 0, 0:nk], scr[:, b % 2, 1, 0:nk]
                        for d, x in enumerate((x0, x1)):
                            ins = V.tensor_tensor_reduce(x, x, PS[:, 2 + b % 2, 0:nk], 1.0, 0.0, ALU.mult, ALU.add,
                                                         dn[:, d:d + 1])
                        ins.then_inc(s_W, 1)
                        if b + 1 < n:
                            args(b + 1, 0)
                        dve.wait_ge(s_W, b + 1)
                        step(V.scalar_tensor_tensor(out=rc, in0=dn, scalar=-1.0, in1=dn, op0=ALU.mult, op1=ALU.max))
                        step(V.tensor_tensor(rc, rc, tm[:, 1, qt, hh, :], ALU.max))
                        steps[0] += 1
                        V.reciprocal(rc, rc).then_inc(s_dve, 1)
                        if b + 1 < n:
                            args(b + 1, 1)
                        dve.wait_ge(s_dve, steps[0])
                        step(V.tensor_scalar(x0, x0, rc[:, 0:1], None, ALU.mult))
                        V.scalar_tensor_tensor(out=x0, in0=x1, scalar=rc[:, 1:2], in1=x0, op0=ALU.mult, op1=ALU.add
                                               ).then_inc(s_P, 1)
                elif kind == "m_norm":
                    for hh in range(MH):
                        dve.wait_ge(s_unit, u + hh + 1)
                        V.tensor_scalar(big[:, hh, :], PS[:, (u + hh) % 4, :], D / MDV, EPS, ALU.mult, ALU.add
                                        ).then_inc(s_free[(u + hh) % 4], 1)
                    for hh in range(MH + 3):
                        if hh < MH:
                            r = big[:, hh, :]
                            dve.wait_ge(s_mrs, hh + 1)
                            step(V.reciprocal(r, r))
                            V.scalar_tensor_tensor(out=hs[:, hh, :], in0=hs[:, hh, :],
                                                   scalar=vec[:, V_HN + hh:V_HN + hh + 1], in1=r,
                                                   op0=ALU.mult, op1=ALU.mult).then_inc(s_hn, 1)
                        if hh >= 3:
                            rest_x(ph["x"] + hh - 3, a_l[:, hh - 3, :], hs[:, hh - 3, :], a_h[:, hh - 3, :])
                elif kind == "s_in":
                    for i, st, u in steps_of(ph):
                        for j in range(st["units"] if i >= 4 else 0):
                            if i == 4:
                                copy_unit(u + j, sk[:, j, :], slice(0, 512))
                            else:
                                copy_unit(u + j, sv[:, j, :], slice(0, 256))

        @block.gpsimd
        def _(pool):
            pool.wait_ge(s_const, CONST)
            steps = [0]
            nb = [0]
            for ph in plan:
                kind, u = ph["kind"], ph["u"]
                cols = ph.get("cols")
                if kind == "norm":
                    w = ph["width"]
                    if ph["which"] == 0 and ph["l"] == 0:
                        pool.wait_ge(s_ctxld, 16 * (ph["block"] + 1))
                        if ph["block"] == 1:
                            pool.wait_ge(s_fin, KC)
                    for k in range(KC):
                        if not (ph["which"] == 0 and ph["l"] == 0):
                            wait_unit(pool, ph["hunits"][k])
                        x = h[:, k, 0:w]
                        if k == 0:
                            steps[0] += 1
                            nc.gpsimd.tensor_tensor(ssum[:, 0:w], x, x, ALU.mult).then_inc(s_pool, 1)
                            continue
                        steps[0] += 1
                        nc.gpsimd.tensor_tensor(sqb[:, k % 2, 0:w], x, x, ALU.mult).then_inc(s_pool, 1)
                        pool.wait_ge(s_pool, steps[0])
                        ins = nc.gpsimd.tensor_tensor(ssum[:, 0:w], ssum[:, 0:w], sqb[:, k % 2, 0:w], ALU.add)
                        if k < KC - 1:
                            steps[0] += 1
                            ins.then_inc(s_pool, 1)
                    ins.then_inc(s_sq, 1)
                elif kind == "to_h" and ph["src"] == "ff":
                    for g in range(16):
                        pool.wait_ge(s_xh, ph["x"] + g + 1)
                        pool.wait_ge(*hidden_free(ph, g))
                        c = slice(4 * (g % 2), 4 * (g % 2) + 4)
                        nc.gpsimd.tensor_tensor(a_l[:, c, 0:cols], hid[:, 4 * (g % 8):4 * (g % 8) + 4, 0:cols],
                                                a_h[:, c, 0:cols].bitcast(F32), ALU.subtract).then_inc(s_xl, 1)
                elif kind == "ff1":
                    for i in range(32):
                        wait_unit(pool, ph["steps"][i // 2]["u"] + i % 2)
                        x = hid[:, i, 0:cols]
                        nc.gpsimd.tensor_tensor(x, x, x, ALU.mult).then_inc(s_ff, 1)
                elif kind == "attn":
                    n = len(ph["heads"])

                    def load_bias(i):
                        hh = ph["heads"][i][1]
                        x = ph["head"] + i
                        if i >= 2:
                            pool.wait_ge(s_nm, x - 1)
                        for r in range(4):
                            off = (8 * ph["l"] + hh) * RPB_H * RPB_W + (7 - r) * RPB_W + 15 - (GRID - 1)
                            src = bass.AP(rpb.tensor, rpb.offset + off, [[1, GRID], [RPB_W, 4], [1, GRID]])
                            dst = bias[GRID * (1 - r % 2):GRID * (1 - r % 2) + GRID, hh % 2,
                                       LAT * (r // 2):LAT * (r // 2) + LAT]
                            pool.dma_start(dst.rearrange("p (i c) -> p i c", i=4), src).then_inc(s_biasld, 16)
                            nb[0] += 16

                    def mask_bias(i):
                        hh = ph["heads"][i][1]
                        pool.wait_ge(s_biasld, nb[0])
                        b = bias[:, hh % 2, :]
                        nc.gpsimd.tensor_tensor(b, b, aux[:, A_MASK:A_MASK + 512], ALU.add).then_inc(s_bias, 1)

                    if ph["block"] == 0:
                        pool.wait_ge(s_aux, AUX_LANDED[ph["layer"]])
                        wait_units(pool, u)
                        load_bias(0)
                        mask_bias(0)
                        load_bias(1)
                        mask_bias(1)
                        for i in range(2, 8):
                            load_bias(i)
                            mask_bias(i)
                elif kind == "m_norm":
                    for hh in range(MH):
                        pool.wait_ge(s_mo, hh + 1)
                        nc.gpsimd.tensor_tensor(msq[:, hh, :], hs[:, hh, :], hs[:, hh, :], ALU.mult).then_inc(s_msq, 1)
                    for hh in range(MH):
                        pool.wait_ge(s_hn, hh + 1)
                        nc.gpsimd.tensor_tensor(hs[:, hh, :], hs[:, hh, :], sigo[:, hh, :], ALU.mult
                                                ).then_inc(s_hs, 1)


_SHAPES = None


def shape_constants():
    c = {}
    c["ones"] = np.full((P, P), 1.0 / D, np.float32)
    c["unit"] = np.ones((P, 2), np.float32)
    c["ident"] = np.eye(P, dtype=np.float32)
    rot = np.zeros((P, 2, P), np.float32)
    for base in (0, HD):
        for j in range(HD // 2):
            lo, hi = base + 2 * j, base + 2 * j + 1
            rot[hi, 0, lo] = -1.0
            rot[lo, 0, hi] = 1.0
            lo, hi = base + j, base + j + HD // 2
            rot[hi, 1, lo] = -1.0
            rot[lo, 1, hi] = 1.0
    c["rot"] = rot
    t = np.arange(LAT)
    nf = HD // 4
    inv = np.float32(10000.0) ** (-np.arange(nf, dtype=np.float32) / np.float32(nf))
    row, col = (t // GRID).astype(np.float32), (t % GRID).astype(np.float32)
    ang = np.concatenate([row[:, None] * inv, col[:, None] * inv], axis=-1)
    cs = np.stack([np.cos(ang), np.sin(ang)]).astype(np.float32).transpose(2, 0, 1)
    c["rope1"] = np.tile(np.repeat(cs, 2, axis=0), (2, 1, 1)).reshape(P, 512)
    c["rope2"] = np.tile(cs, (4, 1, 1)).reshape(P, 512)
    start = np.clip(col - 8, 0, GRID - 16)
    ok = (col[None, :] >= start[:, None]) & (col[None, :] < start[:, None] + 16)

    def tiled(m):
        return np.ascontiguousarray(m.astype(np.float32).reshape(2, P, -1).transpose(1, 0, 2)).reshape(P, -1)

    c["na_mask"] = np.ascontiguousarray(tiled(np.where(ok, 0.0, NEG))[::-1])
    c["swa_mask"] = tiled(np.where(np.abs(t[:, None] - t[None, :]) <= 128, 0.0, NEG))
    fwd = np.concatenate([np.where(t[None, :] <= t[:, None], 0.0, NEG), np.zeros((LAT, CTX))], axis=1)
    bwd = np.concatenate([np.where(t[None, :] >= t[:, None], 0.0, NEG), np.zeros((LAT, CTX))], axis=1)
    c["m_mask"] = np.concatenate([tiled(fwd), tiled(bwd)], axis=1)
    win = np.zeros((4, LAT, LAT), np.float32)
    for g, w in enumerate((2, 4, 8, 16)):
        lo, hi = np.clip(t - w // 2, 0, LAT), np.clip(t + w - w // 2, 0, LAT)
        inside = (t[:, None] >= lo[None, :]) & (t[:, None] < hi[None, :])
        win[g] = np.where(inside, 1.0 / (hi - lo)[None, :].astype(np.float32), 0.0) - np.eye(LAT)
    c["pool_win"] = np.ascontiguousarray(win.reshape(4, 2, P, LAT).transpose(2, 1, 0, 3)).reshape(P, 2048)
    return c


def lay_out(inp):
    f = {k: np.asarray(v) for k, v in inp.items()}

    def colv(x):
        return x.reshape(-1, P).T

    parts = []
    for cc, cx in (("c", "c_ctx"), ("c_2", "c_ctx_2")):
        parts.append(np.stack([colv(f[cc].reshape(-1)), colv(f[cx].reshape(-1))], axis=2).reshape(P, -1))
    for name in ("b_mod", "ada_b_2", "norm1_g", "norm_mix_2", "norm2_g", "norm_ffn_2", "final_g", "final_norm_2",
                 "pool_scale", "mlstm_head_norm_2"):
        parts.append(colv(f[name].reshape(-1)))
    out = {"vec": np.concatenate(parts, axis=1)}
    out["xT"] = f["x"][0].T
    out["ctxT0"] = f["ctx"][0].T
    out["ctxT1"] = f["ctx_2"][0].T
    out["sgu_wT"] = f["sgu_w"].transpose(0, 3, 1, 2).reshape(2, P, 512)
    out["sgub"] = f["sgu_b"].transpose(1, 0, 2)
    out["gateb"] = f["mlstm_gate_b_2"][0].T
    bd = np.zeros((2, P, 2, P), np.float32)
    for g in range(4):
        o = HD * (g % 2)
        bd[:, o:o + HD, g // 2, o:o + HD] = f["w_pool"][:, g]
    out["w_pool_bd"] = bd.reshape(2, P, 256)
    for name in ("w_mod", "ada_w_2", "w_in", "w_pool_out", "w_sgu_out", "w_attn_out", "w_o", "w_ff1", "w_ff2",
                 "ffn_w1_2", "ffn_w2_2", "mlstm_w_in_2", "mlstm_w_out_2", "swa_w_in_2", "swa_w_out_2", "na_rpb"):
        out[name] = f[name]
    out["swa_sink_2"] = f["swa_sink_2"].reshape(-1)
    return out


def kernel(**inputs):
    import concourse.bacc as bacc
    from concourse.bass_utils import run_bass_kernel_spmd

    arrays = lay_out(inputs)
    arrays.update(shape_constants())
    nc = bacc.Bacc("TRN2", target_bir_lowering=False, num_devices=1)
    io, sent = {}, {}
    for name, x in arrays.items():
        x = np.ascontiguousarray(x)
        sent[f"in_{name}"] = x
        io[name] = nc.dram_tensor(f"in_{name}", x.shape, F32, kind="ExternalInput").ap()
    io["out"] = nc.dram_tensor("outT", (D, LAT), F32, kind="ExternalOutput").ap()
    build(nc, io)
    r = run_bass_kernel_spmd(nc, [sent], core_ids=[0])
    return np.ascontiguousarray(r.results[0]["outT"].T).reshape(1, LAT, D)
```

```python
from contextlib import ExitStack

import numpy as np
import concourse.bass as bass
from concourse import mybir

F32 = mybir.dt.float32
F32R = mybir.dt.float32r
ALU = mybir.AluOpType
ACT = mybir.ActivationFunctionType
AX_X = mybir.AxisListType.X

P = 128
D = 1024
KC = D // P
LAT = 256
CTX = 256
ALL = LAT + CTX
DFF = 4 * D
EPS = 1e-6
NEG = -1e30
GRID = 64
HD = 64
QSCALE = HD ** -0.5
RPB_H, RPB_W = 15, 31
HALVES = (slice(0, 1024), slice(1024, 2048))
SLOTS = 4
TILE = 2048
MH = 8
MDV = D // MH

V_COND = 0
V_BMOD = V_COND + 2 * KC * 2
V_N1 = V_BMOD + 4 * 48
V_N2 = V_N1 + 4 * KC
V_FIN = V_N2 + 4 * KC
V_PS = V_FIN + 2 * KC
V_HN = V_PS + 4
V_END = V_HN + MH

A_SGU, A_WP = 0, 512
A_ROPE, A_MASK = 768, 1280
A_SB, A_ROT = 1792, 1920
A_MF = 0
A_SIZE = 2048


def make_plan():
    phases = []
    hunits = []
    n = dict(s=0, u=0, x=0, norm=0, sq=0, sq7=0, head=0, mu=0, final=0, y=0)

    def phase(kind, tiles=(), units=0, mods=(), per=1, every=1, skip=0, splits=0, **kw):
        ph = dict(kind=kind, norm=n["norm"], head=n["head"], x=n["x"], y=n["y"], s=n["s"], u=n["u"], mu=n["mu"], **kw)
        mods = list(mods)
        steps = []
        for i, e in enumerate(tiles):
            st = dict(s=n["s"] if e is not None else None, u=n["u"], units=e or 0, mods=[], modu=None)
            n["s"] += e is not None
            n["u"] += e or 0
            if i >= skip and i % every == 0:
                st["mods"], mods = mods[:per], mods[per:]
                if any(half for _, _, half in st["mods"]):
                    st["modu"] = n["mu"]
                    n["mu"] += 1
            steps.append(st)
        assert not mods
        n["u"] += units
        n["x"] += splits
        ph.update(steps=steps, end=n["u"])
        if kind == "to_h":
            hunits[:] = [st["u"] + c for st in steps for c in range(st["units"])]
        if kind == "norm":
            ph["hunits"] = list(hunits)
            ph["squares"] = {0: "first", 5: "switch"}.get(n["norm"], "layer")
            ph["sq"], ph["sq7"] = n["sq"], n["sq7"]
            n["sq"] += ph["squares"] != "switch"
            n["sq7"] += ph["squares"] == "layer"
        phases.append(ph)
        return ph

    def blocks(layer, first, last):
        return [(layer, b, half) for b in range(first, last) for half in range(2)]

    phase("mod0", tiles=(None,) * 4, mods=blocks(0, 0, 4), per=2, layer=0, cols=ALL)
    for layer in range(4):
        block, l = layer // 2, layer % 2
        cols = ALL if l == 0 else LAT
        nt = cols // P
        base = dict(layer=layer, block=block, l=l, cols=cols)
        phase("aux", **base)
        phase("norm", final=False, which=0, width=ALL, splits=KC, **base)
        n["norm"] += 1
        if block == 0:
            phase("b1_in", tiles=(nt, 2, nt, 2, 2, 2, 2, 4, 4),
                  mods=blocks(0, 4, 8) if l == 0 else blocks(2, 0, 2), every=1 + l, skip=1, **base)
            if layer == 1:
                phase("load_ctx", block=1)
            phase("rope", units=8, chunks=8, **base)
            phase("pool_sgu", units=6, **base)
            heads = [("lat", h) for h in range(8)] + ([("ctx", h) for h in range(8)] if l == 0 else [])
            phase("attn", heads=heads, **base)
            n["head"] += len(heads)
            phase("merge", tiles=(6, 2, 2, 2) * 4, splits=KC, mods=blocks(0, 8, 12) if l == 0 else blocks(2, 2, 6),
                  every=2, **base)
            n["y"] += 24
            phase("to_h", tiles=(2,) * 4, src="y", gate=2, name="w_o", **base)
        elif l == 0:
            phase("m_in", tiles=(4,) + (2,) * 4 + (4,) * 4 + (2,) * 4, **base)
            phase("m_gates", units=1, **base)
            phase("m_heads", splits=KC, **base)
            phase("to_h", tiles=(2,) * 4, src="a", gate=2, name="m_out", **base)
        else:
            phase("s_in", tiles=(2,) * 5 + (4,), **base)
            phase("rope", units=10, chunks=10, **base)
            heads = [("lat", h) for h in range(16)]
            phase("attn", heads=heads, **base)
            n["head"] += len(heads)
            phase("to_h", tiles=(2,) * 4, src="attn", gate=2, name="s_out", **base)
        phase("norm", final=False, which=1, width=cols, splits=KC, **base)
        n["norm"] += 1
        in_ff1, in_ff2 = {0: (blocks(1, 0, 8), blocks(1, 8, 12)), 1: (blocks(2, 6, 10), blocks(2, 10, 12)),
                          2: (blocks(3, 0, 8), blocks(3, 8, 12)), 3: ((), ())}[layer]
        phase("ff1", tiles=(2,) * 16, mods=in_ff1, every=1 + l, **base)
        phase("to_h", tiles=((0,) * 7 + (4,)) * 2, splits=16, mods=in_ff2, every=2, src="ff", gate=5, name="ff2", **base)
        if l == 1:
            phase("norm", final=True, which=2, width=LAT, **base)
            n["norm"] += 1
    return phases


def build(nc, io):
    plan = make_plan()
    ctx = ExitStack()
    with ctx:
        def sb(name, shape, dtype=F32):
            return ctx.enter_context(nc.sbuf_tensor(name, shape, dtype))

        def sem(name):
            return ctx.enter_context(nc.semaphore(name))

        ring = sb("ring", [P, SLOTS, TILE])
        w_h = sb("w_h", [P, 2, TILE], F32R)
        w_l = sb("w_l", [P, 2, TILE], F32R)
        h = sb("h", [P, KC, ALL])
        with nc.sbuf_tensor("hid", [P, 32, 512], F32) as hid:
            pass
        m_h = sb("m_h", [P, KC, 512], F32R)
        m_l = sb("m_l", [P, KC, 512], F32R)
        big = sb("big", [P, 16, 512])
        with nc.sbuf_tensor("af", [P, 16, 512], F32) as af:
            pass
        a_h = sb("a_h", [P, KC, 512], F32R)
        a_l = sb("a_l", [P, KC, 512], F32R)
        bias = sb("bias", [P, 2, 512])
        with nc.sbuf_tensor("x0_h", [P, 4, 512], F32R) as x0_h, nc.sbuf_tensor("x0_l", [P, 4, 512], F32R) as x0_l:
            pass
        scr = sb("scr", [P, 2, 2, 512])
        pt = sb("pt", [P, 2, 2, 4, P])
        aux = sb("aux", [P, A_SIZE])
        ident = sb("ident", [P, P])
        unit = sb("unit", [P, 4])
        mean_d = unit[:, 1:2].broadcast_to([P, P])
        mean_head = unit[:, 2:3].broadcast_to([P, P])
        vec = sb("vec", [P, V_END])
        silu = sb("silu", [P, 2, KC, 2])
        mod = sb("mod", [P, 2, 48, 2])
        gain = sb("gain", [P, 2, KC, 2])
        gateb = sb("gateb", [MH, 4])
        sink = sb("sink", [P, 16])
        nmax = sb("nmax", [P, 2, 2])
        rsum = sb("rsum", [P, 2, 2])
        esink = sb("esink", [P, 2, 2])
        rinv = sb("rinv", [P, 2, 2])
        lnst = sb("lnst", [P, 8])
        tm = sb("tm", [P, 2, 4, MH, 2])
        den = sb("den", [P, 2, 2, 2])
        acc = bias
        PS = ctx.enter_context(nc.psum_tensor("PS", [P, 8, 512], F32))

        qT = big[:, 0:4, :]
        kT = big[:, 4:8, :]
        v_tm = big[:, 8:12, :]
        uT = big[:, 12:14, :]
        p_tm = big[:, 14:16, :].rearrange("p a n -> p (a n)").rearrange("p (t n) -> p t n", t=4)
        yT = big[:, 0:8, :]
        br = big[:, 8:14, :]
        gate = big[:, 14:16, :]
        win = hid[:, 4:8, :].rearrange("p a n -> p (a n)").rearrange("p (k g n) -> p k g n", k=2, g=4)
        vs_tm = scr[:, 0, :, :].rearrange("p a n -> p (a n)").rearrange("p (t n) -> p t n", t=4)
        pooled = pt[:, 0, :, :, :].rearrange("p a b n -> p (a b n)").rearrange("p (c n) -> p c n", c=2)
        mq = big[:, 0:4, :]
        mk = big[:, 4:8, :]
        mv = big[:, 8:16, :].rearrange("p a n -> p (a n)").rearrange("p (t n) -> p t n", t=4)
        sigo = hid[:, 0:8, :]
        hs = hid[:, 8:16, :]
        G = scr[0:MH, :, :, :].rearrange("p a b n -> p (a b) n")
        pt_rows = pt[0:MH, :, :, :, :].rearrange("p a b c n -> p (a b) (c n)")
        Bc = pt_rows[:, 0:2, :]
        one_row = pt_rows[:, 2, :]
        grow = bias[0:MH, :, :]
        msq = af[:, 8:16, :]
        sq_ = big[:, 0:8, 0:LAT]
        sk = big[:, 8:10, :]
        sv = big[:, 10:12, :].rearrange("p a n -> p (a n)").rearrange("p (t n) -> p t n", t=4)
        sqb = scr[:, 0, :, :]
        ssum = pt[:, 0, 0, :, :].rearrange("p b n -> p (b n)")
        nrm = scr[:, 1, :, :]
        rs = pt[:, 1, 0, :, :].rearrange("p b n -> p (b n)")

        s_const = sem("const_loaded")
        s_mcsum = sem("mod_block_summed")
        s_mcol = sem("mod_columns_ready")
        s_vec = sem("vectors_loaded")
        s_slot = [sem(f"weights_loaded_{i}") for i in range(SLOTS)]
        s_inner = sem("tile_done_inside_unit")
        s_wh = sem("weights_rounded")
        s_wl = sem("weights_split")
        s_xh = sem("input_rounded")
        s_xl = sem("input_split")
        s_mtile = sem("mod_tile_used")
        s_mtpe = sem("mod_tile_multiplied")
        s_fin = sem("final_norm_written")
        s_ctxld = sem("context_loaded")
        s_aux = sem("tables_loaded")
        s_unit = sem("unit_done")
        s_free = [sem(f"bank_evacuated_{i}") for i in range(4)]
        s_silu = sem("silu_ready")
        s_silu_a = sem("silu_sigmoid")
        s_sq = sem("square_sum_ready")
        s_sqm = sem("mean_square_done")
        s_rstd = sem("inverse_deviation_ready")
        s_sq7 = sem("last_square_ready")
        s_sqctx = sem("context_square_sum_ready")
        s_sqlat = sem("latent_squares_ready")
        s_sqp = sem("latent_squares_summed")
        s_nrm = sem("normed_ready")
        s_dve = sem("dve_step")
        s_act = sem("act_step")
        s_pool = sem("pool_step")
        s_ff = sem("hidden_ready")
        s_bias = sem("bias_ready")
        s_biasld = [sem(f"bias_loaded_{i}") for i in range(2)]
        s_sc = sem("scores_done")
        s_nm = sem("max_ready")
        s_exp = sem("exp_done")
        s_prob = sem("probs_ready")
        s_tr = sem("transposed")
        s_pta = sem("probsT_by_act")
        s_ptd = sem("probsT_by_dve")
        s_pv = sem("pv_done")
        s_o = sem("attn_out_ready")
        s_y = sem("gated_branch_added")
        s_sgu = sem("sgu_normed")
        s_ga = sem("gate_exp")
        s_gd = sem("gate_rows_ready")
        s_lnv = sem("sgu_variance_ready")
        s_lns = sem("sgu_inverse_deviation_ready")
        s_gr = sem("guard_ready")
        s_rows = sem("m_decay_rows_ready")
        s_qk = sem("m_qk_done")
        s_D = sem("m_decay_args")
        s_A = sem("m_decay_ready")
        s_W = sem("m_weighted")
        s_rc = sem("m_denominator_ready")
        s_scaled = sem("m_forward_scaled")
        s_P = sem("m_probs_ready")
        s_mt = sem("m_transposed")
        s_mpt = sem("m_probsT_ready")
        s_mpv = sem("m_pv_done")
        s_mo = sem("m_out_ready")
        s_msq = sem("m_squares")
        s_mms = sem("m_mean_square")
        s_mroot = sem("m_inverse_deviations_ready")
        s_mvar = sem("m_variance")
        s_hn = sem("m_normed")
        s_hs = sem("m_gated")
        s_out = sem("out_stored")

        def rows(w):
            return w.rearrange("(k p) n -> p k n", p=P)

        split_src = []

        def view8(t):
            return t.rearrange("p (k n) -> p k n", k=8)

        def view4(t):
            return t.rearrange("p (k n) -> p k n", k=4)

        def whole(w, c0):
            split_src.append([(lambda t: view8(t), rows(w[:, c0:c0 + 256]))])

        for ph in plan:
            if not ph["steps"] or ph["kind"] == "mod0":
                continue
            l, b, kind = ph["l"], ph["block"], ph["kind"]
            if kind == "b1_in":
                for i in range(9):
                    whole(io["w_in"][l], 256 * i)
            elif kind == "merge":
                for i in range(4):
                    c = slice(256 * i, 256 * i + 256)
                    split_src.append([(lambda t: view8(t)[:, 0:2, :], rows(io["w_pool_out"][l][:, c])),
                                      (lambda t: view8(t)[:, 2:4, :], rows(io["w_sgu_out"][l][:, c])),
                                      (lambda t: view8(t)[:, 4:8, :], rows(io["w_attn_out"][l][:, c]))])
                    for g in range(3):
                        whole(io["w_in"][l], 2304 + D * g + 256 * i)
            elif kind == "m_in":
                split_src.append([(lambda t, r=r: view8(t)[:, :, 32 * r:32 * r + 32],
                                   rows(io["mlstm_w_in_2"][0][:, 3072:3104])) for r in range(8)])
                for i in range(12):
                    whole(io["mlstm_w_in_2"][0], 256 * i)
            elif kind == "s_in":
                w = io["swa_w_in_2"][0]
                for i in range(2):
                    for jj in range(2):
                        split_src.append([
                            (lambda t, d=P * j + HD * half: view8(t)[:, :, d:d + HD],
                             rows(w[:, 512 * i + 256 * half + HD * (2 * jj + j):
                                    512 * i + 256 * half + HD * (2 * jj + j) + HD]))
                            for half in range(2) for j in range(2)])
                for i in range(2):
                    whole(w, 1024 + 256 * i)
            elif kind == "ff1":
                for i in range(16):
                    whole(io["w_ff1" if b == 0 else "ffn_w1_2"][l], 256 * i)
            elif ph["name"] == "ff2":
                w = io["w_ff2" if b == 0 else "ffn_w2_2"][l]
                for i in range(2):
                    for kb in range(8):
                        split_src.append([(lambda t: view4(t), rows(w[512 * kb:512 * kb + 512, 512 * i:512 * i + 512]))])
            elif ph["name"] == "s_out":
                w = io["swa_w_out_2"][0].rearrange("(g s j d) n -> s d g j n", g=2, s=2, j=4, d=HD)
                for i in range(4):
                    split_src.append([(lambda t, half=half, g=g: view8(t)[HD * half:HD * half + HD, 4 * g:4 * g + 4, :],
                                       w[half, :, g, :, 256 * i:256 * i + 256])
                                      for half in range(2) for g in range(2)])
            else:
                for i in range(4):
                    whole(io["w_o"][l] if ph["name"] == "w_o" else io["mlstm_w_out_2"][0], 256 * i)

        stream, split_raw, mod_raw = [], {}, {}

        by_pe = [(0, b, half) for b in (0, 2) for half in range(2)]

        def push_mods(mods):
            for key in mods:
                layer, b, half = key
                w = io["w_mod" if layer < 2 else "ada_w_2"][layer % 2]
                mod_raw[key] = len(stream)
                if key not in by_pe:
                    what, count = "mod", 1 + sum(x[0] == "mod" for x in stream)
                elif half:
                    what, count = "mod_pe_end", b + 1
                else:
                    what, count = "mod_pe", b // 2 + 1
                stream.append((what, count,
                               [(lambda t: view4(t), rows(w[512 * half:512 * half + 512, 512 * b:512 * b + 512]))]))

        def push_split(s):
            if s < len(split_src):
                split_raw[s] = len(stream)
                stream.append(("split", 2 * s + 2, split_src[s]))

        push_mods([(0, b + up, half) for b in (0, 2) for half in range(2) for up in (1, 0)])
        for ph in plan:
            for st in ph["steps"]:
                if ph["kind"] != "mod0":
                    push_mods(st["mods"])
                if st["s"] is not None:
                    push_split(st["s"] + 1)
            if ph["kind"] == "mod0":
                push_split(0)
        landed, total = [], [0] * SLOTS
        for t, (_, _, parts) in enumerate(stream):
            total[t % SLOTS] += 16 * len(parts)
            landed.append(total[t % SLOTS])

        release, inner = [], 0
        for ph in plan:
            for st in ph["steps"]:
                if st["s"] is not None:
                    inner += not st["units"]
                    release.append((s_unit, st["u"] + st["units"]) if st["units"] else (s_inner, inner))
        NSPLIT = len(release)
        assert NSPLIT == len(split_src)

        def raw_slot(eng, t):
            eng.wait_ge(s_slot[t % SLOTS], landed[t])
            return ring[:, t % SLOTS, :]

        mod_count = {key: stream[t][1] for key, t in mod_raw.items()}

        def wait_units(eng, n):
            for b in range(4):
                if (n - b + 3) // 4 > 0:
                    eng.wait_ge(s_free[b], (n - b + 3) // 4)

        def wait_unit(eng, u):
            eng.wait_ge(s_free[u % 4], u // 4 + 1)

        def segs(width):
            return [(0, slice(0, LAT))] + ([(1, slice(LAT, ALL))] if width == ALL else [])

        def rope_chunk(ph, c):
            if ph["block"] == 0:
                return (qT if c < 4 else kT)[:, c % 4, 0:LAT]
            return sq_[:, c, :] if c < 8 else sk[:, c - 8, 0:LAT]

        def head_parts(ph, i):
            kind, hh = ph["heads"][i]
            if ph["block"] == 0:
                base, ch = HD * (hh % 2), hh // 2
                if kind == "lat":
                    qs, ks, vs, nk = slice(0, LAT), slice(0, ALL), v_tm[:, 0:4, HD * hh:HD * hh + HD], ALL
                else:
                    qs, ks, vs, nk = slice(LAT, ALL), slice(LAT, ALL), v_tm[:, 2:4, HD * hh:HD * hh + HD], CTX
                out = [x[base:base + HD, 4 + ch, qs] for x in (m_h, m_l)]
                return qT[base:base + HD, ch, qs], kT[base:base + HD, ch, ks], vs, base, nk, out
            kv = hh // 4
            base = HD * (kv % 2)
            ch = 4 * (hh // 8) + hh % 4
            out = [x[base:base + HD, ch, 0:LAT] for x in (m_h, m_l)]
            return sq_[base:base + HD, ch, :], sk[base:base + HD, kv // 2, :], sv[:, :, HD * kv:HD * kv + HD], base, ALL, out

        def nbias(ph, i):
            return 8 * ph["l"] + i

        def hidden_pair(g):
            if g == 0:
                return x0_h[:, :, :], x0_l[:, :, :]
            return tuple(x[:, 4 * (g % 2):4 * (g % 2) + 4, :] for x in (a_h, a_l))

        def hidden_free(ph, g):
            return release[ph["steps"][max(g - 2, 0)]["s"] - (1 if g < 3 else 0)]

        def mbuf(b):
            return (scr[:, 0, :, :], scr[:, 1, :, :], af[:, 6:8, :])[b % 3]

        mod_unit_of = {key[:2]: st["modu"] for ph in plan for st in ph["steps"] for key in st["mods"] if key[2]}
        mod_before = {}
        before = None
        for ph in plan:
            for st in ph["steps"]:
                for key in st["mods"]:
                    if key[2] == 0 and before is not None:
                        mod_before[key] = before
                if st["modu"] is not None and st["mods"][-1] not in by_pe:
                    before = st["modu"]

        def mod_vectors(key):
            layer, b, _ = key
            return 2 if layer % 2 == 0 or b < 4 else 1

        rpb = io["na_rpb"]
        block = ctx.enter_context(nc.Block())

        @block.sync
        def _(sp):
            for dst, src in ((vec[:, :], io["vec"]), (unit[:, :], io["unit"])):
                sp.dma_start(dst, src).then_inc(s_vec, 16)
            sent = [0]

            def send(upto):
                for t in range(sent[0], upto):
                    if t >= SLOTS:
                        what, count, _ = stream[t - SLOTS]
                        sp.wait_ge(dict(split=s_wl, mod=s_mtile, mod_pe=s_mtpe, mod_pe_end=s_mcsum)[what], count)
                    for put, src in stream[t][2]:
                        sp.dma_start(put(ring[:, t % SLOTS, :]), src).then_inc(s_slot[t % SLOTS], 16)
                sent[0] = max(sent[0], upto)

            def load_bias(ph, i):
                hh = ph["heads"][i][1]
                for r in range(4):
                    off = (8 * ph["l"] + hh) * RPB_H * RPB_W + (7 - r) * RPB_W + 15 - (GRID - 1)
                    src = bass.AP(rpb.tensor, rpb.offset + off, [[1, GRID], [RPB_W, 4], [1, GRID]])
                    dst = bias[GRID * (1 - r % 2):GRID * (1 - r % 2) + GRID, hh % 2,
                               LAT * (r // 2):LAT * (r // 2) + LAT]
                    sp.dma_start(dst.rearrange("p (i c) -> p i c", i=4), src).then_inc(s_biasld[i % 2], 16)

            send(SLOTS)
            for dst, src in ((ident[:, :], io["ident"]), 
                             (gateb[:, :], io["gateb"]),
                             (sink[:, :], io["swa_sink_2"].partition_broadcast(P)),
                             (h[:, :, 0:LAT], io["xT"].rearrange("(k p) n -> p k n", p=P))):
                sp.dma_start(dst, src).then_inc(s_const, 16)

            def load_ctx(b):
                sp.dma_start(h[:, :, LAT:ALL], io[f"ctxT{b}"].rearrange("(k p) n -> p k n", p=P)).then_inc(s_ctxld, 16)

            load_ctx(0)
            for ph in plan:
                kind = ph["kind"]
                if kind == "load_ctx":
                    sp.wait_ge(s_xl, ph["x"])
                    load_ctx(1)
                elif kind == "aux":
                    if ph["layer"] > 0:
                        send(split_raw[ph["s"] + 1] + 1)
                        wait_units(sp, ph["u"])
                    if ph["block"] == 0:
                        l = ph["l"]
                        parts = ((A_SGU, 512, io["sgu_wT"][l]), (A_WP, 256, io["w_pool_bd"][l]),
                                 (A_ROPE, 512, io["rope1"]), (A_MASK, 512, io["na_mask"]),
                                 (A_ROT, P, io["rot"][:, 0, :]))
                        sp.dma_start(aux[0:4, A_SB:A_SB + P], io["sgub"][:, l, :]).then_inc(s_aux, 16)
                        sp.dma_start(win, io["pool_win"].rearrange("p (k g n) -> p k g n", k=2, g=4)).then_inc(s_aux, 16)
                    elif ph["l"] == 0:
                        parts = ((A_MF, 2048, io["m_mask"]),)
                    else:
                        parts = ((A_ROPE, 512, io["rope2"]), (A_MASK, 512, io["swa_mask"]),
                                 (A_ROT, P, io["rot"][:, 1, :]))
                    for off, n, src in parts:
                        sp.dma_start(aux[:, off:off + n], src).then_inc(s_aux, 16)
                elif kind == "attn" and ph["block"] == 0:
                    wait_units(sp, ph["u"])
                    for i in range(8):
                        if i >= 2:
                            sp.wait_ge(s_nm, ph["head"] + i - 1)
                        load_bias(ph, i)
                for st in ph["steps"]:
                    for key in st["mods"]:
                        send(mod_raw[key] + 1)
                    if st["s"] is not None and st["s"] + 1 in split_raw:
                        send(split_raw[st["s"] + 1] + 1)
                if kind == "mod0":
                    send(split_raw[0] + 1)
            sp.wait_ge(s_fin, 2 * KC)
            sp.dma_start(io["out"].rearrange("(k p) n -> p k n", p=P), h[:, :, 0:LAT]).then_inc(s_out, 16)
            sp.wait_ge(s_out, 16)

        AUX_LANDED = [112, 224, 240, 288]
        CONST = 64

        @block.tensor
        def _(pe):
            pe.wait_ge(s_vec, 32)

            def tile(st):
                pe.wait_ge(s_wl, 2 * st["s"] + 1)
                return w_h[:, st["s"] % 2, :], w_l[:, st["s"] % 2, :]

            def second_half(st):
                pe.wait_ge(s_wl, 2 * st["s"] + 2)

            def bank(u):
                if u >= 4:
                    pe.wait_ge(s_free[u % 4], u // 4)
                return PS[:, u % 4, :]

            def product(out, stat, mov, start, stop):
                kw = dict(skip_group_check=True)
                nc.tensor.matmul(out, stat[0], mov[0], start=start, stop=False, **kw)
                nc.tensor.matmul(out, stat[0], mov[1], start=False, stop=False, **kw)
                return nc.tensor.matmul(out, stat[1], mov[0], start=False, stop=stop, **kw)

            def fm(st, u, w, c, src, n, ks=range(KC), wait_input=None):
                out = bank(u)[:, 0:n]
                for k in ks:
                    if k == KC // 2:
                        second_half(st)
                    if wait_input is not None:
                        pe.wait_ge(s_xl, wait_input + k + 1)
                    mm = product(out, [view8(x)[:, k, c] for x in w], [x[:, k, 0:n] for x in src],
                                 k == ks[0], k == ks[-1])
                mm.then_inc(s_unit, 1)

            def tokm(st, u, w, tt):
                out = bank(u)[:, 0:256]
                for k in range(KC):
                    if k == KC // 2:
                        second_half(st)
                    mm = product(out, [x[:, k, P * tt:P * tt + P] for x in (a_h, a_l)],
                                 [view8(x)[:, k, :] for x in w], k == 0, k == KC - 1)
                mm.then_inc(s_unit, 1)

            def first_tile(st, need, token_major=False, pitch=P):
                w, n_units = tile(st), st["units"]
                outs = [bank(st["u"] + j) for j in range(n_units)]
                for k in range(KC):
                    pe.wait_ge(s_xl, need + k + 1)
                    if k == KC // 2:
                        second_half(st)
                    for j in range(n_units):
                        if token_major:
                            mm = product(outs[j][:, 0:256], [x[:, k, P * j:P * j + P] for x in (a_h, a_l)],
                                         [view8(x)[:, k, :] for x in w], k == 0, k == KC - 1)
                        else:
                            mm = product(outs[j][:, 0:cols], [view8(x)[:, k, pitch * j:pitch * j + P] for x in w],
                                         [x[:, k, 0:cols] for x in (a_h, a_l)], k == 0, k == KC - 1)
                        if k == KC - 1:
                            mm.then_inc(s_unit, 1)
                mod_unit(st)

            def mod_block(st):
                if st["modu"]:
                    pe.wait_ge(s_mcol, st["modu"] - 1)
                for key in st["mods"]:
                    w, half = view4(raw_slot(pe, mod_raw[key])), key[2]
                    for c in range(4):
                        for k in range(4):
                            mm = nc.tensor.matmul(PS[:, c, 0:2], w[:, k, P * c:P * c + P], silu[:, 0, 4 * half + k, :],
                                                  start=(half == 0 and k == 0), stop=(half == 1 and k == 3),
                                                  skip_group_check=True)
                    mm.then_inc(s_mcsum if half else s_mtpe, 1)

            def mod_unit(st):
                if st["modu"] is None:
                    return
                pe.wait_ge(s_mtile, mod_count[st["mods"][-1]])
                if st["modu"]:
                    pe.wait_ge(s_mcol, st["modu"])
                out = PS[:, 5, 0:8].rearrange("p (c s) -> p c s", s=2)
                for s in range(mod_vectors(st["mods"][-1])):
                    for c in range(4):
                        mm = nc.tensor.matmul(out[:, c, s:s + 1], acc[:, s, P * c:P * c + P], unit[:, 0:1],
                                              start=True, stop=True)
                mm.then_inc(s_mcsum, 1)

            PA, PM = (a_h, a_l), (m_h, m_l)
            for ph in plan:
                kind, u = ph["kind"], ph["u"]
                cols = ph.get("cols")
                if kind == "mod0":
                    pe.wait_ge(s_silu, 2)
                    for st in ph["steps"]:
                        if st["mods"][-1] in by_pe:
                            mod_block(st)
                        else:
                            mod_unit(st)
                    pe.wait_ge(s_const, CONST)
                elif kind == "norm":
                    w = ph["width"]
                    if ph["squares"] == "first":
                        pe.wait_ge(s_sq, ph["sq"] + 1)
                        nc.tensor.matmul(PS[:, 4, 0:w], mean_d, ssum[:, 0:w], start=True, stop=True).then_inc(s_sqm, 1)
                    elif ph["squares"] == "layer":
                        pe.wait_ge(s_sq, ph["sq"] + 1)
                        nc.tensor.matmul(PS[:, 4, 0:w], mean_d, ssum[:, 0:w], start=True, stop=False)
                        pe.wait_ge(s_sq7, ph["sq7"] + 1)
                        nc.tensor.matmul(PS[:, 4, 0:w], mean_d, nrm[:, 0, 0:w], start=False, stop=True
                                         ).then_inc(s_sqm, 1)
                    else:
                        pe.wait_ge(s_sqctx, 1)
                        pe.wait_ge(s_sqlat, 1)
                        nc.tensor.matmul(PS[:, 4, LAT:ALL], mean_d, ssum[:, LAT:ALL], start=True, stop=True)
                        for k in range(KC):
                            pe.wait_ge(s_sqlat, k + 1)
                            nc.tensor.matmul(PS[:, 4, 0:LAT], mean_d, sqb[:, k % 2, 0:LAT], start=(k == 0),
                                             stop=(k == KC - 1)).then_inc(s_sqp if k < KC - 1 else s_sqm, 1)
                elif kind == "b1_in":
                    first_tile(ph["steps"][0], ph["x"] - KC, token_major=True)
                    for i, st in enumerate(ph["steps"][1:], 1):
                        w, u = tile(st), st["u"]
                        for j in range(st["units"]):
                            if i in (2, 7, 8):
                                tokm(st, u + j, w, j)
                            else:
                                fm(st, u + j, w, slice(P * j, P * j + P), PA, ALL if i >= 5 else cols)
                        mod_unit(st)
                elif kind == "rope":
                    wait_units(pe, u)
                    pe.wait_ge(s_aux, AUX_LANDED[ph["layer"]])
                    for c in range(ph["chunks"]):
                        src = rope_chunk(ph, c)
                        nc.tensor.matmul(bank(u + c)[:, 0:LAT], aux[:, A_ROT:A_ROT + P], src,
                                         start=True, stop=True).then_inc(s_unit, 1)
                elif kind == "pool_sgu":
                    nseg = cols // LAT
                    pe.wait_ge(s_aux, AUX_LANDED[ph["layer"]])
                    for pair in range(2):
                        out = bank(u)
                        for s in range(nseg):
                            for half in range(2):
                                g = 2 * pair + half
                                for k in range(2):
                                    mm = nc.tensor.matmul(
                                        out[HD * half:HD * half + HD, LAT * s:LAT * s + LAT],
                                        p_tm[:, 2 * s + k, HD * g:HD * g + HD], win[:, k, g, :],
                                        start=(k == 0), stop=(k == 1))
                        mm.then_inc(s_unit, 1)
                        u += 1
                    wp = aux[:, A_WP:A_WP + 256].rearrange("p (c n) -> p c n", c=2)
                    for pair in range(2):
                        wait_unit(pe, u - 2)
                        nc.tensor.matmul(bank(u)[:, 0:cols], wp[:, pair, :], pooled[:, pair, 0:cols],
                                         start=True, stop=True).then_inc(s_unit, 1)
                        u += 1
                    pe.wait_ge(s_sgu, ph["layer"] + 1)
                    sw = aux[:, A_SGU:A_SGU + 512].rearrange("p (g n) -> p g n", g=4)
                    for pair in range(2):
                        out = bank(u)
                        for tt in range(cols // P):
                            for half in range(2):
                                g = 2 * pair + half
                                o = out[HD * half:HD * half + HD, P * tt:P * tt + P]
                                nc.tensor.matmul(o, vs_tm[:, tt, HD * g:HD * g + HD], sw[:, g, :],
                                                 start=True, stop=False)
                                mm = nc.tensor.matmul(o, ident[0:4, g:g + 1].broadcast_to([4, HD]), aux[0:4, A_SB:A_SB + P],
                                                      start=False, stop=True)
                        mm.then_inc(s_unit, 1)
                        u += 1
                elif kind == "ff1":
                    first_tile(ph["steps"][0], ph["x"] - KC)
                    for st in ph["steps"][1:]:
                        w = tile(st)
                        for c in range(2):
                            fm(st, st["u"] + c, w, slice(P * c, P * c + P), PA, cols)
                        mod_unit(st)
                elif kind == "attn":
                    wait_units(pe, u)
                    n = len(ph["heads"])

                    def scores(i):
                        x = ph["head"] + i
                        if x >= 2:
                            pe.wait_ge(s_exp, x - 1)
                        q, k, _, _, nk, _ = head_parts(ph, i)
                        for qt in range(2):
                            mm = nc.tensor.matmul(PS[:, 2 * (x % 2) + qt, 0:nk], q[:, P * qt:P * qt + P], k,
                                                  start=True, stop=True)
                        mm.then_inc(s_sc, 1)

                    def turn(i):
                        x = ph["head"] + i
                        nk = head_parts(ph, i)[4]
                        pe.wait_ge(s_prob, x + 1)
                        if x >= 1:
                            pe.wait_ge(s_pta, x)
                            pe.wait_ge(s_ptd, x)
                        for qt in range(2):
                            for k in range(nk // P):
                                mm = nc.tensor.transpose(PS[:, 4 + qt, P * k:P * k + P],
                                                         scr[:, x % 2, qt, P * k:P * k + P], ident[:, :])
                        mm.then_inc(s_tr, 1)

                    def values(i):
                        x = ph["head"] + i
                        _, _, v, out_base, nk, _ = head_parts(ph, i)
                        pe.wait_ge(s_pta, x + 1)
                        pe.wait_ge(s_ptd, x + 1)
                        if x >= 2:
                            pe.wait_ge(s_o, x - 1)
                        o = PS[out_base:out_base + HD, 6 + x % 2, 0:LAT]
                        for k in range(nk // P):
                            mm = nc.tensor.matmul(o, v[:, k, :], pt[:, x % 2, :, k, :],
                                                  start=(k == 0), stop=(k == nk // P - 1))
                        mm.then_inc(s_pv, 1)

                    scores(0)
                    scores(1)
                    for i in range(n + 1):
                        if i + 2 < n:
                            scores(i + 2)
                        if i < n:
                            turn(i)
                        if i >= 1:
                            values(i - 1)
                elif kind == "merge":
                    pe.wait_ge(s_o, ph["head"])
                    for i, st in enumerate(ph["steps"]):
                        w, u = tile(st), st["u"]
                        if i % 4 == 0:
                            for c in range(2):
                                for b, ks in enumerate((range(0, 2), range(2, 4), range(4, 8))):
                                    fm(st, u + 3 * c + b, w, slice(P * c, P * c + P), PM, cols, ks)
                        else:
                            for c in range(2):
                                fm(st, u + c, w, slice(P * c, P * c + P), PA, cols)
                        mod_unit(st)
                elif kind == "to_h" and ph["src"] != "ff":
                    if ph["src"] == "attn":
                        pe.wait_ge(s_o, ph["head"])
                    for i, st in enumerate(ph["steps"]):
                        w = tile(st)
                        for c in range(2):
                            fm(st, st["u"] + c, w, slice(P * c, P * c + P), PA if ph["src"] == "a" else PM, cols,
                               wait_input=ph["x"] - KC if i == 0 and ph["src"] != "attn" else None)
                        mod_unit(st)
                elif kind == "to_h":
                    for i in range(2):
                        u = ph["steps"][8 * i + 7]["u"]
                        for kb in range(8):
                            st = ph["steps"][8 * i + kb]
                            w = tile(st)
                            g = 8 * i + kb
                            pe.wait_ge(s_xl, ph["x"] + g + 1)
                            for c in range(4):
                                out = (bank(u + c) if kb == 0 else PS[:, (u + c) % 4, :])[:, 0:cols]
                                for k in range(4):
                                    if k == 2:
                                        second_half(st)
                                    mm = product(out, [view4(x)[:, k, P * c:P * c + P] for x in w],
                                                 [x[:, k, 0:cols] for x in hidden_pair(g)], kb == 0 and k == 0,
                                                 kb == 7 and k == 3)
                                if kb == 7:
                                    mm.then_inc(s_unit, 1)
                            if kb < 7:
                                mm.then_inc(s_inner, 1)
                            mod_unit(st)
                elif kind == "m_in":
                    first_tile(ph["steps"][0], ph["x"] - KC, False, MH)
                    for i, st in enumerate(ph["steps"][1:], 1):
                        w, u = tile(st), st["u"]
                        for j in range(st["units"]):
                            if 5 <= i < 9:
                                tokm(st, u + j, w, j)
                            else:
                                fm(st, u + j, w, slice(P * j, P * j + P), PA, ALL)
                        mod_unit(st)
                elif kind == "m_gates":
                    pe.wait_ge(s_gr, 1)
                    out = bank(u).rearrange("p (w t g n) -> p w t g n", w=2, t=4, g=2, n=32)
                    for what in range(2):
                        for d in range(2):
                            src = G[:, 2 * d + 1, :] if what == 0 else Bc[:, d, :]
                            for tt in range(4):
                                mm = nc.tensor.transpose(out[:, what, tt, d, 0:MH], src[:, P * tt:P * tt + P],
                                                         ident[0:MH, 0:MH])
                    mm.then_inc(s_unit, 1)
                elif kind == "m_heads":
                    wait_units(pe, u)
                    pe.wait_ge(s_aux, AUX_LANDED[2])

                    def decay_rows(hh):
                        if hh:
                            pe.wait_ge(s_D, 4 * hh)
                        for d in range(2):
                            mm = nc.tensor.matmul(PS[:, d, :], ident[0:MH, hh:hh + 1].broadcast_to([MH, P]),
                                                  grow[:, d, :], start=True, stop=True)
                        mm.then_inc(s_rows, 1)

                    def qk(b):
                        hh, qt = b // 4, b % 4
                        if b >= 2:
                            pe.wait_ge(s_W, b - 1)
                        c0 = 0 if qt < 2 else LAT
                        base = HD * (hh % 2)
                        nc.tensor.matmul(PS[:, 2 + b % 2, 0:ALL - c0],
                                         mq[base:base + HD, hh // 2, P * qt:P * qt + P],
                                         mk[base:base + HD, hh // 2, c0:ALL], start=True, stop=True).then_inc(s_qk, 1)

                    def turn(b):
                        k0 = 0 if b % 4 < 2 else 2
                        pe.wait_ge(s_P, b + 1)
                        if b >= 2:
                            pe.wait_ge(s_mpt, b - 1)
                        for k in range(k0, 4):
                            mm = nc.tensor.transpose(PS[:, 4 + b % 2, P * (k - k0):P * (k - k0) + P],
                                                     mbuf(b)[:, 0, P * (k - k0):P * (k - k0) + P], ident[:, :])
                        mm.then_inc(s_mt, 1)

                    def values(b):
                        hh, qt = b // 4, b % 4
                        k0 = 0 if qt < 2 else 2
                        pe.wait_ge(s_mpt, b + 1)
                        if qt == 0 and hh >= 2:
                            pe.wait_ge(s_mvar, hh - 1)
                        for k in range(k0, 4):
                            mm = nc.tensor.matmul(PS[:, 6 + hh % 2, P * qt:P * qt + P], mv[:, k, P * hh:P * hh + P],
                                                  pt[:, b % 2, 0, k - k0, :], start=(k == k0), stop=(k == 3))
                        mm.then_inc(s_mpv, 1)

                    def mean_square(hh):
                        pe.wait_ge(s_msq, hh + 1)
                        nc.tensor.matmul(PS[:, 6 + hh % 2, :], mean_head, msq[:, hh, :], start=True, stop=True
                                         ).then_inc(s_mms, 1)

                    n = 4 * MH
                    decay_rows(0)
                    qk(0)
                    qk(1)
                    for b in range(n + 1):
                        if b + 2 < n:
                            qk(b + 2)
                        if b < n:
                            turn(b)
                        if b % 4 == 1 and b + 3 < n:
                            decay_rows((b + 3) // 4)
                        if b >= 1:
                            values(b - 1)
                        if b % 4 == 3 and b > 4:
                            mean_square(b // 4 - 1)
                    mean_square(MH - 1)
                elif kind == "s_in":
                    first_tile(ph["steps"][0], ph["x"] - KC)
                    for i, st in enumerate(ph["steps"][1:], 1):
                        w, u = tile(st), st["u"]
                        for j in range(st["units"]):
                            if i == 5:
                                tokm(st, u + j, w, j)
                            else:
                                fm(st, u + j, w, slice(P * j, P * j + P), PA, ALL if i == 4 else LAT)
                        mod_unit(st)

        @block.scalar
        def _(act):
            act.wait_ge(s_vec, 32)
            steps = [0]

            def step(ins):
                steps[0] += 1
                ins.then_inc(s_act, 1)
                act.wait_ge(s_act, steps[0])

            def copy_unit(u, out, src_cols, func=ACT.Copy, m=P, **kw):
                act.wait_ge(s_unit, u + 1)
                nc.scalar.activation(out, PS[0:m, u % 4, src_cols], func, **kw).then_inc(s_free[u % 4], 1)

            def inverse_root(out, x):
                step(nc.scalar.activation(out, x, ACT.Ln, bias=unit[:, 3:4]))
                return nc.scalar.activation(out, out, ACT.Exp, scale=-0.5)

            rounded = [0]

            def round_w(n):
                if n >= NSPLIT or n < rounded[0]:
                    return
                rounded[0] = n + 1
                raw = raw_slot(act, split_raw[n])
                if n >= 2:
                    act.wait_ge(*release[n - 2])
                for c in HALVES:
                    nc.scalar.activation(w_h[:, n % 2, c], raw[:, c], ACT.Copy).then_inc(s_wh, 1)

            def steps_of(ph):
                for i, st in enumerate(ph["steps"]):
                    if st["s"] is not None:
                        round_w(st["s"] + 1)
                    yield i, st, st["u"]

            def round_hidden(ph, g):
                if g >= 16:
                    return
                cols = ph["cols"]
                act.wait_ge(s_ff, 32 * ph["layer"] + 4 * (g % 8) + 4)
                if g:
                    act.wait_ge(*hidden_free(ph, g))
                nc.scalar.activation(hidden_pair(g)[0][:, :, 0:cols],
                                     hid[:, 4 * (g % 8):4 * (g % 8) + 4, 0:cols], ACT.Copy).then_inc(s_xh, 1)

            for b in range(2):
                c0 = V_COND + b * 2 * KC
                nc.scalar.activation(silu[:, b, :, :].rearrange("p k n -> p (k n)"),
                                     vec[:, c0:c0 + 2 * KC], ACT.Sigmoid).then_inc(s_silu_a, 1)
            for ph in plan:
                kind, u = ph["kind"], ph["u"]
                cols = ph.get("cols")
                if kind == "mod0":
                    round_w(0)
                    act.wait_ge(s_const, CONST)
                elif kind == "norm":
                    n0 = ph["norm"]
                    w = ph["width"]
                    if not ph["final"]:
                        round_w(ph["s"] + 1)
                    act.wait_ge(s_sqm, n0 + 1)
                    inverse_root(rs[:, 0:w], PS[:, 4, 0:w]).then_inc(s_rstd, 1)
                    which, b = ph["which"], ph["block"]
                    if not ph["final"]:
                        act.wait_ge(s_mcol, mod_unit_of[ph["layer"], 6 * which + 3] + 1)
                    for k in range(KC):
                        act.wait_ge(s_nrm, KC * n0 + k + 1)
                        if ph["final"]:
                            nc.scalar.activation(h[:, k, 0:LAT], nrm[:, k % 2, 0:LAT], ACT.Copy,
                                                 scale=vec[:, V_FIN + KC * b + k:V_FIN + KC * b + k + 1]
                                                 ).then_inc(s_fin, 1)
                            continue
                        for s, c in segs(ph["width"]):
                            ins = nc.scalar.activation(a_h[:, k, c], nrm[:, k % 2, c], ACT.Identity,
                                                       bias=mod[:, ph["layer"] % 2, 24 * which + k, s:s + 1])
                        ins.then_inc(s_xh, 1)
                elif kind == "b1_in":
                    for i, st, u in steps_of(ph):
                        for j in range(st["units"]):
                            if i == 0:
                                copy_unit(u + j, p_tm[:, j, :], slice(0, 256))
                            elif i == 1:
                                copy_unit(u + j, uT[:, j, 0:cols], slice(0, cols))
                            elif i == 2:
                                copy_unit(u + j, vs_tm[:, j, :], slice(0, 256))
                            elif i in (3, 4):
                                act.wait_ge(s_unit, u + j + 1)
                                nc.scalar.activation(
                                    qT[:, 2 * (i - 3) + j, 0:cols].rearrange("p (q n) -> p q n", n=P)[:, :, ::-1],
                                    PS[:, (u + j) % 4, 0:cols].rearrange("p (q n) -> p q n", n=P), ACT.Copy,
                                    scale=QSCALE).then_inc(s_free[(u + j) % 4], 1)
                            elif i >= 7:
                                copy_unit(u + j, v_tm[:, j, 256 * (i - 7):256 * (i - 7) + 256], slice(0, 256))
                        for tt in range(cols // P if i == 4 else 0):
                            act.wait_ge(s_lnv, 4 * ph["l"] + tt + 1)
                            inverse_root(lnst[:, 4:5], lnst[:, 3:4]).then_inc(s_lns, 1)
                elif kind == "ff1":
                    for i, st, u in steps_of(ph):
                        for c in range(2):
                            copy_unit(u + c, hid[:, 2 * i + c, 0:cols], slice(0, cols), ACT.Relu)
                        if i == 12:
                            round_hidden(ph, 0)
                elif kind == "to_h" and ph["src"] == "ff":
                    for i, st, u in steps_of(ph):
                        round_hidden(ph, i + 1)
                elif kind == "to_h":
                    for i, st, u in steps_of(ph):
                        pass
                elif kind == "merge":
                    def round_y(c):
                        act.wait_ge(s_y, ph["y"] + 6 * (c // 2) + 4 + c % 2 + 1)
                        nc.scalar.activation(m_h[:, c, 0:cols], yT[:, c, 0:cols], ACT.Copy).then_inc(s_xh, 1)

                    for i, st, u in steps_of(ph):
                        g = i % 4 - 1
                        if g < 0:
                            if i:
                                act.wait_ge(s_y, ph["y"] + 6 * (i // 4))
                            for j in range(6):
                                copy_unit(u + j, br[:, j, 0:cols], slice(0, cols))
                        else:
                            for c in range(2):
                                idx = 6 * (i // 4) + 2 * g + c
                                if idx >= 2:
                                    act.wait_ge(s_y, ph["y"] + idx - 1)
                                copy_unit(u + c, gate[:, c, 0:cols], slice(0, cols), ACT.Sigmoid)
                        if i == 13:
                            act.wait_ge(*release[ph["steps"][12]["s"]])
                        if i >= 13:
                            round_y(2 * (i - 13))
                            round_y(2 * (i - 13) + 1)
                    round_y(6)
                    round_y(7)
                elif kind == "attn":
                    n = len(ph["heads"])

                    def exps(i):
                        x = ph["head"] + i
                        nk = head_parts(ph, i)[4]
                        act.wait_ge(s_nm, x + 1)
                        if x >= 2:
                            act.wait_ge(s_tr, x - 1)
                        for qt in range(2):
                            if ph["block"] == 1:
                                hh = ph["heads"][i][1]
                                nc.scalar.activation(esink[:, x % 2, qt:qt + 1], sink[:, hh:hh + 1], ACT.Exp,
                                                     bias=nmax[:, x % 2, qt:qt + 1])
                            ins = nc.scalar.activation(scr[:, x % 2, qt, 0:nk], PS[:, 2 * (x % 2) + qt, 0:nk], ACT.Exp,
                                                       bias=nmax[:, x % 2, qt:qt + 1],
                                                       accum_out=rsum[:, x % 2, qt:qt + 1])
                        ins.then_inc(s_exp, 1)

                    def probs_t(i):
                        x = ph["head"] + i
                        nk = head_parts(ph, i)[4]
                        act.wait_ge(s_tr, x + 1)
                        if x >= 2:
                            act.wait_ge(s_pv, x - 1)
                        nc.scalar.activation(pt[:, x % 2, 0, 0:nk // P, :],
                                             PS[:, 4, 0:nk].rearrange("p (k n) -> p k n", n=P), ACT.Copy
                                             ).then_inc(s_pta, 1)

                    for i in range(n + 1):
                        if i < n:
                            exps(i)
                        if i >= 1:
                            probs_t(i - 1)
                elif kind == "m_in":
                    for i, st, u in steps_of(ph):
                        if i == 1:
                            for d in range(2):
                                step(nc.scalar.activation(Bc[:, d, :], G[:, 2 * d + 1, :], ACT.Abs))
                                step(nc.scalar.activation(Bc[:, d, :], Bc[:, d, :], ACT.Exp, scale=-1.0))
                                nc.scalar.activation(Bc[:, d, :], Bc[:, d, :], ACT.Ln, bias=1.0).then_inc(s_ga, 1)
                        if i == 5:
                            act.wait_ge(s_gd, 1)
                            nc.scalar.activation(Bc[:, :, :], Bc[:, :, :], ACT.Exp, scale=-1.0).then_inc(s_gr, 1)
                        for j in range(st["units"]):
                            if i == 0:
                                copy_unit(u + j, G[:, j, :], slice(0, 512), ACT.Identity, m=MH, bias=gateb[:, j:j + 1])
                                if j == 3:
                                    wait_units(act, u + 4)
                            elif i < 5:
                                copy_unit(u + j, (mq if i < 3 else mk)[:, 2 * ((i - 1) % 2) + j, :], slice(0, 512),
                                          scale=1.0 if i < 3 else QSCALE)
                            elif i >= 9:
                                copy_unit(u + j, sigo[:, 2 * (i - 9) + j, :], slice(0, 512), ACT.Sigmoid)
                elif kind == "m_heads":
                    def decay(b):
                        nk = ALL if b % 4 < 2 else CTX
                        act.wait_ge(s_D, b + 1)
                        nc.scalar.activation(mbuf(b)[:, :, 0:nk], mbuf(b)[:, :, 0:nk], ACT.Exp).then_inc(s_A, 1)

                    def scale(b):
                        x = mbuf(b)[:, 0, 0:ALL if b % 4 < 2 else CTX]
                        act.wait_ge(s_rc, b + 1)
                        nc.scalar.activation(x, x, ACT.Copy, scale=den[:, b % 2, 1, 0:1]).then_inc(s_scaled, 1)

                    def turned(b):
                        nk = ALL if b % 4 < 2 else CTX
                        act.wait_ge(s_mt, b + 1)
                        if b >= 2:
                            act.wait_ge(s_mpv, b - 1)
                        nc.scalar.activation(pt[:, b % 2, 0, 0:nk // P, :],
                                             PS[:, 4 + b % 2, 0:nk].rearrange("p (k n) -> p k n", n=P), ACT.Copy
                                             ).then_inc(s_mpt, 1)

                    def head_out(hh):
                        act.wait_ge(s_mpv, 4 * hh + 4)
                        nc.scalar.activation(hs[:, hh, :], PS[:, 6 + hh % 2, :], ACT.Copy).then_inc(s_mo, 1)

                    def variance(hh):
                        act.wait_ge(s_mms, hh + 1)
                        nc.scalar.activation(msq[:, hh, :], PS[:, 6 + hh % 2, :], ACT.Copy).then_inc(s_mvar, 1)

                    def deviations(h0, h1):
                        act.wait_ge(s_mvar, h1)
                        x = msq[:, h0:h1, :]
                        inverse_root(x, x).then_inc(s_mroot, 1)

                    def round_out(hh):
                        act.wait_ge(s_hs, hh + 1)
                        nc.scalar.activation(a_h[:, hh, :], hs[:, hh, :], ACT.Copy).then_inc(s_xh, 1)

                    n = 4 * MH
                    decay(0)
                    decay(1)
                    for b in range(n):
                        scale(b)
                        if b + 2 < n:
                            decay(b + 2)
                        turned(b)
                        if b % 4 == 1 and b > 4:
                            head_out(b // 4 - 1)
                        if b % 4 == 0 and b > 4:
                            variance(b // 4 - 2)
                        if b == n - 4:
                            deviations(0, MH - 2)
                        if b >= n - 2:
                            for hh in range(2 * (b - n + 2), 2 * (b - n + 2) + 2):
                                round_out(hh)
                    variance(MH - 2)
                    head_out(MH - 1)
                    round_out(MH - 4)
                    round_out(MH - 3)
                    variance(MH - 1)
                    deviations(MH - 2, MH)
                    round_out(MH - 2)
                    round_out(MH - 1)
                elif kind == "s_in":
                    for i, st, u in steps_of(ph):
                        for j in range(st["units"] if i < 4 else 0):
                            copy_unit(u + j, sq_[:, 2 * i + j, :], slice(0, LAT), scale=QSCALE)

        @block.vector
        def _(dve):
            dve.wait_ge(s_vec, 32)
            steps = [0]

            def step(ins):
                steps[0] += 1
                ins.then_inc(s_dve, 1)
                dve.wait_ge(s_dve, steps[0])

            V = nc.vector

            def copy_unit(u, out, src_cols):
                dve.wait_ge(s_unit, u + 1)
                V.tensor_copy(out, PS[:, u % 4, src_cols]).then_inc(s_free[u % 4], 1)

            split = [0]

            def split_w(n):
                if n >= NSPLIT or n < split[0]:
                    return
                split[0] = n + 1
                for i, c in enumerate(HALVES):
                    dve.wait_ge(s_wh, 2 * n + i + 1)
                    if n >= 2:
                        dve.wait_ge(*release[n - 2])
                    V.tensor_tensor(w_l[:, n % 2, c], ring[:, split_raw[n] % SLOTS, c],
                                    w_h[:, n % 2, c].bitcast(F32), ALU.subtract).then_inc(s_wl, 1)

            def mod_tile(key, st, last, ks=range(4)):
                layer, b, half = key
                w = view4(raw_slot(dve, mod_raw[key]))
                if half == 0 and key in mod_before and ks[0] == 0:
                    dve.wait_ge(s_mcsum, mod_before[key] + 1)
                if half and ks[0] == 0:
                    dve.wait_ge(s_mtile, mod_count[key] - 1)
                nv = mod_vectors(key)
                for k in ks:
                    for v in range(nv):
                        if last[v] is not None:
                            dve.wait_ge(s_dve, last[v])
                        sc = silu[:, layer // 2, 4 * half + k, v:v + 1]
                        if half == 0 and k == 0:
                            ins = V.tensor_scalar(acc[:, v, :], w[:, k, :], sc, None, ALU.mult)
                        else:
                            ins = V.scalar_tensor_tensor(out=acc[:, v, :], in0=w[:, k, :], scalar=sc,
                                                         in1=acc[:, v, :], op0=ALU.mult, op1=ALU.add)
                        if k == 3 and v == nv - 1:
                            ins.then_inc(s_mtile, 1)
                        else:
                            steps[0] += 1
                            last[v] = steps[0]
                            ins.then_inc(s_dve, 1)

            def mod_columns(st):
                if st["modu"] is None:
                    return
                layer, b, _ = st["mods"][-1]
                nv, mu = mod_vectors(st["mods"][-1]), st["modu"]
                dve.wait_ge(s_mcsum, mu + 1)
                m = mod[:, layer % 2, :, :]
                if st["mods"][-1] in by_pe:
                    sums = PS[:, 0:4, 0:nv]
                else:
                    sums = PS[:, 5, 0:8].rearrange("p (c s) -> p c s", s=2)[:, :, 0:nv]
                b0 = V_BMOD + 48 * layer + 4 * b
                ins = V.tensor_tensor(m[:, 4 * b:4 * b + 4, 0:nv],
                                      sums,
                                      vec[:, b0:b0 + 4].unsqueeze(2).broadcast_to([P, 4, nv]), ALU.add)
                if b in (3, 9):
                    which = 0 if b == 3 else 1
                    vg = (V_N1, V_N2)[which]
                    step(ins)
                    out = gain[:, which, :, 0:nv]
                    step(V.tensor_scalar(out, m[:, 24 * which + 8:24 * which + 16, 0:nv], 1.0, None, ALU.add))
                    ins = V.tensor_tensor(out, out, vec[:, vg + KC * layer:vg + KC * layer + KC]
                                          .unsqueeze(2).broadcast_to([P, KC, nv]), ALU.mult)
                ins.then_inc(s_mcol, 1)

            def steps_of(ph):
                for i, st in enumerate(ph["steps"]):
                    last = [None, None]
                    for key in st["mods"]:
                        mod_tile(key, st, last)
                    split_w(st["s"] + 1)
                    yield i, st, st["u"]
                    mod_columns(st)

            def rest_x(n, lo, x, hi):
                dve.wait_ge(s_xh, n + 1)
                V.tensor_tensor(lo, x, hi.bitcast(F32), ALU.subtract).then_inc(s_xl, 1)

            for b in range(2):
                c0 = V_COND + b * 2 * KC
                dve.wait_ge(s_silu_a, b + 1)
                x = silu[:, b, :, :].rearrange("p k n -> p (k n)")
                V.tensor_tensor(x, x, vec[:, c0:c0 + 2 * KC], ALU.mult).then_inc(s_silu, 1)
            dve.wait_ge(s_silu, 2)
            for ph in plan:
                kind, u = ph["kind"], ph["u"]
                cols = ph.get("cols")
                if kind == "mod0":
                    for st in ph["steps"]:
                        if st["mods"][-1] in by_pe:
                            continue
                        for key in st["mods"]:
                            mod_tile(key, st, [None, None])
                        mod_columns(ph["steps"][st["modu"] - 1])
                        mod_columns(st)
                    split_w(0)
                    dve.wait_ge(s_const, CONST)
                elif kind == "norm":
                    n0, w = ph["norm"], ph["width"]
                    if not ph["final"]:
                        split_w(ph["s"] + 1)
                    dve.wait_ge(s_rstd, n0 + 1)
                    if not ph["final"]:
                        dve.wait_ge(s_mcol, mod_unit_of[ph["layer"], 6 * ph["which"] + 3] + 1)

                    def scaled(k):
                        if k < KC:
                            if k >= 2 and not ph["final"]:
                                dve.wait_ge(s_xl, ph["x"] + k - 1)
                            if ph["final"]:
                                V.tensor_tensor(nrm[:, k % 2, 0:w], h[:, k, 0:w], rs[:, 0:w], ALU.mult
                                                ).then_inc(s_nrm, 1)
                                return
                            for s, c in segs(w):
                                ins = V.scalar_tensor_tensor(out=nrm[:, k % 2, c], in0=h[:, k, c],
                                                             scalar=gain[:, ph["which"], k, s:s + 1],
                                                             in1=rs[:, c], op0=ALU.mult, op1=ALU.mult)
                            ins.then_inc(s_nrm, 1)

                    scaled(0)
                    scaled(1)
                    for k in range(KC):
                        if ph["final"]:
                            dve.wait_ge(s_fin, KC * ph["block"] + k + 1)
                        else:
                            dve.wait_ge(s_xh, ph["x"] + k + 1)
                            for s, c in segs(w):
                                ins = V.scalar_tensor_tensor(
                                    out=a_l[:, k, c], in0=nrm[:, k % 2, c],
                                    scalar=mod[:, ph["layer"] % 2, 24 * ph["which"] + k, s:s + 1],
                                    in1=a_h[:, k, c].bitcast(F32), op0=ALU.add, op1=ALU.subtract)
                            ins.then_inc(s_xl, 1)
                        scaled(k + 2)
                elif kind == "b1_in":
                    for i, st, u in steps_of(ph):
                        if i in (5, 6):
                            for j in range(2):
                                copy_unit(u + j, kT[:, 2 * (i - 5) + j, :], slice(0, 512))
                        if i == 4:
                            for tt in range(cols // P):
                                wait_unit(dve, ph["steps"][2]["u"] + tt)
                                x = vs_tm[:, tt, :]
                                step(V.reduce_sum(lnst[:, 0:1], x, AX_X))
                                step(V.tensor_scalar(lnst[:, 1:2], lnst[:, 0:1], 1.0 / 256, None, ALU.mult))
                                step(V.tensor_scalar(x, x, lnst[:, 1:2], None, ALU.subtract))
                                step(V.tensor_tensor_reduce(pt[:, 0, 0, 0:2, :].rearrange("p b n -> p (b n)"), x, x,
                                                            1.0, 0.0, ALU.mult, ALU.add, lnst[:, 2:3]))
                                V.tensor_scalar(lnst[:, 3:4], lnst[:, 2:3], 1.0 / 256, None, ALU.mult
                                                ).then_inc(s_lnv, 1)
                                dve.wait_ge(s_lns, 4 * ph["l"] + tt + 1)
                                ins = V.tensor_scalar(x, x, lnst[:, 4:5], None, ALU.mult)
                                if tt == cols // P - 1:
                                    ins.then_inc(s_sgu, 1)
                elif kind == "rope":
                    dve.wait_ge(s_aux, AUX_LANDED[ph["layer"]])
                    wait_units(dve, u)
                    cs = aux[:, A_ROPE:A_ROPE + 512].rearrange("p (s n) -> p s n", s=2)
                    for c in range(ph["chunks"]):
                        x = rope_chunk(ph, c)
                        dve.wait_ge(s_unit, u + c + 1)
                        tmp = bias[:, 0, 0:LAT].rearrange("p (q n) -> p q n", n=P)

                        def tiles_of(y):
                            return y.rearrange("p (q n) -> p q n", n=P)

                        cos, sin = tiles_of(cs[:, 0, :]), tiles_of(cs[:, 1, :])
                        if ph["block"] == 0 and c < 4:
                            cos, sin = cos[:, :, ::-1], sin[:, :, ::-1]
                        x = tiles_of(x)
                        V.tensor_tensor(tmp, tiles_of(PS[:, (u + c) % 4, 0:LAT]), sin, ALU.mult)
                        step(V.tensor_tensor(x, x, cos, ALU.mult))
                        V.tensor_tensor(x, x, tmp, ALU.add).then_inc(s_free[(u + c) % 4], 1)
                        dve.wait_ge(s_free[(u + c) % 4], (u + c) // 4 + 1)
                elif kind == "pool_sgu":
                    for pair in range(2):
                        copy_unit(u, pooled[:, pair, 0:cols], slice(0, cols))
                        u += 1
                    for pair in range(2):
                        dve.wait_ge(s_unit, u + 1)
                        c = V_PS + 2 * ph["l"] + pair
                        hi = m_h[:, pair, 0:cols]
                        step(V.tensor_scalar(hi, PS[:, u % 4, 0:cols], vec[:, c:c + 1], None, ALU.mult))
                        V.scalar_tensor_tensor(out=m_l[:, pair, 0:cols], in0=PS[:, u % 4, 0:cols], scalar=vec[:, c:c + 1],
                                               in1=hi.bitcast(F32), op0=ALU.mult, op1=ALU.subtract
                                               ).then_inc(s_free[u % 4], 1)
                        u += 1
                    for pair in range(2):
                        dve.wait_ge(s_unit, u + 1)
                        x, hi = uT[:, pair, 0:cols], m_h[:, 2 + pair, 0:cols]
                        step(V.tensor_tensor(x, PS[:, u % 4, 0:cols], x, ALU.mult))
                        step(V.tensor_copy(hi, x))
                        V.tensor_tensor(m_l[:, 2 + pair, 0:cols], x, hi.bitcast(F32), ALU.subtract
                                        ).then_inc(s_free[u % 4], 1)
                        u += 1
                elif kind == "attn":
                    n = len(ph["heads"])
                    if ph["block"] == 1:
                        dve.wait_ge(s_aux, AUX_LANDED[3])

                    def rowmax(i):
                        x = ph["head"] + i
                        what, hh = ph["heads"][i]
                        nk = head_parts(ph, i)[4]
                        S = PS[:, 2 * (x % 2):2 * (x % 2) + 2, :]
                        dve.wait_ge(s_sc, x + 1)
                        if what == "lat":
                            if ph["block"] == 0:
                                dve.wait_ge(s_bias, nbias(ph, i) + 1)
                                add = bias[:, hh % 2, :].rearrange("p (q n) -> p q n", q=2)
                            else:
                                add = aux[:, A_MASK:A_MASK + 512].rearrange("p (q n) -> p q n", q=2)
                            step(V.tensor_tensor(S[:, :, 0:LAT], S[:, :, 0:LAT], add, ALU.add))
                        m = nmax[:, x % 2, :]
                        step(V.tensor_reduce(m, S[:, :, 0:nk], AX_X, ALU.max))
                        if ph["block"] == 1:
                            step(V.tensor_scalar(m, m, sink[:, hh:hh + 1], None, ALU.max))
                        V.tensor_scalar(m, m, -1.0, None, ALU.mult).then_inc(s_nm, 1)

                    def inverse(i):
                        x = ph["head"] + i
                        dve.wait_ge(s_exp, x + 1)
                        if ph["block"] == 1:
                            step(V.tensor_tensor(rsum[:, x % 2, :], rsum[:, x % 2, :], esink[:, x % 2, :], ALU.add))
                        step(V.reciprocal(rinv[:, x % 2, :], rsum[:, x % 2, :]))
                        nk = head_parts(ph, i)[4]
                        for qt in range(2):
                            p_ = scr[:, x % 2, qt, 0:nk]
                            ins = V.tensor_scalar(p_, p_, rinv[:, x % 2, qt:qt + 1], None, ALU.mult)
                        ins.then_inc(s_prob, 1)

                    def probs_t(i):
                        x = ph["head"] + i
                        nk = head_parts(ph, i)[4]
                        dve.wait_ge(s_tr, x + 1)
                        if x >= 2:
                            dve.wait_ge(s_pv, x - 1)
                        V.tensor_copy(pt[:, x % 2, 1, 0:nk // P, :],
                                      PS[:, 5, 0:nk].rearrange("p (k n) -> p k n", n=P)).then_inc(s_ptd, 1)

                    def out(i):
                        x = ph["head"] + i
                        base, o = head_parts(ph, i)[3], head_parts(ph, i)[5]
                        dve.wait_ge(s_pv, x + 1)
                        src = PS[base:base + HD, 6 + x % 2, 0:LAT].rearrange("p (q n) -> p q n", q=2)
                        if ph["block"] == 0:
                            src = src[:, :, ::-1]
                        hi, lo = (y.rearrange("p (q n) -> p q n", q=2) for y in o)
                        step(V.tensor_copy(hi, src))
                        V.tensor_tensor(lo, src, hi.bitcast(F32), ALU.subtract).then_inc(s_o, 1)

                    rowmax(0)
                    for i in range(n + 2):
                        if i + 1 < n:
                            rowmax(i + 1)
                        if 1 <= i <= n:
                            probs_t(i - 1)
                        if i < n:
                            inverse(i)
                        if i >= 2:
                            out(i - 2)
                elif kind == "merge":
                    def rest_y(c):
                        rest_x(ph["x"] + c, m_l[:, c, 0:cols], yT[:, c, 0:cols], m_h[:, c, 0:cols])

                    for i, st, u in steps_of(ph):
                        g = i % 4 - 1
                        for c in range(2 if g >= 0 else 0):
                            wait_unit(dve, ph["steps"][i - 1 - g]["u"] + 3 * c + g)
                            wait_unit(dve, u + c)
                            y, x, gt = yT[:, 2 * (i // 4) + c, 0:cols], br[:, 3 * c + g, 0:cols], gate[:, c, 0:cols]
                            if g == 0:
                                ins = V.tensor_tensor(y, x, gt, ALU.mult)
                            else:
                                step(V.tensor_tensor(x, x, gt, ALU.mult))
                                ins = V.tensor_tensor(y, y, x, ALU.add)
                            ins.then_inc(s_y, 1)
                            if g >= 0 and c == 1:
                                dve.wait_ge(s_y, ph["y"] + 6 * (i // 4) + 2 * g + 2)
                        if i >= 13:
                            rest_y(2 * (i - 13))
                            rest_y(2 * (i - 13) + 1)
                    rest_y(6)
                    rest_y(7)
                elif kind == "to_h":
                    dve.wait_ge(s_mcol, mod_unit_of[ph["layer"], 2 * ph["gate"] + 1] + 1)
                    for i, st, u in steps_of(ph):
                        for j in range(st["units"]):
                            c = (2 * i + j) if ph["src"] != "ff" else 4 * (i // 8) + j
                            dve.wait_ge(s_unit, u + j + 1)
                            for s, cc in segs(cols):
                                ins = V.scalar_tensor_tensor(
                                    out=h[:, c, cc], in0=PS[:, (u + j) % 4, cc],
                                    scalar=mod[:, ph["layer"] % 2, 8 * ph["gate"] + c, s:s + 1],
                                    in1=h[:, c, cc], op0=ALU.mult, op1=ALU.add)
                            ins.then_inc(s_free[(u + j) % 4], 1)
                            if c == KC - 1:
                                wait_unit(dve, u + j)
                                V.tensor_tensor(nrm[:, 0, 0:cols], h[:, c, 0:cols], h[:, c, 0:cols], ALU.mult
                                                ).then_inc(s_sq7, 1)
                elif kind == "ff1":
                    for _ in steps_of(ph):
                        pass
                elif kind == "m_in":
                    def scan_rows(d):
                        li, lf, B = G[:, 2 * d, :], G[:, 2 * d + 1, :], Bc[:, d, :]
                        dve.wait_ge(s_ga, d + 1)
                        step(V.tensor_scalar(lf, lf, 0.0, None, ALU.min))
                        step(V.tensor_tensor(lf, lf, B, ALU.subtract))
                        if d == 0:
                            parts = (slice(LAT, ALL), slice(0, LAT))
                            last = (slice(ALL - 1, ALL), None)
                        else:
                            parts = (slice(ALL - 1, LAT - 1, -1), slice(LAT - 1, None, -1))
                            last = (slice(LAT, LAT + 1), None)
                        ini = 0.0
                        for pr, la in zip(parts, last):
                            step(V.tensor_tensor_scan(B[:, pr], one_row[:, pr], lf[:, pr], ini, ALU.mult, ALU.add))
                            ini = None if la is None else B[:, la]
                        step(V.tensor_tensor(li, li, B, ALU.subtract))
                        M = lf
                        ini = 0.0
                        for pr, la in zip(parts, last):
                            step(V.tensor_tensor_scan(M[:, pr], li[:, pr], li[:, pr], ini, ALU.max, ALU.max))
                            ini = None if la is None else M[:, la]
                        ins = V.tensor_tensor(B, B, M, ALU.add)
                        if d == 1:
                            ins.then_inc(s_gd, 1)
                        else:
                            step(ins)

                    for i, st, u in steps_of(ph):
                        if i == 0:
                            wait_units(dve, u + 4)
                            step(V.memset(one_row, 1.0))
                        if i in (2, 4):
                            scan_rows(i // 2 - 1)
                        for j in range(st["units"] if 5 <= i < 9 else 0):
                            copy_unit(u + j, mv[:, j, 256 * (i - 5):256 * (i - 5) + 256], slice(0, 256))
                elif kind == "m_gates":
                    wait_units(dve, u)
                    for d in range(2):
                        ins = V.tensor_copy(grow[:, d, :], G[:, 2 * d, :])
                    step(ins)
                    dve.wait_ge(s_unit, u + 1)
                    src = PS[:, u % 4, :].rearrange("p (w t g n) -> p w t g n", w=2, t=4, g=2, n=32)
                    for what in range(2):
                        for d in range(2):
                            ins = V.tensor_scalar(tm[:, what, :, :, d], src[:, what, :, d, 0:MH],
                                                  -1.0 if what == 0 else 1.0, None, ALU.mult)
                            if not (what and d):
                                step(ins)
                    ins.then_inc(s_free[u % 4], 1)
                elif kind == "m_heads":
                    dve.wait_ge(s_aux, AUX_LANDED[2])
                    mask = aux[:, A_MF:A_MF + 2048].rearrange("p (d q n) -> p d q n", d=2, q=2)
                    wait_units(dve, u)

                    def args(b, d):
                        hh, qt = b // 4, b % 4
                        c0 = 0 if qt < 2 else LAT
                        nk = ALL - c0
                        if d == 0:
                            dve.wait_ge(s_rows, hh + 1)
                            if b >= 3:
                                dve.wait_ge(s_mt, b - 2)
                        ins = V.scalar_tensor_tensor(out=mbuf(b)[:, d, 0:nk], in0=PS[:, d, c0:ALL],
                                                     scalar=tm[:, 0, qt, hh, d:d + 1],
                                                     in1=mask[:, d, qt % 2, 0:nk], op0=ALU.add, op1=ALU.min)
                        if d == 1:
                            ins.then_inc(s_D, 1)

                    def normed(hh):
                        r = msq[:, hh, :]
                        dve.wait_ge(s_mroot, 1 if hh < MH - 2 else 2)
                        V.scalar_tensor_tensor(out=hs[:, hh, :], in0=hs[:, hh, :],
                                               scalar=vec[:, V_HN + hh:V_HN + hh + 1], in1=r,
                                               op0=ALU.mult, op1=ALU.mult).then_inc(s_hn, 1)

                    n = 4 * MH
                    for b in range(2):
                        args(b, 0)
                        args(b, 1)
                    for b in range(n):
                        hh, qt = b // 4, b % 4
                        nk = ALL if qt < 2 else CTX
                        dve.wait_ge(s_A, b + 1)
                        dn, rc = den[:, b % 2, 0, :], den[:, b % 2, 1, :]
                        x0, x1 = mbuf(b)[:, 0, 0:nk], mbuf(b)[:, 1, 0:nk]
                        dve.wait_ge(s_qk, b + 1)
                        for d, x in enumerate((x0, x1)):
                            ins = V.tensor_tensor_reduce(x, x, PS[:, 2 + b % 2, 0:nk], 1.0, 0.0, ALU.mult, ALU.add,
                                                         dn[:, d:d + 1])
                        ins.then_inc(s_W, 1)
                        if b + 2 < n:
                            args(b + 2, 0)
                        dve.wait_ge(s_W, b + 1)
                        step(V.scalar_tensor_tensor(out=rc, in0=dn, scalar=-1.0, in1=dn, op0=ALU.mult, op1=ALU.max))
                        step(V.tensor_tensor(rc, rc, tm[:, 1, qt, hh, :], ALU.max))
                        V.reciprocal(rc, rc).then_inc(s_rc, 1)
                        if b + 2 < n:
                            args(b + 2, 1)
                        dve.wait_ge(s_scaled, b + 1)
                        V.scalar_tensor_tensor(out=x0, in0=x1, scalar=rc[:, 1:2], in1=x0, op0=ALU.mult, op1=ALU.add
                                               ).then_inc(s_P, 1)
                        if b >= n - 3:
                            for hh in range(2 * (b - n + 3), 2 * (b - n + 3) + 2):
                                normed(hh)
                    for k in range(MH - 2):
                        rest_x(ph["x"] + k, a_l[:, k, :], hs[:, k, :], a_h[:, k, :])
                    normed(MH - 2)
                    k = MH - 2
                    rest_x(ph["x"] + k, a_l[:, k, :], hs[:, k, :], a_h[:, k, :])
                    normed(MH - 1)
                    k = MH - 1
                    rest_x(ph["x"] + k, a_l[:, k, :], hs[:, k, :], a_h[:, k, :])
                elif kind == "s_in":
                    for i, st, u in steps_of(ph):
                        for j in range(st["units"] if i >= 4 else 0):
                            if i == 4:
                                copy_unit(u + j, sk[:, j, :], slice(0, 512))
                            else:
                                copy_unit(u + j, sv[:, j, :], slice(0, 256))

        @block.gpsimd
        def _(pool):
            pool.wait_ge(s_const, CONST)
            steps = [0]
            squared = []

            def square(ph, k):
                if ph["squares"] == "switch":
                    pool.wait_ge(s_fin, k + 1)
                    if k >= 2:
                        pool.wait_ge(s_sqp, k - 1)
                    x = h[:, k, 0:LAT]
                    nc.gpsimd.tensor_tensor(sqb[:, k % 2, 0:LAT], x, x, ALU.mult).then_inc(s_sqlat, 1)
                    return
                if ph["squares"] == "first":
                    if k == 0:
                        pool.wait_ge(s_ctxld, 16)
                    add_square(k, slice(0, ALL), s_sq if k == KC - 1 else None)
                elif k < KC - 1:
                    wait_unit(pool, ph["hunits"][k])
                    add_square(k, slice(0, ph["width"]), s_sq if k == KC - 2 else None)

            def add_square(k, c, last=None):
                x = h[:, k, c]
                if k == 0:
                    steps[0] += 1
                    nc.gpsimd.tensor_tensor(ssum[:, c], x, x, ALU.mult).then_inc(s_pool, 1)
                    return
                steps[0] += 1
                nc.gpsimd.tensor_tensor(sqb[:, k % 2, c], x, x, ALU.mult).then_inc(s_pool, 1)
                pool.wait_ge(s_pool, steps[0])
                ins = nc.gpsimd.tensor_tensor(ssum[:, c], ssum[:, c], sqb[:, k % 2, c], ALU.add)
                if last is None:
                    steps[0] += 1
                    ins.then_inc(s_pool, 1)
                else:
                    ins.then_inc(last, 1)

            def rest_hidden(ph, g):
                x0 = ph["x"]
                cols = ph["cols"]
                pool.wait_ge(s_xh, x0 + g + 1)
                if g:
                    pool.wait_ge(*hidden_free(ph, g))
                hi, lo = (x[:, :, 0:cols] for x in hidden_pair(g))
                nc.gpsimd.tensor_tensor(lo, hid[:, 4 * (g % 8):4 * (g % 8) + 4, 0:cols],
                                        hi.bitcast(F32), ALU.subtract).then_inc(s_xl, 1)

            def gated(hh):
                pool.wait_ge(s_hn, hh + 1)
                nc.gpsimd.tensor_tensor(hs[:, hh, :], hs[:, hh, :], sigo[:, hh, :], ALU.mult).then_inc(s_hs, 1)

            for ph in plan:
                kind, u = ph["kind"], ph["u"]
                cols = ph.get("cols")
                if kind == "norm":
                    for k in range(KC):
                        if k not in squared:
                            square(ph, k)
                    squared.clear()
                elif kind == "ff1":
                    for i in range(32):
                        wait_unit(pool, ph["steps"][i // 2]["u"] + i % 2)
                        x = hid[:, i, 0:cols]
                        nc.gpsimd.tensor_tensor(x, x, x, ALU.mult).then_inc(s_ff, 1)
                        if i == 27:
                            rest_hidden(ph, 0)
                elif kind == "to_h" and ph["src"] == "ff":
                    for g in range(1, 16):
                        rest_hidden(ph, g)
                        if ph["layer"] == 1 and g < 9:
                            if g == 1:
                                pool.wait_ge(s_ctxld, 32)
                                pool.wait_ge(*release[ph["steps"][0]["s"]])
                            add_square(g - 1, slice(LAT, ALL), s_sqctx if g == KC else None)
                        if 10 <= g < 14:
                            square(plan[plan.index(ph) + 1 if ph["layer"] % 2 else plan.index(ph) + 2], g - 10)
                            squared.append(g - 10)
                elif kind == "attn":
                    def mask_bias(i):
                        hh = ph["heads"][i][1]
                        pool.wait_ge(s_biasld[i % 2], 64 * (nbias(ph, i) // 2 + 1))
                        b = bias[:, hh % 2, :]
                        nc.gpsimd.tensor_tensor(b, b, aux[:, A_MASK:A_MASK + 512], ALU.add).then_inc(s_bias, 1)

                    if ph["block"] == 0:
                        pool.wait_ge(s_aux, AUX_LANDED[ph["layer"]])
                        for i in range(8):
                            mask_bias(i)
                elif kind == "m_heads":
                    for hh in range(MH):
                        pool.wait_ge(s_mo, hh + 1)
                        nc.gpsimd.tensor_tensor(msq[:, hh, :], hs[:, hh, :], hs[:, hh, :], ALU.mult).then_inc(s_msq, 1)
                        for done in {MH - 2: range(0, 4), MH - 1: range(4, MH)}.get(hh, ()):
                            gated(done)


def shape_constants():
    c = {}
    c["unit"] = np.tile(np.array([1.0, 1.0 / D, 1.0 / MDV, EPS], np.float32), (P, 1))
    c["ident"] = np.eye(P, dtype=np.float32)
    rot = np.zeros((P, 2, P), np.float32)
    for base in (0, HD):
        for j in range(HD // 2):
            lo, hi = base + 2 * j, base + 2 * j + 1
            rot[hi, 0, lo] = -1.0
            rot[lo, 0, hi] = 1.0
            lo, hi = base + j, base + j + HD // 2
            rot[hi, 1, lo] = -1.0
            rot[lo, 1, hi] = 1.0
    c["rot"] = rot
    t = np.arange(LAT)
    nf = HD // 4
    inv = np.float32(10000.0) ** (-np.arange(nf, dtype=np.float32) / np.float32(nf))
    row, col = (t // GRID).astype(np.float32), (t % GRID).astype(np.float32)
    ang = np.concatenate([row[:, None] * inv, col[:, None] * inv], axis=-1)
    cs = np.stack([np.cos(ang), np.sin(ang)]).astype(np.float32).transpose(2, 0, 1)
    c["rope1"] = np.tile(np.repeat(cs, 2, axis=0), (2, 1, 1)).reshape(P, 512)
    c["rope2"] = np.tile(cs, (4, 1, 1)).reshape(P, 512)
    start = np.clip(col - 8, 0, GRID - 16)
    ok = (col[None, :] >= start[:, None]) & (col[None, :] < start[:, None] + 16)

    def tiled(m):
        return np.ascontiguousarray(m.astype(np.float32).reshape(2, P, -1).transpose(1, 0, 2)).reshape(P, -1)

    c["na_mask"] = np.ascontiguousarray(tiled(np.where(ok, 0.0, NEG))[::-1])
    c["swa_mask"] = tiled(np.where(np.abs(t[:, None] - t[None, :]) <= 128, 0.0, NEG))
    fwd = np.concatenate([np.where(t[None, :] <= t[:, None], 0.0, NEG), np.zeros((LAT, CTX))], axis=1)
    bwd = np.concatenate([np.where(t[None, :] >= t[:, None], 0.0, NEG), np.zeros((LAT, CTX))], axis=1)
    c["m_mask"] = np.concatenate([tiled(fwd), tiled(bwd)], axis=1)
    win = np.zeros((4, LAT, LAT), np.float32)
    for g, w in enumerate((2, 4, 8, 16)):
        lo, hi = np.clip(t - w // 2, 0, LAT), np.clip(t + w - w // 2, 0, LAT)
        inside = (t[:, None] >= lo[None, :]) & (t[:, None] < hi[None, :])
        win[g] = np.where(inside, 1.0 / (hi - lo)[None, :].astype(np.float32), 0.0) - np.eye(LAT)
    c["pool_win"] = np.ascontiguousarray(win.reshape(4, 2, P, LAT).transpose(2, 1, 0, 3)).reshape(P, 2048)
    return c


def lay_out(inp):
    f = {k: np.asarray(v) for k, v in inp.items()}

    def colv(x):
        return x.reshape(-1, P).T

    parts = []
    for cc, cx in (("c", "c_ctx"), ("c_2", "c_ctx_2")):
        parts.append(np.stack([colv(f[cc].reshape(-1)), colv(f[cx].reshape(-1))], axis=2).reshape(P, -1))
    for name in ("b_mod", "ada_b_2", "norm1_g", "norm_mix_2", "norm2_g", "norm_ffn_2", "final_g", "final_norm_2",
                 "pool_scale", "mlstm_head_norm_2"):
        parts.append(colv(f[name].reshape(-1)))
    out = {"vec": np.concatenate(parts, axis=1)}
    out["xT"] = f["x"][0].T
    out["ctxT0"] = f["ctx"][0].T
    out["ctxT1"] = f["ctx_2"][0].T
    out["sgu_wT"] = f["sgu_w"].transpose(0, 3, 1, 2).reshape(2, P, 512)
    out["sgub"] = f["sgu_b"].transpose(1, 0, 2)
    out["gateb"] = f["mlstm_gate_b_2"][0].T
    bd = np.zeros((2, P, 2, P), np.float32)
    for g in range(4):
        o = HD * (g % 2)
        bd[:, o:o + HD, g // 2, o:o + HD] = f["w_pool"][:, g]
    out["w_pool_bd"] = bd.reshape(2, P, 256)
    for name in ("w_mod", "ada_w_2", "w_in", "w_pool_out", "w_sgu_out", "w_attn_out", "w_o", "w_ff1", "w_ff2",
                 "ffn_w1_2", "ffn_w2_2", "mlstm_w_in_2", "mlstm_w_out_2", "swa_w_in_2", "swa_w_out_2", "na_rpb"):
        out[name] = f[name]
    out["swa_sink_2"] = f["swa_sink_2"].reshape(-1)
    return out


def kernel(**inputs):
    import concourse.bacc as bacc
    from concourse.bass_utils import run_bass_kernel_spmd

    arrays = lay_out(inputs)
    arrays.update(shape_constants())
    nc = bacc.Bacc("TRN2", target_bir_lowering=False, num_devices=1)
    io, sent = {}, {}
    for name, x in arrays.items():
        x = np.ascontiguousarray(x)
        sent[f"in_{name}"] = x
        io[name] = nc.dram_tensor(f"in_{name}", x.shape, F32, kind="ExternalInput").ap()
    io["out"] = nc.dram_tensor("outT", (D, LAT), F32, kind="ExternalOutput").ap()
    build(nc, io)
    r = run_bass_kernel_spmd(nc, [sent], core_ids=[0])
    return np.ascontiguousarray(r.results[0]["outT"].T).reshape(1, LAT, D)
```
